# Optimizing a Trainium2 kernel written in Bass

```python
import math
import jax, jax.numpy as jnp
from jax import lax
import numpy as np
import jax
import jax.numpy as jnp

D_MODEL = 1024
BATCH = 1
SEQ = 512
DEPTH = 1

CHUNK = 64
N_META = 16

D_MIX = D_MODEL
HEAD_DIM = 64
LRU_WIDTH = D_MIX // 4
LRU_HEADS = LRU_WIDTH // HEAD_DIM
CONV_A = 4
LRU_C = 8.0
FOX_WIDTH = D_MIX // 2
FOX_HEADS = FOX_WIDTH // HEAD_DIM
Q_BLOCK = 128
RWKV_WIDTH = D_MIX - LRU_WIDTH - FOX_WIDTH
RWKV_HEADS = RWKV_WIDTH // HEAD_DIM
W_RANK = 64
A_RANK = 64
G_RANK = 128
V_RANK = 32
GN_EPS = 64e-5
A_COLS = 2 * LRU_WIDTH
B_COLS = 3 * FOX_WIDTH + FOX_HEADS
C_COLS = 3 * RWKV_WIDTH + W_RANK + A_RANK + G_RANK
D_IN = A_COLS + B_COLS + C_COLS
C_SPLITS = (RWKV_WIDTH, 2 * RWKV_WIDTH, 3 * RWKV_WIDTH, 3 * RWKV_WIDTH + W_RANK, 3 * RWKV_WIDTH + W_RANK + A_RANK)
D_FF = 2816
CONV_F = 3
EPS = 1e-6


def rms_norm(x, g):
    xf = x.astype(jnp.float32)
    y = xf * lax.rsqrt(jnp.mean(xf * xf, axis=-1, keepdims=True) + EPS)
    return (y * g.astype(jnp.float32)).astype(x.dtype)

def causal_dwconv(x, w):
    k = w.shape[0]
    return lax.conv_general_dilated(
        x, w[:, None, :].astype(x.dtype), window_strides=(1,), padding=[(k - 1, 0)],
        dimension_numbers=('NWC', 'WIO', 'NWC'), feature_group_count=x.shape[-1])

def token_shift(p):
    return jnp.pad(p, ((0, 0), (1, 0), (0, 0)))[:, :-1]

def rg_lru_group(xa, ya, conv_w, conv_b, ga_w, ga_b, gx_w, gx_b, lam):
    bsz, t, _ = xa.shape
    u = causal_dwconv(xa, conv_w) + conv_b
    uh = u.reshape(bsz, t, LRU_HEADS, HEAD_DIM)
    r = jax.nn.sigmoid(jnp.einsum('bthi,hij->bthj', uh, ga_w).reshape(bsz, t, LRU_WIDTH) + ga_b)
    i = jax.nn.sigmoid(jnp.einsum('bthi,hij->bthj', uh, gx_w).reshape(bsz, t, LRU_WIDTH) + gx_b)
    log_a = -LRU_C * r.astype(jnp.float32) * jax.nn.softplus(-lam.astype(jnp.float32))
    a = jnp.exp(log_a)
    b = jnp.sqrt(-jnp.expm1(2.0 * log_a)) * (i * u).astype(jnp.float32)

    def combine(left, right):
        a1, b1 = left
        a2, b2 = right
        return a1 * a2, a2 * b1 + b2

    _, h = lax.associative_scan(combine, (a, b), axis=1)
    return h.astype(xa.dtype) * jax.nn.gelu(ya, approximate=True)

def forgetting_attention_group(q, k, v, f_logit, f_bias):
    bsz, t, _ = q.shape
    n_blk = -(-t // Q_BLOCK)
    tp = n_blk * Q_BLOCK

    def heads(z):
        z = jnp.pad(z, ((0, 0), (0, tp - t), (0, 0)))
        return z.reshape(bsz, tp, FOX_HEADS, HEAD_DIM).transpose(0, 2, 1, 3)

    qh = heads(q) * (HEAD_DIM ** -0.5)
    kh = heads(k)
    vh = heads(v)
    log_f = jax.nn.log_sigmoid((f_logit + f_bias).astype(jnp.float32))
    log_f = jnp.pad(log_f, ((0, 0), (0, tp - t), (0, 0)))
    c = jnp.cumsum(log_f, axis=1).transpose(0, 2, 1)
    kpos = jnp.arange(tp)

    def block(i):
        start = i * Q_BLOCK
        qb = lax.dynamic_slice_in_dim(qh, start, Q_BLOCK, axis=2)
        cb = lax.dynamic_slice_in_dim(c, start, Q_BLOCK, axis=2)
        qpos = start + jnp.arange(Q_BLOCK)
        s = jnp.einsum('bhqd,bhkd->bhqk', qb, kh).astype(jnp.float32) + (cb[..., :, None] - c[..., None, :])
        s = jnp.where(kpos[None, :] <= qpos[:, None], s, -jnp.inf)
        p = jax.nn.softmax(s, axis=-1)
        return jnp.einsum('bhqk,bhkd->bhqd', p.astype(vh.dtype), vh)

    o = lax.map(block, jnp.arange(n_blk))
    o = o.transpose(1, 0, 3, 2, 4).reshape(bsz, tp, FOX_WIDTH)
    return o[:, :t]

def rwkv7_group(pc, mu, w0, w_up, a0, a_up, g_up, k_k, k_a, r_k, ln_w, ln_b, v_first, v_mix):
    f32 = jnp.float32
    bsz, t, _ = pc.shape
    pc = pc + (token_shift(pc) - pc) * mu
    r, k, v, wd, ad, gd = jnp.split(pc, C_SPLITS, axis=-1)
    v_own = v
    if v_mix is not None:
        v0, v_down, v_up = v_mix
        v = v + (v_first - v) * jax.nn.sigmoid(v0 + (v @ v_down) @ v_up)
    w_log = -jax.nn.softplus(-(w0 + jnp.tanh(wd) @ w_up).astype(f32)) - 0.5
    decay = jnp.exp(-jnp.exp(w_log))
    a = jax.nn.sigmoid(a0 + ad @ a_up)
    g = jax.nn.sigmoid(gd) @ g_up

    def heads(z):
        return z.astype(f32).reshape(bsz, t, RWKV_HEADS, HEAD_DIM)

    kk = heads(k * k_k)
    kk = kk / jnp.maximum(jnp.sqrt(jnp.sum(kk * kk, axis=-1, keepdims=True)), 1e-12)
    k = k * (1.0 + (a - 1.0) * k_a)
    rh, kh, vh, ah, wh = heads(r), heads(k), heads(v), heads(a), heads(decay)
    xs = tuple(z.transpose(1, 0, 2, 3) for z in (rh, wh, kh, vh, kk, ah))

    def step(S, inp):
        r_t, w_t, k_t, v_t, kk_t, a_t = inp
        s_kk = jnp.einsum('bhij,bhj->bhi', S, kk_t)
        S = S * w_t[:, :, None, :] - s_kk[..., None] * (kk_t * a_t)[:, :, None, :] + v_t[..., None] * k_t[:, :, None, :]
        return S, jnp.einsum('bhij,bhj->bhi', S, r_t)

    s0 = jnp.zeros((bsz, RWKV_HEADS, HEAD_DIM, HEAD_DIM), f32)
    _, o = lax.scan(step, s0, xs)
    o = o.transpose(1, 0, 2, 3)
    mean = jnp.mean(o, axis=-1, keepdims=True)
    var = jnp.mean(jnp.square(o - mean), axis=-1, keepdims=True)
    o = ((o - mean) * lax.rsqrt(var + GN_EPS)).reshape(bsz, t, RWKV_WIDTH) * ln_w + ln_b
    bonus = (jnp.sum(rh * kh * r_k, axis=-1, keepdims=True) * vh).reshape(bsz, t, RWKV_WIDTH)
    out = ((o + bonus) * g.astype(f32)).astype(pc.dtype)
    return out, v_own

def first_inputs(seed: int = 0) -> dict:
    key = jax.random.key(seed)
    ks = iter(jax.random.split(key, 40))
    f32 = jnp.float32

    def nrm(shape, scale):
        return scale * jax.random.normal(next(ks), shape, f32)

    def unif(shape, lo, hi):
        return jax.random.uniform(next(ks), shape, f32, lo, hi)

    L = DEPTH
    Lv = DEPTH - 1
    x = nrm((BATCH, SEQ, D_MODEL), 1.0)
    meta_tokens = nrm((N_META, D_MODEL), 1.0)
    norm_mix_pre = 1.0 + nrm((L, D_MODEL), 0.05)
    norm_mix_post = 1.0 + nrm((L, D_MODEL), 0.05)
    norm_ffn_pre = 1.0 + nrm((L, D_MODEL), 0.05)
    norm_ffn_post = 1.0 + nrm((L, D_MODEL), 0.05)
    w_in = nrm((L, D_MODEL, D_IN), D_MODEL ** -0.5)
    w_out = nrm((L, D_MIX, D_MODEL), D_MIX ** -0.5)
    lru_conv_w = nrm((L, CONV_A, LRU_WIDTH), CONV_A ** -0.5)
    lru_conv_b = nrm((L, LRU_WIDTH), 0.02)
    lru_gate_a_w = nrm((L, LRU_HEADS, HEAD_DIM, HEAD_DIM), HEAD_DIM ** -0.5)
    lru_gate_a_b = nrm((L, LRU_WIDTH), 0.02)
    lru_gate_x_w = nrm((L, LRU_HEADS, HEAD_DIM, HEAD_DIM), HEAD_DIM ** -0.5)
    lru_gate_x_b = nrm((L, LRU_WIDTH), 0.02)
    a_init = unif((L, LRU_WIDTH), 0.9, 0.999) ** (1.0 / LRU_C)
    lru_lambda = jnp.log(a_init) - jnp.log1p(-a_init)
    fox_f_bias = unif((L, FOX_HEADS), 1.0, 4.0)
    rwkv_mu = unif((L, C_COLS), 0.0, 1.0)
    rwkv_w0 = unif((L, RWKV_WIDTH), -6.0, -1.0)
    rwkv_w_up = nrm((L, W_RANK, RWKV_WIDTH), 0.1 * W_RANK ** -0.5)
    rwkv_a0 = nrm((L, RWKV_WIDTH), 0.1)
    rwkv_a_up = nrm((L, A_RANK, RWKV_WIDTH), 0.5 * A_RANK ** -0.5)
    rwkv_g_up = nrm((L, G_RANK, RWKV_WIDTH), G_RANK ** -0.5)
    rwkv_v0 = 1.0 + nrm((Lv, RWKV_WIDTH), 0.1)
    rwkv_v_down = nrm((Lv, RWKV_WIDTH, V_RANK), RWKV_WIDTH ** -0.5)
    rwkv_v_up = nrm((Lv, V_RANK, RWKV_WIDTH), 0.5 * V_RANK ** -0.5)
    rwkv_k_k = 0.85 + nrm((L, RWKV_WIDTH), 0.05)
    rwkv_k_a = 1.0 + nrm((L, RWKV_WIDTH), 0.05)
    rwkv_r_k = nrm((L, RWKV_HEADS, HEAD_DIM), 0.1)
    rwkv_ln_w = 1.0 + nrm((L, RWKV_WIDTH), 0.05)
    rwkv_ln_b = nrm((L, RWKV_WIDTH), 0.02)
    ffn_up = nrm((L, D_MODEL, 2 * D_FF), D_MODEL ** -0.5)
    ffn_conv = nrm((L, CONV_F, 2 * D_FF), CONV_F ** -0.5)
    ffn_down = nrm((L, D_FF, D_MODEL), D_FF ** -0.5)
    return {
        'x': x, 'meta_tokens': meta_tokens,
        'norm_mix_pre': norm_mix_pre, 'norm_mix_post': norm_mix_post,
        'norm_ffn_pre': norm_ffn_pre, 'norm_ffn_post': norm_ffn_post,
        'w_in': w_in, 'w_out': w_out,
        'lru_conv_w': lru_conv_w, 'lru_conv_b': lru_conv_b,
        'lru_gate_a_w': lru_gate_a_w, 'lru_gate_a_b': lru_gate_a_b,
        'lru_gate_x_w': lru_gate_x_w, 'lru_gate_x_b': lru_gate_x_b,
        'lru_lambda': lru_lambda, 'fox_f_bias': fox_f_bias,
        'rwkv_mu': rwkv_mu, 'rwkv_w0': rwkv_w0, 'rwkv_w_up': rwkv_w_up,
        'rwkv_a0': rwkv_a0, 'rwkv_a_up': rwkv_a_up, 'rwkv_g_up': rwkv_g_up,
        'rwkv_v0': rwkv_v0, 'rwkv_v_down': rwkv_v_down, 'rwkv_v_up': rwkv_v_up,
        'rwkv_k_k': rwkv_k_k, 'rwkv_k_a': rwkv_k_a, 'rwkv_r_k': rwkv_r_k,
        'rwkv_ln_w': rwkv_ln_w, 'rwkv_ln_b': rwkv_ln_b,
        'ffn_up': ffn_up, 'ffn_conv': ffn_conv, 'ffn_down': ffn_down,
    }

def first_block(x, meta_tokens, norm_mix_pre, norm_mix_post, norm_ffn_pre, norm_ffn_post,
              w_in, w_out, lru_conv_w, lru_conv_b, lru_gate_a_w, lru_gate_a_b,
              lru_gate_x_w, lru_gate_x_b, lru_lambda, fox_f_bias,
              rwkv_mu, rwkv_w0, rwkv_w_up, rwkv_a0, rwkv_a_up, rwkv_g_up,
              rwkv_v0, rwkv_v_down, rwkv_v_up, rwkv_k_k, rwkv_k_a, rwkv_r_k,
              rwkv_ln_w, rwkv_ln_b, ffn_up, ffn_conv, ffn_down):
    bsz = x.shape[0]
    meta = jnp.broadcast_to(meta_tokens.astype(x.dtype)[None], (bsz, N_META, D_MODEL))
    h = jnp.concatenate([meta, x], axis=1)
    v_first = None
    for l in range(DEPTH):
        p = rms_norm(h, norm_mix_pre[l]) @ w_in[l]
        pa = p[..., :A_COLS]
        pb = p[..., A_COLS:A_COLS + B_COLS]
        pc = p[..., A_COLS + B_COLS:]
        xa, ya = jnp.split(pa, 2, axis=-1)
        oa = rg_lru_group(xa, ya, lru_conv_w[l], lru_conv_b[l], lru_gate_a_w[l], lru_gate_a_b[l],
                          lru_gate_x_w[l], lru_gate_x_b[l], lru_lambda[l])
        ob = forgetting_attention_group(pb[..., :FOX_WIDTH], pb[..., FOX_WIDTH:2 * FOX_WIDTH],
                                        pb[..., 2 * FOX_WIDTH:3 * FOX_WIDTH], pb[..., 3 * FOX_WIDTH:],
                                        fox_f_bias[l])
        v_mix = None if l == 0 else (rwkv_v0[l - 1], rwkv_v_down[l - 1], rwkv_v_up[l - 1])
        oc, v_own = rwkv7_group(pc, rwkv_mu[l], rwkv_w0[l], rwkv_w_up[l], rwkv_a0[l], rwkv_a_up[l],
                                rwkv_g_up[l], rwkv_k_k[l], rwkv_k_a[l], rwkv_r_k[l],
                                rwkv_ln_w[l], rwkv_ln_b[l], v_first, v_mix)
        if l == 0:
            v_first = v_own
        mixed = jnp.concatenate([oa, ob, oc], axis=-1) @ w_out[l]
        h = h + rms_norm(mixed, norm_mix_post[l])
        f = causal_dwconv(rms_norm(h, norm_ffn_pre[l]) @ ffn_up[l], ffn_conv[l])
        gate, val = jnp.split(f, 2, axis=-1)
        f = (jax.nn.gelu(gate, approximate=True) * val) @ ffn_down[l]
        h = h + rms_norm(f, norm_ffn_post[l])
    return h[:, N_META:]


DEPTH_2 = 2

GRID_W = 64
CTX_LEN = 256
A_Q_HEADS = 8
A_KV_HEADS = 2
A_GROUP = A_Q_HEADS // A_KV_HEADS
A_WINDOW = 128
A_BLOCK = 128
B_HEADS = 4
NA_ROWS = 8
NA_COLS = 16
C_CHANNELS = 256
C_CONV_WIDTH = 31
A_Q_W = A_Q_HEADS * HEAD_DIM
A_KV_W = A_KV_HEADS * HEAD_DIM
B_W = B_HEADS * HEAD_DIM
MIX_WIDTH = A_Q_W + B_W + C_CHANNELS
IN_WIDTH = A_Q_W + 2 * A_KV_W + 3 * B_W + 2 * C_CHANNELS
OFF_AQ = 0
OFF_AK = OFF_AQ + A_Q_W
OFF_AV = OFF_AK + A_KV_W
OFF_BQ = OFF_AV + A_KV_W
OFF_BK = OFF_BQ + B_W
OFF_BV = OFF_BK + B_W
OFF_C = OFF_BV + B_W
N_EXPERTS = 16
EXPERT_FF = 1024
EC_CAPACITY = 2
ROPE_BASE = 10000.0
LN_EPS = 1e-6
N_MOD = 6
MOD_INIT = 0.5
DEEPNORM_ALPHA = (2 * DEPTH_2) ** 0.25
DEEPNORM_BETA = (8 * DEPTH_2) ** -0.25
NEG_INF = -1e30


def layer_norm(x, g=None, b=None):
    xf = x.astype(jnp.float32)
    mu = jnp.mean(xf, axis=-1, keepdims=True)
    var = jnp.mean(jnp.square(xf - mu), axis=-1, keepdims=True)
    y = (xf - mu) * lax.rsqrt(var + LN_EPS)
    if g is not None:
        y = y * g.astype(jnp.float32) + b.astype(jnp.float32)
    return y.astype(x.dtype)

def modulate(x, shift, scale):
    return layer_norm(x) * (1 + scale) + shift

def adaln(cond, w_mod_l, b_mod_l, n_chunks):
    m = jax.nn.silu(cond) @ w_mod_l[:, :n_chunks * D_MODEL] + b_mod_l[:n_chunks * D_MODEL]
    return jnp.split(m, n_chunks, axis=-1)

def split_heads(t, n_heads):
    return t.reshape(t.shape[:-1] + (n_heads, HEAD_DIM))

def axial_rope(n_tokens, dtype):
    t = jnp.arange(n_tokens, dtype=jnp.int32)
    row = (t // GRID_W).astype(jnp.float32)[:, None]
    col = (t % GRID_W).astype(jnp.float32)[:, None]
    n_freq = HEAD_DIM // 4
    inv_freq = ROPE_BASE ** (-jnp.arange(n_freq, dtype=jnp.float32) / n_freq)
    ang_r = row * inv_freq
    ang_c = col * inv_freq
    return (jnp.cos(ang_r)[:, None, :].astype(dtype), jnp.sin(ang_r)[:, None, :].astype(dtype),
            jnp.cos(ang_c)[:, None, :].astype(dtype), jnp.sin(ang_c)[:, None, :].astype(dtype))

def rope_half(x, cos, sin):
    x1, x2 = jnp.split(x, 2, axis=-1)
    return jnp.concatenate([x1 * cos - x2 * sin, x2 * cos + x1 * sin], axis=-1)

def apply_axial_rope(x, cos_r, sin_r, cos_c, sin_c):
    xr, xc = jnp.split(x, 2, axis=-1)
    return jnp.concatenate([rope_half(xr, cos_r, sin_r), rope_half(xc, cos_c, sin_c)], axis=-1)

def window_gqa_latent(q, k, v, kc, vc, sink):
    bsz, n_lat = q.shape[:2]
    n_blk = n_lat // A_BLOCK
    span = A_BLOCK + 2 * A_WINDOW
    pad = ((0, 0), (A_WINDOW, A_WINDOW), (0, 0), (0, 0))
    kp = jnp.pad(k, pad)
    vp = jnp.pad(v, pad)
    scale = HEAD_DIM ** -0.5
    sink_l = sink.reshape(1, A_KV_HEADS, A_GROUP, 1, 1).astype(jnp.float32)
    q_off = jnp.arange(A_BLOCK)
    k_off = jnp.arange(span) - A_WINDOW
    band = jnp.abs(k_off[None, :] - q_off[:, None]) <= A_WINDOW

    def block(i):
        start = i * A_BLOCK
        qb = lax.dynamic_slice_in_dim(q, start, A_BLOCK, axis=1)
        kb = lax.dynamic_slice_in_dim(kp, start, span, axis=1)
        vb = lax.dynamic_slice_in_dim(vp, start, span, axis=1)
        kpos = start + k_off
        valid = band & ((kpos >= 0) & (kpos < n_lat))[None, :]
        s_win = jnp.einsum('bqhgd,bkhd->bhgqk', qb, kb).astype(jnp.float32) * scale
        s_win = jnp.where(valid, s_win, NEG_INF)
        s_ctx = jnp.einsum('bqhgd,bkhd->bhgqk', qb, kc).astype(jnp.float32) * scale
        s_sink = jnp.broadcast_to(sink_l, s_win.shape[:-1] + (1,))
        p = jax.nn.softmax(jnp.concatenate([s_win, s_ctx, s_sink], axis=-1), axis=-1).astype(q.dtype)
        return (jnp.einsum('bhgqk,bkhd->bqhgd', p[..., :span], vb)
                + jnp.einsum('bhgqk,bkhd->bqhgd', p[..., span:span + kc.shape[1]], vc))

    out = lax.map(block, jnp.arange(n_blk))
    return jnp.moveaxis(out, 0, 1).reshape(bsz, n_lat, A_Q_W)

def context_gqa(qc, kc, vc, sink):
    s = jnp.einsum('bqhgd,bkhd->bhgqk', qc, kc).astype(jnp.float32) * HEAD_DIM ** -0.5
    s_sink = jnp.broadcast_to(sink.reshape(1, A_KV_HEADS, A_GROUP, 1, 1).astype(jnp.float32), s.shape[:-1] + (1,))
    p = jax.nn.softmax(jnp.concatenate([s, s_sink], axis=-1), axis=-1).astype(qc.dtype)
    o = jnp.einsum('bhgqk,bkhd->bqhgd', p[..., :-1], vc)
    return o.reshape(qc.shape[0], qc.shape[1], A_Q_W)

def neighbourhood_latent(q, k, v, kc, vc, rel_bias):
    bsz, n_lat = q.shape[:2]
    rows = n_lat // GRID_W
    kr_n = min(NA_ROWS, rows)
    n_keys = kr_n * GRID_W
    scale = HEAD_DIM ** -0.5
    qg = q.reshape(bsz, rows, GRID_W, B_HEADS, HEAD_DIM)
    kg = k.reshape(bsz, rows, GRID_W, B_HEADS, HEAD_DIM)
    vg = v.reshape(bsz, rows, GRID_W, B_HEADS, HEAD_DIM)
    cols = jnp.arange(GRID_W)
    c_start = jnp.clip(cols - NA_COLS // 2, 0, GRID_W - NA_COLS)
    col_mask = (cols[None, :] >= c_start[:, None]) & (cols[None, :] < c_start[:, None] + NA_COLS)
    mask = jnp.broadcast_to(col_mask[:, None, :], (GRID_W, kr_n, GRID_W)).reshape(GRID_W, n_keys)
    dc = jnp.clip(cols[None, :] - cols[:, None], -(NA_COLS - 1), NA_COLS - 1) + NA_COLS - 1

    def row(r):
        r_start = jnp.clip(r - kr_n // 2, 0, rows - kr_n)
        qr = lax.dynamic_index_in_dim(qg, r, axis=1, keepdims=False)
        kr = lax.dynamic_slice_in_dim(kg, r_start, kr_n, axis=1).reshape(bsz, n_keys, B_HEADS, HEAD_DIM)
        vr = lax.dynamic_slice_in_dim(vg, r_start, kr_n, axis=1).reshape(bsz, n_keys, B_HEADS, HEAD_DIM)
        dr = r_start + jnp.arange(kr_n) - r + NA_ROWS - 1
        bias = rel_bias[:, dr[None, :, None], dc[:, None, :]].reshape(B_HEADS, GRID_W, n_keys)
        s_nb = jnp.einsum('bqhd,bkhd->bhqk', qr, kr).astype(jnp.float32) * scale + bias.astype(jnp.float32)
        s_nb = jnp.where(mask, s_nb, NEG_INF)
        s_ctx = jnp.einsum('bqhd,bkhd->bhqk', qr, kc).astype(jnp.float32) * scale
        p = jax.nn.softmax(jnp.concatenate([s_nb, s_ctx], axis=-1), axis=-1).astype(q.dtype)
        return (jnp.einsum('bhqk,bkhd->bqhd', p[..., :n_keys], vr)
                + jnp.einsum('bhqk,bkhd->bqhd', p[..., n_keys:], vc))

    out = lax.map(row, jnp.arange(rows))
    return jnp.moveaxis(out, 0, 1).reshape(bsz, n_lat, B_W)

def context_mha(qc, kc, vc):
    s = jnp.einsum('bqhd,bkhd->bhqk', qc, kc).astype(jnp.float32) * HEAD_DIM ** -0.5
    p = jax.nn.softmax(s, axis=-1).astype(qc.dtype)
    o = jnp.einsum('bhqk,bkhd->bqhd', p, vc)
    return o.reshape(qc.shape[0], qc.shape[1], B_W)

def conformer_conv(u, conv_w, conv_b, ln_g, ln_b):
    a, gate = jnp.split(u, 2, axis=-1)
    h = a * jax.nn.sigmoid(gate)
    half = C_CONV_WIDTH // 2
    h = lax.conv_general_dilated(h, conv_w[:, None, :], window_strides=(1,), padding=((half, half),),
                                 dimension_numbers=('NWC', 'WIO', 'NWC'),
                                 feature_group_count=C_CHANNELS) + conv_b
    return jax.nn.silu(layer_norm(h, ln_g, ln_b))

def ec_moe(h, w_router, w_gate, w_up, w_down):
    bsz, n_tok, d = h.shape
    cap = EC_CAPACITY * n_tok // N_EXPERTS
    aff = jax.nn.softmax(jnp.einsum('bnd,de->bne', h, w_router).astype(jnp.float32), axis=-1)
    g, idx = lax.top_k(jnp.swapaxes(aff, 1, 2), cap)
    xs = jax.vmap(lambda hb, ib: hb[ib])(h, idx)
    hid = jax.nn.silu(jnp.einsum('becd,edf->becf', xs, w_gate)) * jnp.einsum('becd,edf->becf', xs, w_up)
    ye = jnp.einsum('becf,efd->becd', hid, w_down) * g[..., None].astype(h.dtype)
    return jax.vmap(lambda yb, ib: jnp.zeros((n_tok, d), h.dtype).at[ib.reshape(-1)].add(yb.reshape(-1, d)))(ye, idx)

def context_kv(hc, w_in_l):
    ka, va = jnp.split(hc @ w_in_l[:, OFF_AK:OFF_BQ], 2, axis=-1)
    kb, vb = jnp.split(hc @ w_in_l[:, OFF_BK:OFF_C], 2, axis=-1)
    return (split_heads(ka, A_KV_HEADS), split_heads(va, A_KV_HEADS),
            split_heads(kb, B_HEADS), split_heads(vb, B_HEADS))

def second_inputs(seed: int = 0) -> dict:
    key = jax.random.key(seed)
    ks = jax.random.split(key, 22)
    L, D = DEPTH_2, D_MODEL

    def nrm(k, shape, s):
        return s * jax.random.normal(k, shape, jnp.float32)

    return {
        'x': nrm(ks[0], (BATCH, SEQ, D), 1.0),
        'c': nrm(ks[1], (BATCH, D), 1.0),
        'ctx': nrm(ks[2], (BATCH, CTX_LEN, D), 1.0),
        'c_ctx': nrm(ks[3], (D,), 1.0),
        'w_mod': nrm(ks[4], (L, D, N_MOD * D), MOD_INIT * D ** -0.5),
        'b_mod': nrm(ks[5], (L, N_MOD * D), 0.02),
        'w_in': nrm(ks[6], (L, D, IN_WIDTH), D ** -0.5),
        'a_sink': nrm(ks[7], (L, A_Q_HEADS), 0.5),
        'nat_bias': nrm(ks[8], (L, B_HEADS, 2 * NA_ROWS - 1, 2 * NA_COLS - 1), 0.1),
        'conv_w': nrm(ks[9], (L, C_CONV_WIDTH, C_CHANNELS), C_CONV_WIDTH ** -0.5),
        'conv_b': nrm(ks[10], (L, C_CHANNELS), 0.02),
        'conv_ln_g': 1.0 + nrm(ks[11], (L, C_CHANNELS), 0.05),
        'conv_ln_b': nrm(ks[12], (L, C_CHANNELS), 0.02),
        'w_out': nrm(ks[13], (L, MIX_WIDTH, D), DEEPNORM_BETA * MIX_WIDTH ** -0.5),
        'ln1_g': 1.0 + nrm(ks[14], (L, D), 0.05),
        'ln1_b': nrm(ks[15], (L, D), 0.02),
        'w_router': nrm(ks[16], (L, D, N_EXPERTS), D ** -0.5),
        'w_gate': nrm(ks[17], (L, N_EXPERTS, D, EXPERT_FF), D ** -0.5),
        'w_up': nrm(ks[18], (L, N_EXPERTS, D, EXPERT_FF), D ** -0.5),
        'w_down': nrm(ks[19], (L, N_EXPERTS, EXPERT_FF, D), DEEPNORM_BETA * EXPERT_FF ** -0.5),
        'ln2_g': 1.0 + nrm(ks[20], (L, D), 0.05),
        'ln2_b': nrm(ks[21], (L, D), 0.02),
    }

def second_block(x, c, ctx, c_ctx, w_mod, b_mod, w_in, a_sink, nat_bias, conv_w, conv_b, conv_ln_g, conv_ln_b,
              w_out, ln1_g, ln1_b, w_router, w_gate, w_up, w_down, ln2_g, ln2_b):
    bsz, n_lat, _ = x.shape
    n_ctx = ctx.shape[1]
    rope = axial_rope(n_lat, x.dtype)
    for l in range(DEPTH_2):
        last = l == DEPTH_2 - 1
        w_in_l = w_in[l]
        sh1, sc1, g1, sh2, sc2, g2 = [m[:, None, :] for m in adaln(c, w_mod[l], b_mod[l], N_MOD)]

        ctx_mod = adaln(c_ctx, w_mod[l], b_mod[l], 2 if last else N_MOD)
        hc = modulate(ctx, ctx_mod[0], ctx_mod[1])
        kc_a, vc_a, kc_b, vc_b = context_kv(hc, w_in_l)
        if not last:
            qc_a = split_heads(hc @ w_in_l[:, OFF_AQ:OFF_AK], A_Q_HEADS).reshape(bsz, n_ctx, A_KV_HEADS, A_GROUP, HEAD_DIM)
            qc_b = split_heads(hc @ w_in_l[:, OFF_BQ:OFF_BK], B_HEADS)
            oc = jnp.concatenate([
                context_gqa(qc_a, kc_a, vc_a, a_sink[l]),
                context_mha(qc_b, kc_b, vc_b),
                conformer_conv(hc @ w_in_l[:, OFF_C:], conv_w[l], conv_b[l], conv_ln_g[l], conv_ln_b[l]),
            ], axis=-1) @ w_out[l]
            ctx_new = layer_norm(DEEPNORM_ALPHA * ctx + ctx_mod[2] * oc, ln1_g[l], ln1_b[l])
            hc2 = modulate(ctx_new, ctx_mod[3], ctx_mod[4])
            ctx_new = layer_norm(DEEPNORM_ALPHA * ctx_new + ctx_mod[5] * ec_moe(hc2, w_router[l], w_gate[l], w_up[l], w_down[l]),
                                 ln2_g[l], ln2_b[l])

        h = modulate(x, sh1, sc1)
        u = h @ w_in_l
        q_a = apply_axial_rope(split_heads(u[..., OFF_AQ:OFF_AK], A_Q_HEADS), *rope)
        k_a = apply_axial_rope(split_heads(u[..., OFF_AK:OFF_AV], A_KV_HEADS), *rope)
        v_a = split_heads(u[..., OFF_AV:OFF_BQ], A_KV_HEADS)
        q_b = split_heads(u[..., OFF_BQ:OFF_BK], B_HEADS)
        k_b = split_heads(u[..., OFF_BK:OFF_BV], B_HEADS)
        v_b = split_heads(u[..., OFF_BV:OFF_C], B_HEADS)
        o_a = window_gqa_latent(q_a.reshape(bsz, n_lat, A_KV_HEADS, A_GROUP, HEAD_DIM), k_a, v_a, kc_a, vc_a, a_sink[l])
        o_b = neighbourhood_latent(q_b, k_b, v_b, kc_b, vc_b, nat_bias[l])
        o_c = conformer_conv(u[..., OFF_C:], conv_w[l], conv_b[l], conv_ln_g[l], conv_ln_b[l])
        o = jnp.concatenate([o_a, o_b, o_c], axis=-1) @ w_out[l]
        x = layer_norm(DEEPNORM_ALPHA * x + g1 * o, ln1_g[l], ln1_b[l])
        h2 = modulate(x, sh2, sc2)
        x = layer_norm(DEEPNORM_ALPHA * x + g2 * ec_moe(h2, w_router[l], w_gate[l], w_up[l], w_down[l]),
                       ln2_g[l], ln2_b[l])
        if not last:
            ctx = ctx_new
    return x


def setup_inputs(seed=0):
    out = dict(first_inputs(seed))
    for name, value in second_inputs(seed + 1).items():
        if name != "x":
            out[name + "_2"] = value
    return out


def reference(
    x, meta_tokens, norm_mix_pre, norm_mix_post, norm_ffn_pre, norm_ffn_post, w_in, w_out,
    lru_conv_w, lru_conv_b, lru_gate_a_w, lru_gate_a_b, lru_gate_x_w, lru_gate_x_b, lru_lambda,
    fox_f_bias, rwkv_mu, rwkv_w0, rwkv_w_up, rwkv_a0, rwkv_a_up, rwkv_g_up, rwkv_v0,
    rwkv_v_down, rwkv_v_up, rwkv_k_k, rwkv_k_a, rwkv_r_k, rwkv_ln_w, rwkv_ln_b, ffn_up,
    ffn_conv, ffn_down, c_2, ctx_2, c_ctx_2, w_mod_2, b_mod_2, w_in_2, a_sink_2, nat_bias_2,
    conv_w_2, conv_b_2, conv_ln_g_2, conv_ln_b_2, w_out_2, ln1_g_2, ln1_b_2, w_router_2,
    w_gate_2, w_up_2, w_down_2, ln2_g_2, ln2_b_2,
):
    x = first_block(
        x, meta_tokens, norm_mix_pre, norm_mix_post, norm_ffn_pre, norm_ffn_post, w_in, w_out,
        lru_conv_w, lru_conv_b, lru_gate_a_w, lru_gate_a_b, lru_gate_x_w, lru_gate_x_b,
        lru_lambda, fox_f_bias, rwkv_mu, rwkv_w0, rwkv_w_up, rwkv_a0, rwkv_a_up, rwkv_g_up,
        rwkv_v0, rwkv_v_down, rwkv_v_up, rwkv_k_k, rwkv_k_a, rwkv_r_k, rwkv_ln_w, rwkv_ln_b,
        ffn_up, ffn_conv, ffn_down,
    )
    return second_block(
        x, c_2, ctx_2, c_ctx_2, w_mod_2, b_mod_2, w_in_2, a_sink_2, nat_bias_2, conv_w_2,
        conv_b_2, conv_ln_g_2, conv_ln_b_2, w_out_2, ln1_g_2, ln1_b_2, w_router_2, w_gate_2,
        w_up_2, w_down_2, ln2_g_2, ln2_b_2,
    )


_drawn_inputs = setup_inputs


def setup_inputs(seed=0):
    import zlib

    import numpy as np

    out = dict(_drawn_inputs(seed))
    spreads = {}
    factors = {'lru_gate_a_b': 29.652,
     'lru_gate_x_b': 8.0,
     'rwkv_w_up': 8.0,
     'rwkv_ln_b': 5.088,
     'ctx_2': 7.267,
     'c_ctx_2': 2.995,
     'b_mod_2': 8.0,
     'a_sink_2': 42.024,
     'nat_bias_2': 64.0,
     'conv_b_2': 8.0,
     'conv_ln_g_2': 22.104,
     'conv_ln_b_2': 53.144}
    for name, (base, spread) in spreads.items():
        noise = np.random.default_rng([zlib.crc32(name.encode()), seed]).standard_normal(out[name].shape)
        drawn = base * np.exp(spread * noise) if base else spread * noise
        out[name] = jnp.asarray(drawn.astype(out[name].dtype))
    for name, factor in factors.items():
        out[name] = (out[name] * factor).astype(out[name].dtype)
    return out
```

```python
from contextlib import ExitStack

import numpy as np

import concourse.bass as bass
from concourse import mybir

F32 = mybir.dt.float32
ALU = mybir.AluOpType
ACT = mybir.ActivationFunctionType
AX = mybir.AxisListType

P = 128
D = 1024
KD = D // P
SEQ = 512
N_META = 16
T1 = SEQ + N_META
HALF1 = T1 // 2
HD = 64
BANK = 512
NEG = -1e30

LRU_W = 256
FOX_W = 512
FOX_HEADS = FOX_W // HD
RW = 256
RW_HEADS = RW // HD
D_FF = 2816
FT = D_FF // P
CH = 16
NCH = T1 // CH
CPT = P // CH
EXP_HALF = float(np.exp(-0.5))
GN_EPS = 64e-5
RMS_EPS = 1e-6

CTX = 256
T2 = SEQ + CTX
NT2 = T2 // P
NTL = SEQ // P
LAYERS = 2
A_WIDTH = 512
CW = 31
CH_HALF = CW // 2
N_EXP = 16
CAP_L = 2 * SEQ // N_EXP
CAP_C = 2 * CTX // N_EXP
SLOTS = CAP_L + CAP_C
FF = 1024
ALPHA = float((2 * LAYERS) ** 0.25)
LN_EPS = 1e-6
GRID_W = 64
GRID_H = SEQ // GRID_W
NA_COLS = 16
BIAS_ROWS = 2 * GRID_H - 1
BIAS_PAD = 128

RING = 8
CHUNK = 2048


def constants():
    p = np.arange(P)
    f = np.float32
    parts = {}
    parts["ident"] = np.eye(P)
    parts["ones"] = np.ones((P, P))
    parts["head_ones"] = (p[:, None] // HD == p[None, :] // HD)
    parts["causal"] = np.where(p[None, :] <= p[:, None], 0, NEG)
    parts["band_prev"] = np.where(p[None, :] >= p[:, None], 0, NEG)
    parts["band_next"] = np.where(p[None, :] <= p[:, None], 0, NEG)
    same = p[:, None] // CH == p[None, :] // CH
    upper = same & (p[:, None] < p[None, :])
    upper_in = same & (p[:, None] <= p[None, :])
    lower = same & (p[:, None] > p[None, :])
    parts["mask_u"] = np.concatenate([-1.0 * upper, 1.0 * upper], 1)
    parts["mask_o"] = np.concatenate([-1.0 * upper_in, 1.0 * upper_in], 1)
    parts["mask_l"] = -1.0 * lower
    parts["chunk_of"] = (p[:, None] // CH == np.arange(CPT)[None, :])
    parts["eye_head"] = (p[:, None] % HD == np.arange(HD)[None, :])
    parts["scan_keep"] = np.broadcast_to(np.arange(T1) % CH != 0, (P, T1))
    first_only = len(parts)
    parts["iota"] = np.broadcast_to(np.arange(CAP_L), (P, CAP_L))
    rot = np.zeros((P, P))
    for m in range(P):
        first = (m % 32) < 16
        rot[m + 16 if first else m - 16, m] = -1.0 if first else 1.0
    parts["rot"] = rot
    n_freq = HD // 4
    inv = (f(10000.0) ** (-np.arange(n_freq, dtype=f) / f(n_freq))).astype(f)
    t = np.arange(SEQ)
    ang = np.zeros((P, SEQ), f)
    for m in range(P):
        pos = (t // GRID_W if (m % HD) < 32 else t % GRID_W).astype(f)
        ang[m] = pos * inv[m % 16]
    parts["cos"] = np.cos(ang)
    parts["sin"] = np.sin(ang)
    parts["flip"] = (p[:, None] // GRID_W == p[None, :] // GRID_W) & (p[:, None] % GRID_W + p[None, :] % GRID_W == GRID_W - 1)
    qc = p % GRID_W
    c0 = np.clip(qc - NA_COLS // 2, 0, GRID_W - NA_COLS)
    kc = np.arange(GRID_W)
    parts["col_mask"] = np.where((kc[None] >= c0[:, None]) & (kc[None] < c0[:, None] + NA_COLS), 0, NEG)
    both = ("ident", "ones")
    first = [n for i, n in enumerate(parts) if i < first_only and n not in both and not n.startswith("band")]
    second = [n for n in parts if n not in both and n not in first]
    packed = []
    for names in (both, first, second):
        at, n = {}, 0
        for name in names:
            at[name] = (n, parts[name].shape[1])
            n += parts[name].shape[1]
        packed.append((np.ascontiguousarray(np.concatenate([np.asarray(parts[x], f) for x in names], 1)), at))
    return packed


CONSTS = constants()

COLS1 = ["norm_mix_pre", "norm_ffn_pre", "lru_conv_w", "lru_conv_b", "lru_gate_a_b", "lru_gate_x_b",
         "lru_lambda", "rwkv_mu", "rwkv_w0", "rwkv_a0", "rwkv_k_k", "rwkv_k_a", "rwkv_r_k", "rwkv_ln_w",
         "rwkv_ln_b", "fox_f_bias", "w_f", "gate_a", "gate_x", "wa_up", "g_up", "ffn_conv"]
WIDTH1 = dict(norm_mix_pre=8, norm_ffn_pre=8, lru_conv_w=8, lru_conv_b=2, lru_gate_a_b=2, lru_gate_x_b=2,
              lru_lambda=2, rwkv_mu=8, rwkv_w0=2, rwkv_a0=2, rwkv_k_k=2, rwkv_k_a=2, rwkv_r_k=2,
              rwkv_ln_w=2, rwkv_ln_b=2, fox_f_bias=1, w_f=8 * FOX_HEADS, gate_a=256, gate_x=256,
              wa_up=256, g_up=256, ffn_conv=3 * 44)
COLS2 = ["b_mod", "conv_w", "conv_b", "ln_g", "ln_b", "router", "sink"]
WIDTH2 = dict(b_mod=48, conv_w=2 * CW, conv_b=2, ln_g=2, ln_b=2, router=8 * N_EXP, sink=8)


def offsets(names, widths):
    at, n = {}, 0
    for name in names:
        at[name] = n
        n += widths[name]
    return at, n


AT1, NP1 = offsets(COLS1, WIDTH1)
AT2, NP2 = offsets(COLS2, WIDTH2)

N_IN, N_OUT, N_UP, N_DOWN = 12, 4, FT, FT // 2
N_MOD, N_IN2, N_OUT2 = 24, 8, 4
FIRST_CHUNKS = N_IN + N_OUT + N_UP + N_DOWN
LAYER_CHUNKS = N_MOD + N_IN2 + N_OUT2


class Signal:

    def __init__(self, sem):
        self.sem, self.base = sem, 0

    def of(self, n):
        return self.base + n

    def close(self, n):
        self.base += n


class Steps:

    def __init__(self, eng, sem):
        self.eng, self.sem, self.n = eng, sem, 0

    def __call__(self, ins):
        self.free(ins)
        self.join()

    def free(self, ins):
        ins.then_inc(self.sem, 1)
        self.n += 1

    def join(self):
        self.eng.wait_ge(self.sem, self.n)

    def tell(self, sem):
        self.join()
        self.eng.sem_inc(sem, 1)


class Stream:

    def __init__(self, ring, loaded, chunks):
        self.ring, self.loaded, self.chunks = ring, loaded, chunks
        self.issued = self.taken = 0
        self.limit = len(chunks)
        self.freed_by = {}

    def take(self):
        self.taken += 1
        return self.taken - 1

    def slot(self, n):
        return self.ring[:, n % RING, :]

    def wait(self, eng, n):
        eng.wait_ge(self.loaded[n % RING], 16 * (n // RING + 1))

    def freed(self, n, sem, value):
        self.freed_by[n] = (sem, value)

    def issue(self, sp):
        while self.issued < self.limit and (self.issued < RING or self.issued - RING in self.freed_by):
            n = self.issued
            if n >= RING:
                sp.wait_ge(*self.freed_by[n - RING])
            sp.dma_start(self.slot(n), self.chunks[n]).then_inc(self.loaded[n % RING], 16)
            self.issued += 1


class Kernel:
    pass


def split(off, width):
    out, at = [], 0
    while at < width:
        n = min(width - at, BANK - (off + at) % BANK)
        out.append((at, n))
        at += n
    return out


def products(k, groups, evacuate):
    nc = k.nc
    ready, free_v, free_s = k.sig["product"], k.sig["taken_v"], k.sig["taken_s"]
    places = groups[0]["places"]

    def turn(i):
        return i // 2 + 1

    with nc.Block() as block:
        @block.tensor
        def _(pe):
            for i, g in enumerate(groups):
                for n in g.get("needs", ()):
                    k.stream.wait(pe, n)
                if i >= places:
                    before = i - places
                    free = free_v if before % 2 == 0 else free_s
                    pe.wait_ge(free.sem, free.of(turn(before)))
                for out, lhsT, rhs, start, stop in g.get("mm", ()):
                    mm = pe.matmul(out, lhsT, rhs, start=start, stop=stop, skip_group_check=True)
                for out, src, n in g.get("tr", ()):
                    mm = pe.transpose(out, src, k.c("ident")[0:n, 0:n])
                mm.then_inc(ready.sem, 1)
                for n in g.get("last", ()):
                    k.stream.freed(n, ready.sem, ready.of(i + 1))

        @block.vector
        def _(dve):
            steps = k.steps(dve, "v")
            for i in range(0, len(groups), 2):
                dve.wait_ge(ready.sem, ready.of(i + 1))
                finish(steps, free_v.sem, evacuate(k, "v", i, steps))
            dve.wait_ge(free_v.sem, free_v.of((len(groups) + 1) // 2))

        @block.scalar
        def _(act):
            steps = k.steps(act, "s")
            for i in range(1, len(groups), 2):
                act.wait_ge(ready.sem, ready.of(i + 1))
                finish(steps, free_s.sem, evacuate(k, "s", i, steps))
            if len(groups) > 1:
                act.wait_ge(free_s.sem, free_s.of(len(groups) // 2))

        @block.sync
        def _(sp):
            k.stream.issue(sp)
    ready.close(len(groups))
    free_v.close((len(groups) + 1) // 2)
    free_s.close(len(groups) // 2)


def finish(steps, sem, made):
    if isinstance(made, list):
        for x in made:
            steps.free(x)
        steps.tell(sem)
    else:
        made.then_inc(sem, 1)


def copy_out(k, who, out, src, scale=None, bias=None):
    nc = k.nc
    if who == "v":
        if scale is None and bias is None:
            return nc.vector.tensor_copy(out, src)
        if bias is None:
            return nc.vector.tensor_scalar(out, src, scale, None, ALU.mult)
        if scale is None:
            return nc.vector.tensor_scalar(out, src, bias, None, ALU.add)
        return nc.vector.tensor_scalar(out, src, scale, bias, ALU.mult, ALU.add)
    kw = {}
    if scale is not None:
        kw["scale"] = scale
    if bias is not None:
        kw["bias"] = bias
    return nc.scalar.activation(out, src, ACT.Identity, **kw)


def load(k, pairs):
    loads = k.sig["load"]
    with k.nc.Block() as block:
        @block.sync
        def _(sp):
            for dst, src in pairs:
                sp.dma_start(dst, src).then_inc(loads.sem, 16)
            k.stream.issue(sp)
            sp.wait_ge(loads.sem, loads.of(16 * len(pairs)))
    loads.close(16 * len(pairs))


def to_channels(k, tiles, dst, scale, bias=None):
    groups, todo = [], []
    for src, n, at, which in tiles:
        for c in range(0, KD, 4):
            bank = len(groups) % 8
            groups.append(dict(places=8, tr=[(k.ps[0:P, bank, j * P:j * P + n], src[:, (c + j) * P:(c + j + 1) * P], n)
                                             for j in range(4)]))
            todo.append((bank, c, n, at, which))

    def take(k, who, i, steps):
        bank, c, n, at, which = todo[i]
        return [copy_out(k, who, dst[:, c + j, at:at + n], k.ps[:, bank, j * P:j * P + n],
                         scale(which, c + j), bias(which, c + j) if bias else None) for j in range(4)]
    products(k, groups, take)


def attention(k, units):
    nc = k.nc
    sg = k.sig
    scores, maxed, exped, probs = sg["scores"], sg["row_max"], sg["exp"], sg["probs"]
    turned, pt_ready, out_ready, out_taken = sg["turned"], sg["pt"], sg["out"], sg["out_taken"]
    N = len(units)
    with ExitStack() as ctx:
        sb = k.alloc(ctx)
        prob = sb("prob", [P, 2, BANK * 2])
        probT = sb("probT", [P, 2, 6, P])
        nmax = sb("nmax", [P, 4])
        rsum = sb("rsum", [P, 4])
        rinv = sb("rinv", [P, 4])
        S = [k.psf[:, 2 * BANK * s:2 * BANK * (s + 1)] for s in range(2)]
        T = k.psf[:, 4 * BANK:6 * BANK].rearrange("p (t q) -> p t q", q=P)
        O = [k.psf[:, (6 + s) * BANK:(7 + s) * BANK] for s in range(2)]

        def full(u):
            return u["width"] + (u["sink"] is not None)

        with nc.Block() as block:
            @block.tensor
            def _(pe):
                def score(i):
                    u, qn = units[i], units[i]["q"].shape[1]
                    if i >= 2:
                        pe.wait_ge(exped.sem, exped.of(i - 1))
                    for col, terms in u["scores"]:
                        width = terms[0][1].shape[1]
                        for at, n in split(col, width):
                            for t, (lhsT, rhs) in enumerate(terms):
                                mm = pe.matmul(S[i % 2][0:qn, col + at:col + at + n], lhsT, rhs[:, at:at + n],
                                               start=t == 0, stop=t == len(terms) - 1, skip_group_check=True)
                    mm.then_inc(scores.sem, 1)

                def turn(i):
                    u, qn = units[i], units[i]["q"].shape[1]
                    pe.wait_ge(probs.sem, probs.of(i + 1))
                    if i >= 1:
                        pe.wait_ge(pt_ready.sem, pt_ready.of(i))
                    for t, (v, kn, col) in enumerate(u["values"]):
                        mm = pe.transpose(T[0:kn, t, 0:qn], prob[0:qn, i % 2, col:col + kn], k.c("ident")[0:qn, 0:qn])
                    mm.then_inc(turned.sem, 1)

                def mix(i):
                    u, qn = units[i], units[i]["q"].shape[1]
                    pe.wait_ge(pt_ready.sem, pt_ready.of(i + 1))
                    if i >= 2:
                        pe.wait_ge(out_taken.sem, out_taken.of(i - 1))
                    b = u["base"]
                    for t, (v, kn, col) in enumerate(u["values"]):
                        mm = pe.matmul(O[i % 2][b:b + HD, 0:qn], v, probT[0:kn, i % 2, t, 0:qn],
                                       start=t == 0, stop=t == len(u["values"]) - 1, skip_group_check=True)
                    mm.then_inc(out_ready.sem, 1)

                score(0)
                for i in range(N):
                    if i + 1 < N:
                        score(i + 1)
                    turn(i)
                    if i >= 1:
                        mix(i - 1)
                mix(N - 1)

            @block.vector
            def _(dve):
                steps = k.steps(dve, "v")

                def row_max(i):
                    u, qn = units[i], units[i]["q"].shape[1]
                    dve.wait_ge(scores.sem, scores.of(i + 1))
                    for col, mask in u["adds"]:
                        s = S[i % 2][0:qn, col:col + mask.shape[1]]
                        steps.free(dve.tensor_tensor(s, s, mask, ALU.add))
                    if u["sink"] is not None:
                        steps.free(dve.tensor_copy(S[i % 2][0:qn, u["width"]:u["width"] + 1], u["sink"]))
                    steps.join()
                    steps(dve.tensor_reduce(nmax[0:qn, i % 4:i % 4 + 1], S[i % 2][0:qn, 0:full(u)], AX.X, ALU.max))
                    dve.tensor_scalar(nmax[0:qn, i % 4:i % 4 + 1], nmax[0:qn, i % 4:i % 4 + 1], -1.0, None,
                                      ALU.mult).then_inc(maxed.sem, 1)

                def normalise(i):
                    u, qn = units[i], units[i]["q"].shape[1]
                    dve.wait_ge(exped.sem, exped.of(i + 1))
                    steps(dve.reciprocal(rinv[0:qn, i % 4:i % 4 + 1], rsum[0:qn, i % 4:i % 4 + 1]))
                    pr = prob[0:qn, i % 2, 0:u["width"]]
                    dve.tensor_scalar(pr, pr, rinv[0:qn, i % 4:i % 4 + 1], None, ALU.mult).then_inc(probs.sem, 1)

                def take(i):
                    u, qn = units[i], units[i]["q"].shape[1]
                    dve.wait_ge(out_ready.sem, out_ready.of(i + 1))
                    dve.tensor_copy(u["out"], O[i % 2][u["base"]:u["base"] + HD, 0:qn]).then_inc(out_taken.sem, 1)

                row_max(0)
                for i in range(N):
                    if i + 1 < N:
                        row_max(i + 1)
                    normalise(i)
                    if i >= 2:
                        take(i - 2)
                for i in range(max(N - 2, 0), N):
                    take(i)
                dve.wait_ge(out_taken.sem, out_taken.of(N))

            @block.scalar
            def _(act):
                def exps(i):
                    u, qn = units[i], units[i]["q"].shape[1]
                    act.wait_ge(maxed.sem, maxed.of(i + 1))
                    if i >= 2:
                        act.wait_ge(turned.sem, turned.of(i - 1))
                    act.activation(prob[0:qn, i % 2, 0:full(u)], S[i % 2][0:qn, 0:full(u)], ACT.Exp,
                                   bias=nmax[0:qn, i % 4:i % 4 + 1],
                                   accum_out=rsum[0:qn, i % 4:i % 4 + 1]).then_inc(exped.sem, 1)

                steps = k.steps(act, "s")

                def copies(i):
                    u, qn = units[i], units[i]["q"].shape[1]
                    act.wait_ge(turned.sem, turned.of(i + 1))
                    if i >= 2:
                        act.wait_ge(out_ready.sem, out_ready.of(i - 1))
                    whole = sum(kn == P for _, kn, _ in u["values"])
                    rest = u["values"][whole:]
                    last = act.copy(probT[:, i % 2, 0:whole, 0:qn], T[:, 0:whole, 0:qn])
                    if rest:
                        steps(last)
                        kn = rest[0][1]
                        last = act.copy(probT[0:kn, i % 2, whole, 0:qn], T[0:kn, whole, 0:qn])
                    last.then_inc(pt_ready.sem, 1)

                exps(0)
                for i in range(N):
                    if i + 1 < N:
                        exps(i + 1)
                    copies(i)
                act.wait_ge(pt_ready.sem, pt_ready.of(N))

            @block.sync
            def _(sp):
                k.stream.issue(sp)
    for s in (scores, maxed, exped, probs, turned, pt_ready, out_ready, out_taken):
        s.close(N)


def token_tiles(src_x, src_meta):
    return [(src_meta, N_META, 0, 0)] + [(src_x[:, j, :], P, N_META + P * j, 0) for j in range(NTL)]


def rms_scale(k, jobs):
    nc = k.nc
    squared, rooted, meant = k.sig["squared"], k.sig["rooted"], k.sig["meant"]
    with ExitStack() as ctx:
        sb = k.alloc(ctx)
        junk = sb("junk", [P, 2, D])
        ssq = sb("ssq", [P, 8])
        root = sb("root", [P, 8])
        with nc.Block() as block:
            @block.scalar
            def _(act):
                for i, (x, out, n, gain, res) in enumerate(jobs):
                    if i >= 2:
                        act.wait_ge(squared.sem, squared.of(i - 1))
                    act.activation(junk[0:n, i % 2, :], x, ACT.Square,
                                   accum_out=ssq[0:n, i:i + 1]).then_inc(squared.sem, 1)
                for i, (x, out, n, gain, res) in enumerate(jobs):
                    act.wait_ge(meant.sem, meant.of(i + 1))
                    act.activation(root[0:n, i:i + 1], ssq[0:n, i:i + 1], ACT.Sqrt).then_inc(rooted.sem, 1)

            @block.vector
            def _(dve):
                steps = k.steps(dve, "v")
                for i, (x, out, n, gain, res) in enumerate(jobs):
                    dve.wait_ge(squared.sem, squared.of(i + 1))
                    dve.tensor_scalar(ssq[0:n, i:i + 1], ssq[0:n, i:i + 1], 1.0 / D, RMS_EPS, ALU.mult,
                                      ALU.add).then_inc(meant.sem, 1)
                for i, (x, out, n, gain, res) in enumerate(jobs):
                    dve.wait_ge(rooted.sem, rooted.of(i + 1))
                    steps(dve.reciprocal(root[0:n, i:i + 1], root[0:n, i:i + 1]))
                    if gain is None:
                        steps.free(dve.tensor_scalar(out, x, root[0:n, i:i + 1], None, ALU.mult))
                    else:
                        steps(dve.scalar_tensor_tensor(out, x, root[0:n, i:i + 1], gain, ALU.mult, ALU.mult))
                        steps.free(dve.tensor_tensor(res, out, res, ALU.add))
                steps.join()

            @block.sync
            def _(sp):
                k.stream.issue(sp)
    for s in (squared, rooted, meant):
        s.close(len(jobs))


def project_channels(k, hT, tiles, take):
    groups = []
    for i, (w, m, needs, last, *_) in enumerate(tiles):
        slot = i % 4
        mm = [(k.ps[0:m, 2 * slot + h, 0:HALF1], w(c), hT[:, c, h * HALF1:(h + 1) * HALF1], c == 0, c == KD - 1)
              for c in range(KD) for h in range(2)]
        groups.append(dict(places=4, mm=mm, needs=needs, last=last))

    def evacuate(k, who, i, steps):
        slot = i % 4
        m = tiles[i][1]
        return take(who, i, k.ps[0:m, 2 * slot:2 * slot + 2, 0:HALF1], steps)
    products(k, groups, evacuate)


def halves(ap):
    return ap.rearrange("p (h t) -> p h t", h=2)


def first_block(k):
    nc = k.nc
    stream, c1 = k.stream, k.c1
    d = k.dram
    with ExitStack() as ctx:
        sb = k.alloc(ctx)
        hT = sb("hT", [P, KD, T1])
        OT = sb("OT", [P, 2, T1])
        with ExitStack() as inner:
            sbi = k.alloc(inner)
            xt = sbi("xt", [P, NTL, D])
            mt = sbi("mt", [N_META, D])
            load(k, [(xt[:, :, :], d["x"]), (mt[:, :], d["meta"])])
            rms_scale(k, [(mt[:, :], mt[:, :], N_META, None, None)] +
                      [(xt[:, j, :], xt[:, j, :], P, None, None) for j in range(NTL)])
            to_channels(k, token_tiles(xt, mt[:, :]), hT, lambda w, c: c1("norm_mix_pre", c))
        delta_rule(k, hT, OT)
        k.stream.limit = k.moe_at[0]
        mixT = sb("mixT", [P, 6, T1])
        recurrence(k, hT, mixT)
        forgetting(k, hT, mixT)
        mix_out(k, sb, mixT, OT)
    feed_forward(k)


def column_chunk(k, n, j):
    s = k.stream.slot(n).rearrange("p (k c) -> p k c", k=KD)
    return lambda c: s[:, c, j * P:(j + 1) * P]


def column_tiles(k, count):
    out = []
    for _ in range(count):
        n = k.stream.take()
        out.append((column_chunk(k, n, 0), P, [n], []))
        out.append((column_chunk(k, n, 1), P, [], [n]))
    return out


def delta_rule(k, hT, OT):
    nc = k.nc
    c1, c = k.c1, k.c
    GT = [(0, 1), (2, 3), (4,)]
    with ExitStack() as ctx:
        sb = k.alloc(ctx)
        G = sb("G", [P, 2, T1])
        bonusT = sb("bonusT", [P, 2, T1])
        kap = sb("kap", [P, 2, T1])
        bet = sb("bet", [P, 2, T1])
        kti = sb("kti", [P, 2, T1])
        rho = sb("rho", [P, 2, T1])
        bend = sb("bend", [P, 2, T1])
        kend = sb("kend", [P, 2, T1])
        vv = sb("vv", [P, 2, T1])
        Wend = sb("Wend", [P, 2, NCH])
        with ExitStack() as inner:
            sbi = k.alloc(inner)
            pc = sbi("pc", [P, 8, T1 + 1])

            def take(who, i, src, steps):
                return copy_out(k, who, halves(pc[:, i, 1:T1 + 1]), src)
            with nc.Block() as block:
                @block.vector
                def _(dve):
                    steps = k.steps(dve, "v")
                    steps(dve.memset(pc[:, :, 0:1], 0.0))
            project_channels(k, hT, column_tiles(k, 4), take)
            rwkv_inputs(k, sbi, pc, G, bonusT, kap, bet, kti, rho, bend, kend, vv, Wend)
        with ExitStack() as inner:
            sbi = k.alloc(inner)
            X = sbi("X", [P, 2, HD])
            with nc.Block() as block:
                @block.vector
                def _(dve):
                    steps = k.steps(dve, "v")
                    steps(dve.memset(X[:, :, :], 0.0))
            for tiles in GT:
                with ExitStack() as scope:
                    chunk_group(k, k.alloc(scope), tiles, X, OT, kap, bet, kti, rho, bend, kend, vv, Wend)
        with ExitStack() as inner:
            group_norm(k, k.alloc(inner), OT, bonusT, G)


def rwkv_inputs(k, sb, pc, G, bonusT, kap, bet, kti, rho, bend, kend, vv, Wend):
    nc, c1, c = k.nc, k.c1, k.c
    t1 = sb("t1", [P, 8, T1])
    a = t1[:, 0:2, :]
    sg = t1[:, 2:4, :]
    kk = t1[:, 4:6, :]
    tmp = t1[:, 6:8, :]
    cum = sb("cum", [P, 2, T1])
    low, fine, fin2 = k.sig["low"], k.sig["fine"], k.sig["fin2"]
    r, kr, v = pc[:, 0:2, 1:], pc[:, 2:4, 1:], pc[:, 4:6, 1:]
    with nc.Block() as block:
        @block.vector
        def _(dve):
            steps = k.steps(dve, "v")
            steps(dve.tensor_tensor(t1[:, :, :], pc[:, :, 0:T1], pc[:, :, 1:T1 + 1], ALU.subtract))
            for i in range(8):
                x = pc[:, i, 1:T1 + 1]
                steps.free(dve.scalar_tensor_tensor(x, t1[:, i, :], c1("rwkv_mu", i), x, ALU.mult, ALU.add))
            steps.join()

        @block.sync
        def _(sp):
            k.stream.issue(sp)
    with nc.Block() as block:
        @block.scalar
        def _(act):
            steps = k.steps(act, "s")
            steps(act.activation(pc[0:HD, 6, 1:], pc[0:HD, 6, 1:], ACT.Tanh))
            steps(act.activation(pc[:, 7, 1:], pc[:, 7, 1:], ACT.Sigmoid))
    up = k.c1m("wa_up", 256)
    gu = k.c1m("g_up", 256)
    wt, at_, gt = pc[0:HD, 6, 1:], pc[HD:P, 6, 1:], pc[:, 7, 1:]
    groups, where = [], []
    for kind, (w, x, b) in enumerate(((up[0:HD], wt, 0), (up[HD:P], at_, 1), (gu, gt, 0))):
        for g in range(2):
            slot = len(groups) % 4
            groups.append(dict(places=4, mm=[(k.ps[:, 2 * slot + h, 0:HALF1], w[:, g * P:(g + 1) * P],
                                              x[:, h * HALF1:(h + 1) * HALF1], True, True) for h in range(2)]))
            where.append((kind, g))

    def take(k, who, i, steps):
        kind, g = where[i]
        src = k.ps[:, 2 * (i % 4):2 * (i % 4) + 2, 0:HALF1]
        dst = (sg, a, G)[kind][:, g, :]
        return copy_out(k, who, halves(dst), src)
    products(k, groups, take)
    with nc.Block() as block:
        @block.scalar
        def _(act):
            for g in range(2):
                act.activation(sg[:, g, :], sg[:, g, :], ACT.Sigmoid, bias=c1("rwkv_w0", g)).then_inc(low.sem, 1)
            for g in range(2):
                act.activation(a[:, g, :], a[:, g, :], ACT.Sigmoid, bias=c1("rwkv_a0", g)).then_inc(low.sem, 1)
            act.wait_ge(fine.sem, fine.of(1))
            act.activation(rho[:, :, :], cum[:, :, :], ACT.Exp, scale=-EXP_HALF).then_inc(fin2.sem, 1)
            act.activation(kti[:, :, :], cum[:, :, :], ACT.Exp, scale=EXP_HALF).then_inc(fin2.sem, 1)
            act.wait_ge(fine.sem, fine.of(3))
            act.activation(kap[:, :, :], sg[:, :, :], ACT.Exp, scale=-EXP_HALF).then_inc(fin2.sem, 1)
            act.activation(kend[:, :, :], bend[:, :, :], ACT.Exp, scale=-EXP_HALF).then_inc(fin2.sem, 1)
            act.wait_ge(fin2.sem, fin2.of(4))

        @block.vector
        def _(dve):
            steps = k.steps(dve, "v")
            dve.wait_ge(low.sem, low.of(2))
            for g in range(2):
                steps.free(dve.tensor_tensor_scan(cum[:, g, :], c("scan_keep"), sg[:, g, :], 0.0, ALU.mult, ALU.add))
            steps.tell(fine.sem)
            dve.tensor_tensor(sg[:, :, :], cum[:, :, :], sg[:, :, :], ALU.subtract).then_inc(fine.sem, 1)
            for g in range(2):
                e = cum[:, g, CH - 1:T1:CH].unsqueeze(2).to_broadcast([P, NCH, CH])
                x = dve.tensor_tensor(bend[:, g, :].rearrange("p (c t) -> p c t", t=CH), e,
                                      cum[:, g, :].rearrange("p (c t) -> p c t", t=CH), ALU.subtract)
                steps.free(x)
            steps.tell(fine.sem)
            for g in range(2):
                steps.free(dve.tensor_scalar(kk[:, g, :], kr[:, g, :], c1("rwkv_k_k", g), None, ALU.mult))
            steps.join()
            steps(dve.tensor_tensor(tmp[:, :, :], kk[:, :, :], kk[:, :, :], ALU.mult))
            dve.wait_ge(low.sem, low.of(4))
            dve.wait_ge(fin2.sem, fin2.of(4))
            steps(dve.tensor_copy(Wend[:, :, :], rho[:, :, CH - 1:T1:CH]))
    low.close(4)
    fine.close(3)
    fin2.close(4)

    def head_sums(src):
        groups = [dict(places=2, mm=[(k.ps[:, 2 * g + h, 0:HALF1], c("head_ones"),
                                      src[:, g, h * HALF1:(h + 1) * HALF1], True, True) for h in range(2)])
                  for g in range(2)]
        return groups

    norm = sb("norm", [P, 2, T1])

    def take_norm(k, who, i, steps):
        return copy_out(k, who, halves(norm[:, i, :]), k.ps[:, 2 * i:2 * i + 2, 0:HALF1])
    products(k, head_sums(tmp), take_norm)
    with nc.Block() as block:
        @block.scalar
        def _(act):
            act.activation(norm[:, :, :], norm[:, :, :], ACT.Sqrt).then_inc(low.sem, 1)

        @block.vector
        def _(dve):
            steps = k.steps(dve, "v")
            for g in range(2):
                steps(dve.tensor_scalar(tmp[:, g, :], a[:, g, :], -1.0, c1("rwkv_k_a", g), ALU.add, ALU.mult))
                steps.free(dve.scalar_tensor_tensor(kr[:, g, :], tmp[:, g, :], 1.0, kr[:, g, :], ALU.add, ALU.mult))
            dve.wait_ge(low.sem, low.of(1))
            steps.join()
            steps(dve.tensor_scalar(norm[:, :, :], norm[:, :, :], 1e-12, None, ALU.max))
            steps(dve.reciprocal(norm[:, :, :], norm[:, :, :]))
            steps(dve.tensor_tensor(kk[:, :, :], kk[:, :, :], norm[:, :, :], ALU.mult))
            steps(dve.tensor_tensor(a[:, :, :], kk[:, :, :], a[:, :, :], ALU.mult))
            steps.free(dve.tensor_tensor(kap[:, :, :], kap[:, :, :], kk[:, :, :], ALU.mult))
            steps.free(dve.tensor_tensor(bet[:, :, :], kti[:, :, :], a[:, :, :], ALU.mult))
            steps.free(dve.tensor_tensor(bend[:, :, :], kend[:, :, :], a[:, :, :], ALU.mult))
            steps.join()
            steps.free(dve.tensor_tensor(kti[:, :, :], kti[:, :, :], kr, ALU.mult))
            steps.free(dve.tensor_tensor(kend[:, :, :], kend[:, :, :], kr, ALU.mult))
            steps.free(dve.tensor_tensor(rho[:, :, :], rho[:, :, :], r, ALU.mult))
            for g in range(2):
                steps.free(dve.scalar_tensor_tensor(tmp[:, g, :], r[:, g, :], c1("rwkv_r_k", g), kr[:, g, :],
                                                    ALU.mult, ALU.mult))
            steps.free(dve.tensor_copy(vv[:, :, :], v))
            steps.join()
    low.close(1)

    def take_bonus(k, who, i, steps):
        return copy_out(k, who, halves(bonusT[:, i, :]), k.ps[:, 2 * i:2 * i + 2, 0:HALF1])
    products(k, head_sums(tmp), take_bonus)
    with nc.Block() as block:
        @block.vector
        def _(dve):
            steps = k.steps(dve, "v")
            steps(dve.tensor_tensor(bonusT[:, :, :], bonusT[:, :, :], vv[:, :, :], ALU.mult))


def chunk_group(k, sb, tiles, X, OT, kap, bet, kti, rho, bend, kend, vv, Wend):
    nc, c = k.nc, k.c
    ps = k.ps
    n_t = len(tiles)
    ns = [P if t < NTL else N_META for t in tiles]
    H = RW_HEADS
    mats = k.h1[:, :, :].rearrange("p a c -> p (a c)")[:, 0:n_t * 5 * H * P].rearrange(
        "p (n a h t) -> p n a h t", n=n_t, a=5, h=H)
    pw = sb("pw", [P, n_t, 3, H, P])
    tok = sb("tok", [P, n_t, 4, RW])
    tk = sb("tk", [P, n_t, 3, RW])
    spare = k.stream.ring[:, RING // 2:RING, :].rearrange("p s c -> p (s c)")
    n_ex, n_a = 3 * CPT * RW, n_t * 2 * CPT * HD
    ex = spare[:, 0:n_ex].rearrange("p (a c h) -> p a c h", a=3, c=CPT)
    aT = spare[:, n_ex:n_ex + n_a].rearrange("p (n g c j) -> p n g c j", n=n_t, g=2, c=CPT)
    gT = sb("gT", [P, n_t, 2, P])
    hT_ = sb("hT_", [P, n_t, 2, P])
    fT = sb("fT", [P, n_t, 2, CPT, HD])
    xs = sb("xs", [P, 2, n_t * CPT + 1, HD])
    made, moved = k.sig["made"], k.sig["moved"]

    def ts(t):
        return slice(P * t, P * t + (P if t < NTL else N_META))

    def steps_of(it):
        t, n = tiles[it], ns[it]
        m, q, tkn, w = mats[:, it], pw[:, it], tok[:, it], tk[:, it]
        b0 = 4 * (it % 2)
        nc_ = n // CH

        def hp(x, g, p):
            return x[HD * p:HD * p + HD, g, ts(t)]

        out = []

        def pe1(pe):
            for a, src in enumerate((kap, bend, kend, vv)):
                for g in range(2):
                    mm = pe.transpose(ps[0:n, b0 + a // 2, (a % 2) * RW + g * P:(a % 2) * RW + g * P + P], src[:, g, ts(t)],
                                      c("ident"))
            return mm

        def dv1(dve):
            return [dve.tensor_copy(tkn[0:n, 0:2, :], ps[0:n, b0, :].rearrange("p (a c) -> p a c", a=2)),
                    dve.tensor_copy(tkn[0:n, 2:4, :], ps[0:n, b0 + 1, :].rearrange("p (a c) -> p a c", a=2))]
        out.append((pe1, dv1))

        def grams(kinds):
            def pe2(pe):
                for a, (l, r) in enumerate(kinds):
                    for p in range(2):
                        for g in range(2):
                            col = ((a % 2) * 2 + g) * P
                            mm = pe.matmul(ps[0:n, b0 + 2 * (a // 2) + p, col:col + n], hp(l, g, p), hp(r, g, p), start=True, stop=True,
                                           skip_group_check=True)
                return mm
            return pe2

        def masked(mask, dsts, bank):
            def f(dve):
                res = []
                for a, dst in enumerate(dsts):
                    for p in range(2):
                        src = ps[0:n, b0 + bank + p, a * 256:(a + 1) * 256].rearrange("p (g t) -> p g t", g=2)[:, :, 0:n]
                        mk = c(mask)[0:n, a * P:a * P + n].unsqueeze(1).to_broadcast([n, 2, n])
                        res.append(dve.tensor_tensor(m[0:n, dst, 2 * p:2 * p + 2, 0:n], src, mk, ALU.mult))
                return res
            return f
        out.append((grams(((bet, kap), (kti, kap), (bet, rho), (kti, rho))),
                    lambda dve: masked("mask_u", (0, 2), 0)(dve) + masked("mask_o", (3, 4), 2)(dve)))
        out.append((grams(((kap, bet),)), masked("mask_l", (1,), 0)))

        def mm4(dst_bank, lhs, rhs):
            def f(pe):
                for h in range(H):
                    mm = pe.matmul(ps[0:n, b0 + dst_bank, h * P:h * P + n], lhs[0:n, h, 0:n], rhs[0:n, h, 0:n], start=True, stop=True,
                                   skip_group_check=True)
                return mm
            return f

        def both(*fs):
            def f(e):
                for x in fs:
                    r = x(e)
                return r
            return f

        def bank4(bank):
            return ps[0:n, b0 + bank, :].rearrange("p (h t) -> p h t", h=H)[:, :, 0:n]
        U, UT, U2, U2T, R = m[:, 0], m[:, 1], q[:, 0], q[:, 1], q[:, 2]
        eye = c("ident")[0:n, 0:n].unsqueeze(1).to_broadcast([n, H, n])
        v = lambda x: x[0:n, :, 0:n]
        out.append((both(mm4(0, UT, U), mm4(1, U, UT)),
                    lambda dve: [dve.tensor_copy(v(U2), bank4(0)), dve.tensor_copy(v(U2T), bank4(1)),
                                 dve.tensor_tensor(v(R), v(U), eye, ALU.add)]))
        out.append((both(mm4(0, U2T, R), mm4(1, U2T, U2), mm4(2, U2, U2T)),
                    lambda dve: [dve.tensor_tensor(v(R), bank4(0), v(R), ALU.add), dve.tensor_copy(v(U), bank4(1)),
                                 dve.tensor_copy(v(UT), bank4(2))]))
        out.append((both(mm4(0, UT, R), mm4(1, U, UT)),
                    lambda dve: [dve.tensor_tensor(v(R), bank4(0), v(R), ALU.add), dve.tensor_copy(v(U2T), bank4(1))]))

        def head_cols(p, g):
            return slice(g * P + p * HD, g * P + p * HD + HD)

        def by_head(bank, col, lhs, rhs, a):
            def f(pe):
                for p in range(2):
                    for g in range(2):
                        s = head_cols(p, g)
                        mm = pe.matmul(ps[0:n, b0 + bank, col + s.start:col + s.stop], lhs[0:n, 2 * p + g, 0:n], rhs[0:n, a, s],
                                       start=True, stop=True, skip_group_check=True)
                return mm
            return f
        out.append((both(mm4(0, U2T, R), by_head(1, 0, m[:, 2], tkn, 3)),
                    lambda dve: [dve.tensor_tensor(v(R), bank4(0), v(R), ALU.add),
                                 dve.tensor_copy(w[0:n, 2, :], ps[0:n, b0 + 1, 0:RW])]))
        out.append((both(by_head(0, 0, R, tkn, 0), by_head(0, RW, R, w, 2)),
                    lambda dve: [dve.tensor_copy(w[0:n, 0:2, :], ps[0:n, b0, :].rearrange("p (a c) -> p a c", a=2))]))

        def pe9(pe):
            for g in range(2):
                for p in range(2):
                    s, h = head_cols(p, g), 2 * p + g
                    o = ps[HD * p:HD * p + HD, b0, g * P:g * P + n]
                    pe.matmul(o, w[0:n, 0, s], m[0:n, 3, h, 0:n], start=True, stop=True, skip_group_check=True)
                    o = ps[HD * p:HD * p + HD, b0 + 1, g * P:g * P + n]
                    pe.matmul(o, tkn[0:n, 3, s], m[0:n, 4, h, 0:n], start=True, stop=False, skip_group_check=True)
                    mm = pe.matmul(o, w[0:n, 1, s], m[0:n, 3, h, 0:n], start=False, stop=True, skip_group_check=True)
            return mm

        def dv9(dve):
            x = lambda bank: ps[:, b0 + bank, 0:2 * P].rearrange("p (g t) -> p g t", g=2)[:, :, 0:n]
            res = [dve.tensor_tensor(gT[:, it, :, 0:n], x(0), rho[:, :, ts(t)], ALU.add),
                   dve.tensor_copy(hT_[:, it, :, 0:n], x(1))]
            for a, src in enumerate((tkn[0:n, 1, :], tkn[0:n, 3, :], w[0:n, 1, :])):
                for ch in range(nc_):
                    col = c("chunk_of")[0:n, ch:ch + 1]
                    if a < 2:
                        res.append(dve.tensor_scalar(ex[0:n, a, ch, :], src, col, None, ALU.mult))
                    else:
                        res.append(dve.tensor_scalar(ex[0:n, a, ch, :], src, col, -1.0, ALU.mult, ALU.mult))
            return res
        out.append((pe9, dv9))

        def pe10(pe):
            for g in range(2):
                for p in range(2):
                    s = head_cols(p, g)
                    o = ps[HD * p:HD * p + HD, b0 + g, 0:nc_ * HD]
                    pe.matmul(o, w[0:n, 0, s], ex[0:n, 0, 0:nc_, s], start=True, stop=True, skip_group_check=True)
                    o = ps[HD * p:HD * p + HD, b0 + 2 + g, 0:nc_ * HD]
                    pe.matmul(o, tkn[0:n, 2, s], ex[0:n, 1, 0:nc_, s], start=True, stop=False, skip_group_check=True)
                    mm = pe.matmul(o, tkn[0:n, 1, s], ex[0:n, 2, 0:nc_, s], start=False, stop=True, skip_group_check=True)
            return mm

        def dv10(dve):
            steps = k.v_steps
            res = []
            for g in range(2):
                d_ = Wend[:, g, CPT * t:CPT * t + nc_].unsqueeze(2).to_broadcast([P, nc_, HD])
                e_ = c("eye_head").unsqueeze(1).to_broadcast([P, nc_, HD])
                steps(dve.tensor_tensor(aT[:, it, g, 0:nc_, :], d_, e_, ALU.mult))
                x = lambda bank: ps[:, b0 + bank, 0:nc_ * HD].rearrange("p (c j) -> p c j", j=HD)
                res.append(dve.tensor_tensor(aT[:, it, g, 0:nc_, :], aT[:, it, g, 0:nc_, :], x(g), ALU.subtract))
                steps.free(res.pop())
                res.append(dve.tensor_copy(fT[:, it, g, 0:nc_, :], x(2 + g)))
                steps.free(res.pop())
            return res
        out.append((pe10, dv10))
        return out

    lists = [steps_of(it) for it in range(n_t)]
    n_steps = len(lists[0])
    order = [(s, it) for s in range(n_steps - 2) for it in range(n_t)]
    order += [(s, it) for it in range(n_t) for s in (n_steps - 2, n_steps - 1)]
    at = {x: i + 1 for i, x in enumerate(order)}
    with nc.Block() as block:
        @block.tensor
        def _(pe):
            for s, it in order:
                if s >= 1:
                    pe.wait_ge(moved.sem, moved.of(at[s - 1, it]))
                lists[it][s][0](pe).then_inc(made.sem, 1)

        @block.vector
        def _(dve):
            steps = k.steps(dve, "v")
            k.v_steps = steps
            for s, it in order:
                dve.wait_ge(made.sem, made.of(at[s, it]))
                for x in lists[it][s][1](dve):
                    steps.free(x)
                steps.tell(moved.sem)
    made.close(n_t * n_steps)
    moved.close(n_t * n_steps)

    chunks = [(it, ch) for it in range(n_t) for ch in range(ns[it] // CH)]
    with nc.Block() as block:
        @block.tensor
        def _(pe):
            for i, (it, ch) in enumerate(chunks):
                pe.wait_ge(moved.sem, moved.of(i + 1))
                for p in range(2):
                    for g in range(2):
                        b = slice(HD * p, HD * p + HD)
                        mm = pe.matmul(ps[b, 2 * (i % 2) + p, g * HD:(g + 1) * HD], aT[b, it, g, ch, :], xs[b, g, i, :],
                                       start=True, stop=True, skip_group_check=True)
                mm.then_inc(made.sem, 1)

        @block.vector
        def _(dve):
            steps = k.steps(dve, "v")
            dve.tensor_copy(xs[:, :, 0, :], X[:, :, :]).then_inc(moved.sem, 1)
            for i, (it, ch) in enumerate(chunks):
                dve.wait_ge(made.sem, made.of(i + 1))
                for p in range(2):
                    b = slice(HD * p, HD * p + HD)
                    x = dve.tensor_tensor(xs[b, :, i + 1, :],
                                          ps[b, 2 * (i % 2) + p, 0:2 * HD].rearrange("p (g j) -> p g j", g=2),
                                          fT[b, it, :, ch, :], ALU.add)
                    steps.free(x)
                steps.tell(moved.sem)
            dve.wait_ge(moved.sem, moved.of(len(chunks) + 1))
            steps(dve.tensor_copy(X[:, :, :], xs[:, :, len(chunks), :]))
    made.close(len(chunks))
    moved.close(len(chunks) + 1)

    with nc.Block() as block:
        @block.tensor
        def _(pe):
            for i, (it, ch) in enumerate(chunks):
                for p in range(2):
                    for g in range(2):
                        b = slice(HD * p, HD * p + HD)
                        mm = pe.matmul(ps[b, 2 * it + p, g * P + ch * CH:g * P + ch * CH + CH], xs[b, g, i, :],
                                       gT[b, it, g, ch * CH:ch * CH + CH], start=True, stop=True, skip_group_check=True)
            mm.then_inc(made.sem, 1)

        @block.vector
        def _(dve):
            steps = k.steps(dve, "v")
            dve.wait_ge(made.sem, made.of(1))
            for it in range(n_t):
                for p in range(2):
                    b = slice(HD * p, HD * p + HD)
                    n = ns[it]
                    x = ps[b, 2 * it + p, 0:2 * P].rearrange("p (g t) -> p g t", g=2)[:, :, 0:n]
                    steps.free(dve.tensor_tensor(OT[b, :, ts(tiles[it])], x, hT_[b, it, :, 0:n], ALU.add))
            steps.join()
    made.close(1)


def group_norm(k, sb, OT, bonusT, G):
    nc, c, c1 = k.nc, k.c, k.c1
    sq = sb("sq", [P, 2, T1])
    low = k.sig["low"]

    def means(src):
        return [dict(places=2, mm=[(k.ps[:, 2 * g + h, 0:HALF1], c("head_ones"), src[:, g, h * HALF1:(h + 1) * HALF1],
                                    True, True) for h in range(2)]) for g in range(2)]

    def take(k, who, i, steps):
        return copy_out(k, who, halves(sq[:, i, :]), k.ps[:, 2 * i:2 * i + 2, 0:HALF1], 1.0 / HD)
    products(k, means(OT), take)
    with nc.Block() as block:
        @block.vector
        def _(dve):
            steps = k.steps(dve, "v")
            steps(dve.tensor_tensor(OT[:, :, :], OT[:, :, :], sq[:, :, :], ALU.subtract))
            steps(dve.tensor_tensor(sq[:, :, :], OT[:, :, :], OT[:, :, :], ALU.mult))
    products(k, means(sq), take)
    with nc.Block() as block:
        @block.vector
        def _(dve):
            steps = k.steps(dve, "v")
            dve.tensor_scalar(sq[:, :, :], sq[:, :, :], GN_EPS, None, ALU.add).then_inc(low.sem, 1)
            dve.wait_ge(low.sem, low.of(2))
            steps(dve.reciprocal(sq[:, :, :], sq[:, :, :]))
            steps(dve.tensor_tensor(OT[:, :, :], OT[:, :, :], sq[:, :, :], ALU.mult))
            for g in range(2):
                steps(dve.scalar_tensor_tensor(OT[:, g, :], OT[:, g, :], c1("rwkv_ln_w", g), bonusT[:, g, :],
                                               ALU.mult, ALU.add))
                steps(dve.scalar_tensor_tensor(OT[:, g, :], OT[:, g, :], c1("rwkv_ln_b", g), G[:, g, :],
                                               ALU.add, ALU.mult))

        @block.scalar
        def _(act):
            act.wait_ge(low.sem, low.of(1))
            act.activation(sq[:, :, :], sq[:, :, :], ACT.Sqrt).then_inc(low.sem, 1)
    low.close(2)


def recurrence(k, hT, mixT):
    nc, c1 = k.nc, k.c1
    low, fine = k.sig["low"], k.sig["fine"]
    PAD = 3
    with ExitStack() as ctx:
        sb = k.alloc(ctx)
        xa = sb("xa", [P, 2, T1 + PAD])
        ya = sb("ya", [P, 2, T1])
        u = sb("u", [P, 2, T1])
        rg = sb("rg", [P, 2, T1])
        ig = sb("ig", [P, 2, T1])
        w = sb("w", [P, 2, T1])
        sp_ = sb("sp_", [P, 4, 2])

        def take(who, i, src, steps):
            dst = xa[:, i, PAD:] if i < 2 else ya[:, i - 2, :]
            return copy_out(k, who, halves(dst), src)
        with nc.Block() as block:
            @block.vector
            def _(dve):
                steps = k.steps(dve, "v")
                steps(dve.memset(xa[:, :, 0:PAD], 0.0))
        project_channels(k, hT, column_tiles(k, 2), take)
        with nc.Block() as block:
            @block.vector
            def _(dve):
                steps = k.steps(dve, "v")
                for g in range(2):
                    for tap in range(4):
                        x = xa[:, g, tap:tap + T1]
                        cw = c1("lru_conv_w", 2 * tap + g)
                        if tap == 0:
                            steps(dve.tensor_scalar(u[:, g, :], x, cw, c1("lru_conv_b", g), ALU.mult, ALU.add))
                        else:
                            steps(dve.scalar_tensor_tensor(u[:, g, :], x, cw, u[:, g, :], ALU.mult, ALU.add))

            @block.scalar
            def _(act):
                steps = k.steps(act, "s")
                for g in range(2):
                    steps.free(act.activation(ya[:, g, :], ya[:, g, :], ACT.Gelu_apprx_tanh))
                steps(act.activation(sp_[:, 0, :], c1("lru_lambda", 0, 2), ACT.Exp, scale=-1.0))
                steps(act.activation(sp_[:, 1, :], sp_[:, 0, :], ACT.Identity, bias=k.one))
                steps(act.activation(sp_[:, 2, :], sp_[:, 1, :], ACT.Ln))
        with nc.Block() as block:
            @block.vector
            def _(dve):
                steps = k.steps(dve, "v")
                log1p_fix(dve, steps, sp_[:, 0, :], sp_[:, 1, :], sp_[:, 2, :], sp_[:, 3, :])
                steps(dve.tensor_scalar(sp_[:, 2, :], sp_[:, 2, :], 8.0, None, ALU.mult))
        groups = []
        for kind, name in enumerate(("gate_a", "gate_x")):
            for g in range(2):
                i = len(groups)
                groups.append(dict(places=4, mm=[(k.ps[:, 2 * i + h, 0:HALF1], k.c1m(name, 256)[:, g * P:(g + 1) * P],
                                                  u[:, g, h * HALF1:(h + 1) * HALF1], True, True) for h in range(2)]))

        def take2(k, who, i, steps):
            dst = (rg if i < 2 else ig)[:, i % 2, :]
            return copy_out(k, who, halves(dst), k.ps[:, 2 * i:2 * i + 2, 0:HALF1])
        products(k, groups, take2)
        with nc.Block() as block:
            @block.scalar
            def _(act):
                steps = k.steps(act, "s")
                for g in range(2):
                    steps.free(act.activation(rg[:, g, :], rg[:, g, :], ACT.Sigmoid, bias=c1("lru_gate_a_b", g)))
                    steps.free(act.activation(ig[:, g, :], ig[:, g, :], ACT.Sigmoid, bias=c1("lru_gate_x_b", g)))
                steps.tell(low.sem)
                act.wait_ge(fine.sem, fine.of(1))
                steps.free(act.activation(w[:, :, :], rg[:, :, :], ACT.Tanh))
                steps.tell(low.sem)
                steps(act.activation(rg[:, :, :], rg[:, :, :], ACT.Exp, scale=-1.0))
                act.wait_ge(fine.sem, fine.of(2))
                steps.free(act.activation(w[:, :, :], w[:, :, :], ACT.Sqrt))
                steps.tell(low.sem)

            @block.vector
            def _(dve):
                steps = k.steps(dve, "v")
                dve.wait_ge(low.sem, low.of(1))
                for g in range(2):
                    steps.free(dve.tensor_scalar(rg[:, g, :], rg[:, g, :], sp_[:, 2, g:g + 1], None, ALU.mult))
                steps.tell(fine.sem)
                steps(dve.tensor_tensor(u[:, :, :], ig[:, :, :], u[:, :, :], ALU.mult))
                dve.wait_ge(low.sem, low.of(2))
                steps(dve.tensor_scalar(ig[:, :, :], w[:, :, :], 1.0, None, ALU.add))
                steps(dve.reciprocal(ig[:, :, :], ig[:, :, :]))
                steps.free(dve.scalar_tensor_tensor(w[:, :, :], w[:, :, :], 2.0, ig[:, :, :], ALU.mult, ALU.mult))
                steps.tell(fine.sem)
                dve.wait_ge(low.sem, low.of(3))
                steps(dve.tensor_tensor(u[:, :, :], u[:, :, :], w[:, :, :], ALU.mult))
                for g in range(2):
                    steps(dve.tensor_tensor_scan(w[:, g, :], rg[:, g, :], u[:, g, :], 0.0, ALU.mult, ALU.add))
                steps(dve.tensor_tensor(mixT[:, 0:2, :], w[:, :, :], ya[:, :, :], ALU.mult))
        low.close(3)
        fine.close(2)


def log1p_fix(dve, steps, z, w, lnw, tmp):
    steps(dve.tensor_scalar(tmp, w, -1.0, None, ALU.add))
    steps(dve.tensor_tensor(tmp, z, tmp, ALU.subtract))
    steps(dve.reciprocal(w, w))
    steps(dve.tensor_tensor(tmp, tmp, w, ALU.mult))
    steps(dve.tensor_tensor(lnw, lnw, tmp, ALU.add))


def forgetting(k, hT, mixT):
    nc, c1, c = k.nc, k.c1, k.c
    with ExitStack() as ctx:
        sb = k.alloc(ctx)
        qT = sb("qT", [P, 4, T1])
        kT = sb("kT", [P, 4, T1])
        v = sb("v", [P, 5, FOX_W])
        fl = sb("fl", [FOX_HEADS, 5, T1])

        def take(who, i, src, steps):
            if i < 4:
                return copy_out(k, who, halves(qT[:, i, :]), src, HD ** -0.5)
            if i < 8:
                return copy_out(k, who, halves(kT[:, i - 4, :]), src)
            return copy_out(k, who, halves(fl[:, 0, :]), src)
        tiles = column_tiles(k, 4)
        wf = k.c1m("w_f", 8 * FOX_HEADS).rearrange("p (k h) -> p k h", k=KD)
        tiles.append((lambda c_: wf[:, c_, :], FOX_HEADS, [], []))
        project_channels(k, hT, tiles, take)
        groups, where = [], []
        for half in range(2):
            n = k.stream.take()
            s = k.stream.slot(n).rearrange("p (k c) -> p k c", k=KD)
            for t in range(5):
                m = P if t < NTL else N_META
                i = len(groups)
                groups.append(dict(places=8, needs=[n] if t == 0 else [], last=[n] if t == 4 else [],
                                   mm=[(k.ps[0:m, i % 8, 0:256], hT[:, c_, P * t:P * t + m], s[:, c_, :], c_ == 0, c_ == KD - 1)
                                       for c_ in range(KD)]))
                where.append((t, half, m))

        def take_v(k, who, i, steps):
            t, half, m = where[i]
            return copy_out(k, who, v[0:m, t, half * 256:half * 256 + 256], k.ps[0:m, i % 8, 0:256])
        products(k, groups, take_v)
        low, fine = k.sig["low"], k.sig["fine"]
        with nc.Block() as block:
            @block.vector
            def _(dve):
                steps = k.steps(dve, "v")
                x = fl[:, 0, :]
                steps(dve.tensor_scalar(x, x, c1("fox_f_bias", 0)[0:FOX_HEADS], None, ALU.add))
                steps(dve.tensor_scalar(fl[:, 1, :], x, -1.0, None, ALU.mult))
                steps.free(dve.tensor_tensor(fl[:, 1, :], fl[:, 1, :], x, ALU.min))
                steps.tell(low.sem)
                steps.free(dve.tensor_scalar(x, x, 0.0, None, ALU.min))
                dve.wait_ge(fine.sem, fine.of(1))
                log1p_fix(dve, steps, fl[:, 1, :], fl[:, 2, :], fl[:, 3, :], fl[:, 4, :])
                steps(dve.tensor_tensor(x, fl[:, 3, :], x, ALU.subtract))
                steps(dve.memset(fl[:, 2, :], 1.0))
                steps(dve.tensor_tensor_scan(fl[:, 1, :], fl[:, 2, :], x, 0.0, ALU.mult, ALU.add))

            @block.scalar
            def _(act):
                steps = k.steps(act, "s")
                act.wait_ge(low.sem, low.of(1))
                steps(act.activation(fl[:, 1, :], fl[:, 1, :], ACT.Exp))
                steps(act.activation(fl[:, 2, :], fl[:, 1, :], ACT.Identity, bias=k.one[0:FOX_HEADS]))
                steps.free(act.activation(fl[:, 3, :], fl[:, 2, :], ACT.Ln))
                steps.tell(fine.sem)

        low.close(1)
        fine.close(1)
        units = []
        for t in range(5):
            n = P if t < NTL else N_META
            width = P * t + n
            for h in range(FOX_HEADS):
                b = slice(HD * (h % 2), HD * (h % 2) + HD)
                q = qT[b, h // 2, P * t:P * t + n]
                sel = c("ident")[0:FOX_HEADS, h:h + 1].to_broadcast([FOX_HEADS, n])
                units.append(dict(q=q, base=b.start, width=width, sink=None,
                                  scores=[(0, [(q, kT[b, h // 2, 0:width]), (sel, fl[:, 1, 0:width])])],
                                  adds=[(P * t, c("causal")[0:n, 0:n])],
                                  values=[(v[0:(P if s < NTL else N_META), s, HD * h:HD * h + HD],
                                           P if s < NTL else N_META, P * s) for s in range(t + 1)],
                                  out=mixT[b, 2 + h // 2, P * t:P * t + n]))
        attention(k, units)


def mix_out(k, sb, mixT, OT):
    nc = k.nc
    y = k.h1
    lhs = lambda c_, at, n: (mixT[:, c_, at:at + n] if c_ < 6 else OT[:, c_ - 6, at:at + n])
    tiles = [(N_META + P * j, P, j) for j in range(NTL)] + [(0, N_META, NTL)]
    groups, where = [], []
    for half in range(2):
        a, b = k.stream.take(), k.stream.take()
        s = [k.stream.slot(x).rearrange("p (k c) -> p k c", k=4) for x in (a, b)]
        for at, n, j in tiles:
            i = len(groups)
            groups.append(dict(places=8, needs=[a, b] if j == 0 else [], last=[a, b] if j == NTL else [],
                               mm=[(k.ps[0:n, i % 8, :], lhs(c_, at, n), s[c_ // 4][:, c_ % 4, :], c_ == 0, c_ == KD - 1)
                                   for c_ in range(KD)]))
            where.append((j, n, half))
    mo = sb("mo", [P, 5, D])

    def take(k, who, i, steps):
        j, n, half = where[i]
        return copy_out(k, who, mo[0:n, j, half * BANK:(half + 1) * BANK], k.ps[0:n, i % 8, :])
    products(k, groups, take)
    row = sb("row", [P, D])
    load(k, [(row[:, :], k.dram["rows1"][0].partition_broadcast(P)), (y[:, 0:NTL, :], k.dram["x"]),
             (y[0:N_META, NTL, :], k.dram["meta"])])
    rms_scale(k, [(mo[0:n, j, :], mo[0:n, j, :], n, row[0:n, :], y[0:n, j, :]) for _, n, j in tiles])


def feed_forward(k):
    nc, c1 = k.nc, k.c1
    y = k.h1
    with ExitStack() as ctx:
        sb = k.alloc(ctx)
        actT = sb("actT", [P, FT, SEQ])
        with ExitStack() as inner:
            sbi = k.alloc(inner)
            hT = sbi("hT2", [P, KD, T1])
            with ExitStack() as i2:
                un = k.alloc(i2)("un", [P, 5, D])
                rms_scale(k, [(y[0:N_META, NTL, :], un[0:N_META, NTL, :], N_META, None, None)] +
                          [(y[:, j, :], un[:, j, :], P, None, None) for j in range(NTL)])
                to_channels(k, token_tiles(un, un[0:N_META, NTL, :]), hT, lambda w, c: c1("norm_ffn_pre", c))
            feed_up(k, sbi, hT, actT)
        with nc.Block() as block:
            ready = k.sig["product"]

            @block.tensor
            def _(pe):
                for cc in range(N_DOWN):
                    n = k.stream.take()
                    k.stream.wait(pe, n)
                    s = k.stream.slot(n).rearrange("p (k c) -> p k c", k=2)
                    for kk in range(2):
                        f = 2 * cc + kk
                        for j in range(NTL):
                            for half in range(2):
                                mm = pe.matmul(k.ps[:, 2 * j + half, :], actT[:, f, P * j:P * j + P],
                                               s[:, kk, half * BANK:(half + 1) * BANK], start=f == 0, stop=f == FT - 1,
                                               skip_group_check=True)
                    mm.then_inc(ready.sem, 1)
                    k.stream.freed(n, ready.sem, ready.of(cc + 1))

            @block.sync
            def _(sp):
                k.stream.issue(sp)
        ready.close(N_DOWN)
    with ExitStack() as ctx:
        sb = k.alloc(ctx)
        mo = sb("mo2", [P, NTL, D])
        row = sb("row2", [P, D])
        with nc.Block() as block:
            @block.vector
            def _(dve):
                steps = k.steps(dve, "v")
                for j in range(2):
                    steps.free(dve.tensor_copy(mo[:, j, :], k.psf[:, D * j:D * j + D]))
                steps.join()

            @block.scalar
            def _(act):
                steps = k.steps(act, "s")
                for j in range(2, NTL):
                    steps.free(act.copy(mo[:, j, :], k.psf[:, D * j:D * j + D]))
                steps.join()
        load(k, [(row[:, :], k.dram["rows1"][1].partition_broadcast(P))])
        rms_scale(k, [(mo[:, j, :], mo[:, j, :], P, row[:, :], y[:, j, :]) for j in range(NTL)])


def feed_up(k, sb, hT, actT):
    nc, c1 = k.nc, k.c1
    raw = sb("raw", [P, 2, 2, T1])
    conv = sb("conv", [P, 2, 2, SEQ])
    ready, copied, conved, gelued, mixed = (k.sig[x] for x in ("product", "taken_s", "fine", "low", "taken_v"))
    FIRST = N_META - 2
    with nc.Block() as block:
        @block.tensor
        def _(pe):
            for j in range(FT):
                n = k.stream.take()
                k.stream.wait(pe, n)
                if j >= 2:
                    pe.wait_ge(copied.sem, copied.of(j - 1))
                for gv in range(2):
                    w = column_chunk(k, n, gv)
                    for c_ in range(KD):
                        for h in range(2):
                            mm = pe.matmul(k.ps[:, 4 * (j % 2) + 2 * gv + h, 0:HALF1], w(c_),
                                           hT[:, c_, h * HALF1:(h + 1) * HALF1], start=c_ == 0, stop=c_ == KD - 1,
                                           skip_group_check=True)
                mm.then_inc(ready.sem, 1)
                k.stream.freed(n, ready.sem, ready.of(j + 1))

        @block.scalar
        def _(act):
            steps = k.steps(act, "s")

            def gelu(j):
                act.wait_ge(conved.sem, conved.of(j + 1))
                g = conv[:, j % 2, 0, :]
                act.activation(g, g, ACT.Gelu_apprx_tanh).then_inc(gelued.sem, 1)
            for j in range(FT):
                act.wait_ge(ready.sem, ready.of(j + 1))
                if j >= 2:
                    act.wait_ge(conved.sem, conved.of(j - 1))
                for gv in range(2):
                    b = 4 * (j % 2) + 2 * gv
                    steps.free(act.copy(halves(raw[:, j % 2, gv, :]), k.ps[:, b:b + 2, 0:HALF1]))
                steps.tell(copied.sem)
                if j >= 1:
                    gelu(j - 1)
            gelu(FT - 1)
            act.wait_ge(gelued.sem, gelued.of(FT))

        @block.vector
        def _(dve):
            steps = k.steps(dve, "v")

            def mix(j):
                dve.wait_ge(gelued.sem, gelued.of(j + 1))
                dve.tensor_tensor(actT[:, j, :], conv[:, j % 2, 0, :], conv[:, j % 2, 1, :],
                                  ALU.mult).then_inc(mixed.sem, 1)
            for j in range(FT):
                dve.wait_ge(copied.sem, copied.of(j + 1))
                if j >= 2:
                    dve.wait_ge(mixed.sem, mixed.of(j - 1))
                for tap in range(3):
                    for gv in range(2):
                        x = raw[:, j % 2, gv, FIRST + tap:FIRST + tap + SEQ]
                        y = conv[:, j % 2, gv, :]
                        cw = c1("ffn_conv", tap * 2 * FT + gv * FT + j)
                        if tap == 0:
                            steps.free(dve.tensor_scalar(y, x, cw, None, ALU.mult))
                        else:
                            steps.free(dve.scalar_tensor_tensor(y, x, cw, y, ALU.mult, ALU.add))
                    steps.join()
                dve.sem_inc(conved.sem, 1)
                if j >= 1:
                    mix(j - 1)
            mix(FT - 1)
            dve.wait_ge(mixed.sem, mixed.of(FT))

        @block.sync
        def _(sp):
            k.stream.issue(sp)
    for s in (ready, copied, conved, gelued, mixed):
        s.close(FT)


def second_block(k):
    nc = k.nc
    x = k.h1
    with ExitStack() as ctx:
        sb = k.alloc(ctx)
        const2 = sb("const2", [P, CONSTS[2][0].shape[1]])
        cols2 = sb("cols2", [P, LAYERS, NP2])
        cond = sb("cond", [P, KD, 2])
        mod = sb("mod", [P, 6 * KD, 2])
        at = {n: (const2, v) for n, v in CONSTS[2][1].items()}
        first = k.c
        k.c = lambda name: (at[name][0][:, at[name][1][0]:at[name][1][0] + at[name][1][1]] if name in at
                            else first(name))
        load(k, [(const2[:, :], k.dram["const2"]), (cond[:, :, :], k.dram["cond"]),
                 (cols2[:, :, :], k.dram["cols2"].rearrange("l p c -> p l c")), (x[:, NTL:NT2, :], k.dram["ctx"])])
        with nc.Block() as block:
            @block.scalar
            def _(act):
                steps = k.steps(act, "s")
                steps(act.activation(cond[:, :, :], cond[:, :, :], ACT.Silu))
        for l in range(LAYERS):
            k.c2 = lambda name, i, n=1, l=l: cols2[:, l, AT2[name] + i:AT2[name] + i + n]
            adaln(k, l, cond, mod)
            layer(k, l, x, mod)


def adaln(k, l, cond, mod):
    ready = k.sig["product"]
    with k.nc.Block() as block:
        @block.tensor
        def _(pe):
            for i in range(N_MOD):
                n = k.stream.take()
                k.stream.wait(pe, n)
                for j in range(2):
                    w = column_chunk(k, n, j)
                    col = 2 * (2 * i + j)
                    for c_ in range(KD):
                        mm = pe.matmul(k.ps[:, 0, col:col + 2], w(c_), cond[:, c_, :], start=c_ == 0, stop=c_ == KD - 1,
                                       skip_group_check=True)
                mm.then_inc(ready.sem, 1)
                k.stream.freed(n, ready.sem, ready.of(i + 1))

        @block.vector
        def _(dve):
            steps = k.steps(dve, "v")
            dve.wait_ge(ready.sem, ready.of(N_MOD))
            steps(dve.tensor_tensor(mod[:, :, :], k.ps[:, 0, 0:12 * KD].rearrange("p (c w) -> p c w", w=2),
                                    k.c2("b_mod", 0, 6 * KD).unsqueeze(2).to_broadcast([P, 6 * KD, 2]), ALU.add))
            for s in (1, 4):
                steps.free(dve.tensor_scalar(mod[:, s * KD:(s + 1) * KD, :], mod[:, s * KD:(s + 1) * KD, :], 1.0,
                                             None, ALU.add))
            steps.join()

        @block.sync
        def _(sp):
            k.stream.issue(sp)
    ready.close(N_MOD)


def layer_norm(k, jobs):
    nc = k.nc
    meant, rooted = k.sig["meant"], k.sig["rooted"]
    width = jobs[0][0].shape[1]
    nb = (width + BANK - 1) // BANK
    with ExitStack() as ctx:
        sb = k.alloc(ctx)
        stats = sb("stats", [P, NT2, nb, 6])
        mv = sb("mv", [P, NT2, 2])
        rstd = sb("rstd", [P, NT2])
        with nc.Block() as block:
            @block.vector
            def _(dve):
                steps = k.steps(dve, "v")
                for i, (x, out, gain, bias) in enumerate(jobs):
                    for b in range(nb):
                        steps.free(dve.bn_stats(stats[:, i, b, :], x[:, b * BANK:min(width, (b + 1) * BANK)]))
                    steps.join()
                    steps(dve.bn_aggr(mv[:, i, :], stats[:, i, :, :]))
                    dve.tensor_scalar(rstd[:, i:i + 1], mv[:, i, 1:2], LN_EPS, None, ALU.add).then_inc(meant.sem, 1)
                for i, (x, out, gain, bias) in enumerate(jobs):
                    dve.wait_ge(rooted.sem, rooted.of(i + 1))
                    steps(dve.reciprocal(rstd[:, i:i + 1], rstd[:, i:i + 1]))
                    steps(dve.tensor_scalar(out, x, mv[:, i, 0:1], rstd[:, i:i + 1], ALU.subtract, ALU.mult))
                    if gain is not None:
                        steps(dve.tensor_tensor(out, out, gain, ALU.mult))
                        steps(dve.tensor_tensor(out, out, bias, ALU.add))

            @block.scalar
            def _(act):
                for i in range(len(jobs)):
                    act.wait_ge(meant.sem, meant.of(i + 1))
                    act.activation(rstd[:, i:i + 1], rstd[:, i:i + 1], ACT.Sqrt).then_inc(rooted.sem, 1)

            @block.sync
            def _(sp):
                k.stream.issue(sp)
    meant.close(len(jobs))
    rooted.close(len(jobs))


def modulated(k, sb, u, uT, mod, base):
    to_channels(k, [(u[:, t, :], P, P * t, int(t >= NTL)) for t in range(NT2 if u.shape[1] == NT2 else NTL)], uT,
                lambda w, c_: mod[:, (base + 1) * KD + c_, w:w + 1], lambda w, c_: mod[:, base * KD + c_, w:w + 1])


def layer(k, l, x, mod):
    nc, c = k.nc, k.c
    last = l == LAYERS - 1
    nq = SEQ if last else T2
    ntq = nq // P
    with ExitStack() as ctx:
        sb = k.alloc(ctx)
        mixT = sb("mixT2", [P, KD, T2])
        with ExitStack() as inner:
            sbi = k.alloc(inner)
            qa = sbi("qa", [P, 4, T2])
            ka = sbi("ka", [P, T2])
            qb = sbi("qb", [P, 2, T2])
            kb = sbi("kb", [P, 2, T2])
            va = sbi("va", [P, NT2, 2 * HD])
            vb = sbi("vb", [P, NT2, 4 * HD])
            with ExitStack() as scope:
                cin = k.alloc(scope)("cin", [P, 2, 2, T2])
                with ExitStack() as i2:
                    u = k.alloc(i2)("u", [P, NT2, D])
                    layer_norm(k, [(x[:, t, :], u[:, t, :], None, None) for t in range(NT2)])
                    modulated(k, sbi, u, mixT, mod, 0)
                project2(k, mixT, nq, qa, ka, qb, kb, va, vb, cin)
                conformer(k, cin, mixT, nq)
            rotate(k, [(qa, i) for i in range(4)] + [(ka, None)])
            with ExitStack() as i2:
                mixers(k, k.alloc(i2), l, ntq, qa, ka, qb, kb, va, vb, mixT)
        with ExitStack() as inner:
            sbi = k.alloc(inner)
            o = sbi("o", [P, NT2, D])
            project_out(k, mixT, o, ntq)
            residual(k, sbi, l, 0, x, o, mod, ntq)
    with ExitStack() as ctx:
        sb = k.alloc(ctx)
        moe = sb("moe", [P, NT2, D])
        experts(k, sb, l, x, mod, ntq, moe)
        residual(k, sb, l, 1, x, moe, mod, ntq)


def project2(k, uT, nq, qa, ka, qb, kb, va, vb, cin):
    groups, where = [], []

    def channels(n, j, dst, tokens, scale, needs, last):
        w = column_chunk(k, n, j)
        half = tokens // 2
        i = len(groups)
        groups.append(dict(places=4, needs=needs, last=last,
                           mm=[(k.ps[:, 2 * (i % 4) + h, 0:half], w(c_), uT[:, c_, h * half:(h + 1) * half], c_ == 0,
                                c_ == KD - 1) for c_ in range(KD) for h in range(2)]))
        where.append((dst, 0, half, scale))

    def tokens_(n, lo, width, dst, needs, last):
        s = k.stream.slot(n).rearrange("p (k c) -> p k c", k=KD)
        for t in range(NT2):
            i = len(groups)
            groups.append(dict(places=4, needs=needs if t == 0 else [], last=last if t == NT2 - 1 else [],
                               mm=[(k.ps[:, 2 * (i % 4), 0:width], uT[:, c_, P * t:P * t + P], s[:, c_, lo:lo + width],
                                    c_ == 0, c_ == KD - 1) for c_ in range(KD)]))
            where.append((dst[:, t, :], 1, width, None))

    for i in range(2):
        n = k.stream.take()
        channels(n, 0, qa[:, 2 * i, :], nq, HD ** -0.5, [n], [])
        channels(n, 1, qa[:, 2 * i + 1, :], nq, HD ** -0.5, [], [n])
    n = k.stream.take()
    channels(n, 0, ka[:, :], T2, None, [n], [])
    tokens_(n, P, 2 * HD, va, [], [n])
    n = k.stream.take()
    channels(n, 0, qb[:, 0, :], nq, HD ** -0.5, [n], [])
    channels(n, 1, qb[:, 1, :], nq, HD ** -0.5, [], [n])
    n = k.stream.take()
    channels(n, 0, kb[:, 0, :], T2, None, [n], [])
    channels(n, 1, kb[:, 1, :], T2, None, [], [n])
    n = k.stream.take()
    tokens_(n, 0, 4 * HD, vb, [n], [n])
    for i in range(2):
        n = k.stream.take()
        channels(n, 0, cin[:, i, 0, :], nq, None, [n], [])
        channels(n, 1, cin[:, i, 1, :], nq, None, [], [n])

    def take(k, who, i, steps):
        dst, kind, width, scale = where[i]
        b = 2 * (i % 4)
        if kind:
            return copy_out(k, who, dst, k.ps[:, b, 0:width])
        return copy_out(k, who, dst[:, 0:2 * width].rearrange("p (h t) -> p h t", h=2), k.ps[:, b:b + 2, 0:width], scale)
    products(k, groups, take)


def rotate(k, tiles):
    nc, c = k.nc, k.c
    made, moved = k.sig["made"], k.sig["moved"]

    def lat(i):
        t, j = tiles[i]
        return t[:, j, 0:SEQ] if j is not None else t[:, 0:SEQ]
    with ExitStack() as ctx:
        tmp = k.alloc(ctx)("rtmp", [P, SEQ])
        with nc.Block() as block:
            @block.tensor
            def _(pe):
                for i in range(len(tiles)):
                    pe.matmul(k.ps[:, i, :], c("rot"), lat(i), start=True, stop=True).then_inc(made.sem, 1)

            @block.vector
            def _(dve):
                steps = k.steps(dve, "v")
                for i in range(len(tiles)):
                    dve.wait_ge(made.sem, made.of(i + 1))
                    steps.free(dve.tensor_tensor(tmp[:, :], k.ps[:, i, :], c("sin"), ALU.mult))
                    steps(dve.tensor_tensor(lat(i), lat(i), c("cos"), ALU.mult))
                    steps(dve.tensor_tensor(lat(i), lat(i), tmp[:, :], ALU.add))
    made.close(len(tiles))


def conformer(k, cin, mixT, nq):
    nc, c2 = k.nc, k.c2
    GAP = 2 * CH_HALF
    with_ctx = nq > SEQ
    n_out = SEQ + (GAP + CTX if with_ctx else 0)
    at_ctx = SEQ + GAP
    low = k.sig["low"]
    ntq = nq // P
    with ExitStack() as ctx:
        sb = k.alloc(ctx)
        pad = sb("pad", [P, 2, n_out + GAP])
        z = sb("z", [P, 2, n_out])
        zt = sb("zt", [P, NT2, 2 * P])
        with nc.Block() as block:
            @block.scalar
            def _(act):
                steps = k.steps(act, "s")
                steps.free(act.activation(cin[:, 1, :, 0:nq], cin[:, 1, :, 0:nq], ACT.Sigmoid))
                steps.tell(low.sem)

            @block.vector
            def _(dve):
                steps = k.steps(dve, "v")
                steps(dve.memset(pad[:, :, :], 0.0))
                dve.wait_ge(low.sem, low.of(1))
                steps.free(dve.tensor_tensor(pad[:, :, CH_HALF:CH_HALF + SEQ], cin[:, 0, :, 0:SEQ], cin[:, 1, :, 0:SEQ],
                                             ALU.mult))
                if with_ctx:
                    steps.free(dve.tensor_tensor(pad[:, :, at_ctx + CH_HALF:at_ctx + CH_HALF + CTX],
                                                 cin[:, 0, :, SEQ:T2], cin[:, 1, :, SEQ:T2], ALU.mult))
                steps.join()
                for tap in range(CW):
                    for g in range(2):
                        w = c2("conv_w", 2 * tap + g)
                        src = pad[:, g, tap:tap + n_out]
                        if tap == 0:
                            steps.free(dve.tensor_scalar(z[:, g, :], src, w, c2("conv_b", g), ALU.mult, ALU.add))
                        else:
                            steps.free(dve.scalar_tensor_tensor(z[:, g, :], src, w, z[:, g, :], ALU.mult, ALU.add))
                    steps.join()
        low.close(1)

        def column(t):
            return P * t if t < NTL else at_ctx + P * (t - NTL)
        groups = []
        for t in range(ntq):
            groups.append(dict(places=8, tr=[(k.ps[:, t, g * P:(g + 1) * P], z[:, g, column(t):column(t) + P], P)
                                             for g in range(2)]))

        def take(k, who, i, steps):
            return copy_out(k, who, zt[:, i, :], k.ps[:, i, 0:2 * P])
        products(k, groups, take)
        layer_norm(k, [(zt[:, t, :], zt[:, t, :], None, None) for t in range(ntq)])
        made = k.sig["made"]
        with nc.Block() as block:
            @block.tensor
            def _(pe):
                for t in range(ntq):
                    for g in range(2):
                        mm = pe.transpose(k.ps[:, t, g * P:(g + 1) * P], zt[:, t, g * P:(g + 1) * P], k.c("ident"))
                    mm.then_inc(made.sem, 1)

            @block.scalar
            def _(act):
                steps = k.steps(act, "s")
                for t in range(ntq):
                    act.wait_ge(made.sem, made.of(t + 1))
                    for g in range(2):
                        steps.free(act.activation(mixT[:, 6 + g, P * t:P * t + P], k.ps[:, t, g * P:(g + 1) * P], ACT.Silu,
                                                  bias=c2("ln_b", g), scale=c2("ln_g", g)))
                steps.join()
        made.close(ntq)


def mixers(k, sb, l, ntq, qa, ka, qb, kb, va, vb, mixT):
    nc, c, c2 = k.nc, k.c, k.c2
    NB = 4
    bias = sb("bias", [P, NB, BIAS_ROWS, GRID_W])
    raw = sb("raw", [P, NB, BIAS_ROWS, GRID_W])
    src = k.dram["bias"]
    loads, made = k.sig["load"], k.sig["made"]
    cut = BANK // GRID_W
    with nc.Block() as block:
        @block.sync
        def _(sp):
            for half in range(2):
                for h in range(NB):
                    a = src[l, h, 1 - half:1 - half + BIAS_ROWS, 0:GRID_W]
                    sp.dma_start(raw[GRID_W * half:GRID_W * (half + 1), h, :, :],
                                 bass.AP(a.tensor, a.offset,
                                         [[1, GRID_W], [BIAS_PAD, BIAS_ROWS], [1, GRID_W]])).then_inc(loads.sem, 16)

        @block.tensor
        def _(pe):
            pe.wait_ge(loads.sem, loads.of(16 * 2 * NB))
            for h in range(NB):
                pe.matmul(k.ps[:, 2 * h, :], c("flip"), raw[:, h, 0:cut, :].rearrange("p r c -> p (r c)"), start=True,
                          stop=True)
                pe.matmul(k.ps[:, 2 * h + 1, 0:(BIAS_ROWS - cut) * GRID_W], c("flip"),
                          raw[:, h, cut:BIAS_ROWS, :].rearrange("p r c -> p (r c)"), start=True,
                          stop=True).then_inc(made.sem, 1)

        @block.vector
        def _(dve):
            steps = k.steps(dve, "v")
            for h in range(NB):
                dve.wait_ge(made.sem, made.of(h + 1))
                rows = k.psf[:, 2 * h * BANK:2 * h * BANK + BIAS_ROWS * GRID_W].rearrange("p (r c) -> p r c", c=GRID_W)
                steps.free(dve.tensor_tensor(bias[:, h, :, :], rows,
                                             c("col_mask").unsqueeze(1).to_broadcast([P, BIAS_ROWS, GRID_W]), ALU.add))
            steps.join()
    loads.close(16 * 2 * NB)
    made.close(NB)
    units = []
    ctx_values = lambda v, s: [(v[:, NTL + i, s], P, P * i) for i in range(2)]
    for t in range(ntq):
        for h in range(8):
            kv, g = h // 4, h % 4
            b = slice(HD * kv, HD * kv + HD)
            q = qa[b, g, P * t:P * t + P]
            scores = [(0, [(q, ka[b, SEQ:T2])])]
            values, adds, width = ctx_values(va, b), [], CTX
            if t < NTL:
                w0, w1 = max(0, t - 1), min(NTL - 1, t + 1)
                scores.append((CTX, [(q, ka[b, P * w0:P * (w1 + 1)])]))
                for w in range(w0, w1 + 1):
                    col = CTX + P * (w - w0)
                    values.append((va[:, w, b], P, col))
                    if w != t:
                        adds.append((col, c("band_prev" if w < t else "band_next")))
                width += P * (w1 - w0 + 1)
            units.append(dict(q=q, base=b.start, width=width, sink=c2("sink", h), scores=scores, adds=adds,
                              values=values, out=mixT[b, g, P * t:P * t + P]))
        for h in range(NB):
            b = slice(HD * (h % 2), HD * (h % 2) + HD)
            s = slice(HD * h, HD * h + HD)
            q = qb[b, h // 2, P * t:P * t + P]
            if t < NTL:
                m0 = GRID_H - 1 - 2 * t
                units.append(dict(q=q, base=b.start, width=T2, sink=None,
                                  scores=[(0, [(q, kb[b, h // 2, 0:SEQ])]), (SEQ, [(q, kb[b, h // 2, SEQ:T2])])],
                                  adds=[(0, bias[:, h, m0:m0 + GRID_H, :].rearrange("p r c -> p (r c)"))],
                                  values=[(vb[:, w, s], P, P * w) for w in range(NT2)],
                                  out=mixT[b, 4 + h // 2, P * t:P * t + P]))
            else:
                units.append(dict(q=q, base=b.start, width=CTX, sink=None, scores=[(0, [(q, kb[b, h // 2, SEQ:T2])])],
                                  adds=[], values=ctx_values(vb, s), out=mixT[b, 4 + h // 2, P * t:P * t + P]))
    attention(k, units)


def project_out(k, mixT, o, ntq):
    groups, where = [], []
    for half in range(2):
        a, b = k.stream.take(), k.stream.take()
        s = [k.stream.slot(x).rearrange("p (k c) -> p k c", k=4) for x in (a, b)]
        for t in range(ntq):
            i = len(groups)
            groups.append(dict(places=8, needs=[a, b] if t == 0 else [], last=[a, b] if t == ntq - 1 else [],
                               mm=[(k.ps[:, i % 8, :], mixT[:, c_, P * t:P * t + P], s[c_ // 4][:, c_ % 4, :],
                                    c_ == 0, c_ == KD - 1) for c_ in range(KD)]))
            where.append((t, half))

    def take(k, who, i, steps):
        t, half = where[i]
        return copy_out(k, who, o[:, t, half * BANK:(half + 1) * BANK], k.ps[:, i % 8, :])
    products(k, groups, take)


def residual(k, sb, l, which, x, o, mod, ntq):
    nc, c = k.nc, k.c
    made, moved = k.sig["made"], k.sig["moved"]
    nw = 2 if ntq > NTL else 1
    with ExitStack() as ctx:
        sbi = k.alloc(ctx)
        gb = sbi("gb", [P, 2, D])
        grow = sbi("grow", [P, 2, D])
        diag = sbi("diag", [P, 2, P])
        load(k, [(gb[:, i, :], k.dram["rows2"][l, 2 * which + i].partition_broadcast(P)) for i in range(2)])
        todo = [(w, c_) for w in range(nw) for c_ in range(KD)]
        with nc.Block() as block:
            @block.vector
            def _(dve):
                steps = k.steps(dve, "v")
                for i, (w, c_) in enumerate(todo):
                    if i >= 2:
                        dve.wait_ge(made.sem, made.of(i - 1))
                    gate = mod[:, (3 * which + 2) * KD + c_, w:w + 1]
                    dve.tensor_scalar(diag[:, i % 2, :], c("ident"), gate, None, ALU.mult).then_inc(moved.sem, 1)
                dve.wait_ge(made.sem, made.of(len(todo)))
                for w in range(nw):
                    steps.free(dve.tensor_copy(grow[:, w, :], k.psf[:, D * w:D * w + D]))
                steps.join()
                for t in range(ntq):
                    w = int(t >= NTL)
                    steps.free(dve.tensor_tensor(o[:, t, :], o[:, t, :], grow[:, w, :], ALU.mult))
                steps.join()
                for t in range(ntq):
                    steps.free(dve.scalar_tensor_tensor(x[:, t, :], x[:, t, :], ALPHA, o[:, t, :], ALU.mult, ALU.add))
                steps.join()

            @block.tensor
            def _(pe):
                for i, (w, c_) in enumerate(todo):
                    pe.wait_ge(moved.sem, moved.of(i + 1))
                    pe.matmul(k.psf[:, D * w + P * c_:D * w + P * c_ + P], c("ones"), diag[:, i % 2, :], start=True,
                              stop=True, skip_group_check=True).then_inc(made.sem, 1)
        made.close(len(todo))
        moved.close(len(todo))
        layer_norm(k, [(x[:, t, :], x[:, t, :], gb[:, 0, :], gb[:, 1, :]) for t in range(ntq)])


def experts(k, sb, l, x, mod, ntq, moe):
    nc, c, c2 = k.nc, k.c, k.c2
    with_ctx = ntq > NTL
    u = sb("u2", [P, NT2, D])
    aff = sb("aff", [P, NT2, N_EXP])
    pos = sb("pos", [P, NT2, N_EXP + 2])
    layer_norm(k, [(x[:, t, :], u[:, t, :], None, None) for t in range(ntq)])
    with ExitStack() as ctx:
        sbi = k.alloc(ctx)
        uT = sbi("uT2", [P, KD, T2])
        to_channels(k, [(u[:, t, :], P, P * t, int(t >= NTL)) for t in range(ntq)], uT,
                    lambda w, c_: mod[:, 4 * KD + c_, w:w + 1], lambda w, c_: mod[:, 3 * KD + c_, w:w + 1])
        route(k, sbi, uT, aff, pos, ntq)
    xsL = sb("xsL", [P, KD, 2, CAP_L])
    xsC = sb("xsC", [P, KD, 2, CAP_C])
    choL = sb("choL", [P, NTL, 2, CAP_L])
    choC = sb("choC", [P, 2, 2, CAP_C])
    gatL = sb("gatL", [P, NTL, 2, CAP_L])
    gatC = sb("gatC", [P, 2, 2, 2, 2, CAP_C])
    gtL = sb("gtL", [P, NTL, P])
    gtC = sb("gtC", [P, 2, 2, P])
    hidL = sb("hidL", [P, FF])
    hidC = sb("hidC", [P, BANK])
    htL = sb("htL", [P, KD, P])
    htC = sb("htC", [P, KD // 2, P])
    yeL = sb("yeL", [P, D])
    yeC = sb("yeC", [P, BANK])
    sg = k.sig
    used, choice, gath, xs_, gatd, gtr, gts = (sg[n] for n in ("used", "choice", "gath", "xs", "gatd", "gtr", "gts"))
    silu, hid, htr, hts, yes, scat, added = (sg[n] for n in ("silu", "hid", "htr", "hts", "yes", "scat", "added"))
    inner_v, inner_s = sg["inner_v"], sg["inner_s"]
    base = k.moe_at[l]
    stream = k.stream
    loaded = stream.loaded
    assert stream.taken == base and 24 % RING == 0 and RING == 8
    PAIRS = N_EXP // 2
    PER = 24
    C = int(with_ctx)
    NG = 2 + C
    n_sc = 2 * NTL + 4 * C
    GB, UB, CG, CU, MISC = 0, 2, 4, 5, 6

    def weight(e, j):
        m, kh, half, par = j // 8, j % 8 // 4, j % 4 // 2, j % 2
        return k.dram[("w_gate", "w_up", "w_down")[m]][l, e + par, BANK * kh:BANK * (kh + 1),
                                                       BANK * half:BANK * (half + 1)].rearrange("(k p) c -> p k c", p=P)

    def slot(j):
        return stream.slot(base + j).rearrange("p (k c) -> p k c", k=4)

    for j in range(RING):
        stream.chunks[base + j] = weight(0, j)
    stream.limit = base + RING
    with nc.Block() as block:
        @block.vector
        def _(dve):
            steps = k.steps(dve, "v")
            for t_ in (gatC, yeL, yeC, moe, gtL, gtC):
                steps.free(dve.memset(t_[tuple([slice(None)] * len(t_.shape))], 0.0))
            steps.join()
            for s in (yes, gtr, htr):
                dve.sem_inc(s.sem, 1)

        @block.sync
        def _(sp):
            stream.issue(sp)
    for s in (yes, gtr, htr):
        s.close(1)

    with nc.Block() as block:
        @block.sync
        def _(sp):
            def fetch(pr, j, freed):
                sp.wait_ge(used.sem, used.of(freed))
                sp.dma_start(slot(j), weight(2 * pr, j)).then_inc(loaded[(base + j) % RING], 16)
            with sp.Fori(0, PAIRS - 1) as pr:
                for j in range(RING, PER):
                    fetch(pr, j, 6 * pr + j // 4 - 1)
                for j in range(RING):
                    fetch(pr + 1, j, 6 * pr + 5 + j // 4)
            for j in range(RING, PER):
                fetch(PAIRS - 1, j, 6 * (PAIRS - 1) + j // 4 - 1)

        @block.tensor
        def _(pe):
            def gather(n):
                pe.wait_ge(choice.sem, choice.of(n))
                for part in range(2):
                    for c_ in range(4):
                        for t in range(NTL):
                            ch = 4 * part + c_
                            mm = pe.matmul(k.ps[:, MISC + part, c_ * P:(c_ + 1) * P], u[:, t, ch * P:(ch + 1) * P],
                                           choL[:, t, :, :].rearrange("p a s -> p (a s)"), start=t == 0,
                                           stop=t == NTL - 1, skip_group_check=True)
                    mm.then_inc(gath.sem, 1)
                if C:
                    pe.wait_ge(xs_.sem, xs_.of(NG * (n - 1) + 1))
                    for ch in range(KD):
                        for t in range(2):
                            mm = pe.matmul(k.ps[:, MISC, ch * HD:(ch + 1) * HD], u[:, NTL + t, ch * P:(ch + 1) * P],
                                           choC[:, t, :, :].rearrange("p a s -> p (a s)"), start=t == 0, stop=t == 1,
                                           skip_group_check=True)
                    mm.then_inc(gath.sem, 1)

            def matrix(pr, m, bank, cbank, lhsL, lhsC):
                for kh in range(2):
                    for x in range(4):
                        j = 8 * m + 4 * kh + x
                        pe.wait_ge(loaded[(base + j) % RING], 16 * ((base + j) // RING + 1) + 16 * (PER // RING) * pr)
                    w = [[slot(8 * m + 4 * kh + 2 * half + par) for par in range(2)] for half in range(2)]
                    for kk in range(4):
                        for half in range(2):
                            for par in range(2):
                                mm = pe.matmul(k.ps[HD * par:HD * par + HD, bank + half, :], lhsL(4 * kh + kk, par),
                                               w[half][par][:, kk, :], start=kh + kk == 0, stop=kh == 1 and kk == 3,
                                               skip_group_check=True)
                    if C:
                        for kk in range(4):
                            for par in range(2):
                                for half in range(2):
                                    q = 32 * (2 * par + half)
                                    mm = pe.matmul(k.ps[q:q + CAP_C, cbank, :], lhsC(4 * kh + kk, par),
                                                   w[half][par][:, kk, :], start=kh + kk == 0, stop=kh == 1 and kk == 3,
                                                   skip_group_check=True)
                    mm.then_inc(used.sem, 1)

            def scatter(n):
                for i in range(n_sc):
                    if i >= 2:
                        pe.wait_ge(added.sem, added.of(n_sc * n + i - 1))
                    lat = i < 2 * NTL
                    half = i % 2
                    if lat:
                        lhsT, rhs = gtL[:, i // 2, :], yeL[:, half * BANK:(half + 1) * BANK]
                    else:
                        lhsT, rhs = gtC[:, i // 2 - NTL, half, :], yeC[:, :]
                    pe.matmul(k.ps[:, MISC + i % 2, :], lhsT, rhs, start=True, stop=True,
                              skip_group_check=True).then_inc(scat.sem, 1)

            gather(1)
            with pe.Fori(0, PAIRS) as pr:
                pe.wait_ge(xs_.sem, xs_.of(NG * pr + NG))
                matrix(pr, 0, GB, CG, lambda c_, par: xsL[:, c_, par, :], lambda c_, par: xsC[:, c_, par, :])
                pe.wait_ge(yes.sem, yes.of((1 + C) * pr))
                scatter(pr)
                matrix(pr, 1, UB, CU, lambda c_, par: xsL[:, c_, par, :], lambda c_, par: xsC[:, c_, par, :])
                pe.wait_ge(added.sem, added.of(n_sc * pr + n_sc))
                gather(pr + 2)
                pe.wait_ge(gatd.sem, gatd.of(pr + 1))
                pe.wait_ge(xs_.sem, xs_.of(NG * (pr + 1) + 2))
                for t in range(NTL):
                    mm = pe.transpose(k.ps[:, MISC + 1, t * P:(t + 1) * P], gatL[:, t, :, :].rearrange("p a s -> p (a s)"),
                                      c("ident"))
                mm.then_inc(gtr.sem, 1)
                if C:
                    pe.wait_ge(xs_.sem, xs_.of(NG * (pr + 1) + 3))
                    for t in range(2):
                        for half in range(2):
                            mm = pe.transpose(k.ps[:, MISC, (2 * t + half) * P:(2 * t + half + 1) * P],
                                              gatC[:, t, half, :, :, :].rearrange("p a h s -> p (a h s)"), c("ident"))
                    mm.then_inc(gtr.sem, 1)
                for part in range(1 + C):
                    pe.wait_ge(hid.sem, hid.of((1 + C) * pr + part + 1))
                    for c_ in range(KD if part == 0 else KD // 2):
                        bank = GB + c_ // 4 if part == 0 else CG
                        src = (hidL if part == 0 else hidC)[:, c_ * P:(c_ + 1) * P]
                        mm = pe.transpose(k.ps[:, bank, (c_ % 4) * P:(c_ % 4 + 1) * P], src, c("ident"))
                    mm.then_inc(htr.sem, 1)
                pe.wait_ge(hts.sem, hts.of((1 + C) * (pr + 1)))
                matrix(pr, 2, UB, CU, lambda c_, par: htL[:, c_, par * HD:(par + 1) * HD],
                       lambda c_, par: htC[:, c_ % 4, par * HD + CAP_C * (c_ // 4):par * HD + CAP_C * (c_ // 4) + CAP_C])
            pe.wait_ge(yes.sem, yes.of((1 + C) * PAIRS))
            pe.wait_ge(gts.sem, gts.of((1 + C) * PAIRS))
            scatter(PAIRS)

        @block.vector
        def _(dve):
            done = [0]

            def tick(ins):
                ins.then_inc(inner_v.sem, 1)
                done[0] += 1

            def settle(ticks):
                dve.wait_ge(inner_v.sem, inner_v.of(ticks + done[0]))

            def shape(ap, n, w):
                return ap.unsqueeze(3).to_broadcast([P, n, 2, w])

            def iota(n, w):
                return c("iota")[:, 0:w].unsqueeze(1).unsqueeze(1).to_broadcast([P, n, 2, w])

            def choose(e, ticks):
                tick(dve.tensor_tensor(choL[:, :, :, :], iota(NTL, CAP_L), shape(pos[:, 0:NTL, bass.ds(e, 2)], NTL, CAP_L),
                                       ALU.is_equal))
                if C:
                    tick(dve.tensor_tensor(choC[:, :, :, :], iota(2, CAP_C), shape(pos[:, NTL:NT2, bass.ds(e, 2)], 2, CAP_C),
                                           ALU.is_equal))
                settle(ticks)
                dve.sem_inc(choice.sem, 1)

            def gate(e, ticks):
                tick(dve.tensor_tensor(gatL[:, :, :, :], iota(NTL, CAP_L), shape(pos[:, 0:NTL, bass.ds(e, 2)], NTL, CAP_L),
                                       ALU.is_equal))
                if C:
                    for half in range(2):
                        tick(dve.tensor_tensor(gatC[:, :, half, :, half, :], iota(2, CAP_C),
                                               shape(pos[:, NTL:NT2, bass.ds(e, 2)], 2, CAP_C), ALU.is_equal))
                settle(ticks)
                tick(dve.tensor_tensor(gatL[:, :, :, :], gatL[:, :, :, :], shape(aff[:, 0:NTL, bass.ds(e, 2)], NTL, CAP_L),
                                       ALU.mult))
                if C:
                    for half in range(2):
                        g = gatC[:, :, half, :, half, :]
                        tick(dve.tensor_tensor(g, g, shape(aff[:, NTL:NT2, bass.ds(e, 2)], 2, CAP_C), ALU.mult))
                settle(ticks)
                dve.sem_inc(gatd.sem, 1)

            def tokens_out(n, ticks):
                for part in range(NG):
                    dve.wait_ge(gath.sem, gath.of(NG * (n - 1) + part + 1))
                    w, lo, nc_, m = (0, 4 * part, 4, P) if part < 2 else (1, 0, KD, HD)
                    src = k.ps[:, MISC + part % 2, :].rearrange("p (k s) -> p k s", s=m)
                    dst = (xsL if part < 2 else xsC)[:, lo:lo + nc_, :, :].rearrange("p k a s -> p k (a s)")
                    sc = mod[:, 4 * KD + lo:4 * KD + lo + nc_, w:w + 1].to_broadcast([P, nc_, m])
                    sh = mod[:, 3 * KD + lo:3 * KD + lo + nc_, w:w + 1].to_broadcast([P, nc_, m])
                    tick(dve.tensor_tensor(dst, src, sc, ALU.mult))
                    settle(ticks)
                    tick(dve.tensor_tensor(dst, dst, sh, ALU.add))
                    settle(ticks)
                    dve.sem_inc(xs_.sem, 1)

            def add(n):
                for i in range(n_sc):
                    dve.wait_ge(scat.sem, scat.of(n_sc * n + i + 1))
                    y = moe[:, i // 2, (i % 2) * BANK:(i % 2 + 1) * BANK]
                    dve.tensor_tensor(y, y, k.ps[:, MISC + i % 2, :], ALU.add).then_inc(added.sem, 1)

            choose(0, 0)
            tokens_out(1, 0)
            before = done[0]
            body = (1 + C) + (2 + 4 * C) + 2 * NG
            with dve.Fori(0, PAIRS) as pr:
                ticks = body * pr + before
                done[0] = 0
                choose(2 * pr + 2, ticks)
                dve.wait_ge(gtr.sem, gtr.of((1 + C) * pr))
                gate(2 * pr, ticks)
                add(pr)
                for part in range(1 + C):
                    dve.wait_ge(used.sem, used.of(6 * pr + 4))
                    dve.wait_ge(silu.sem, silu.of((1 + C) * pr + part + 1))
                    h, src = ((hidL, k.psf[:, UB * BANK:(UB + 2) * BANK]), (hidC, k.ps[:, CU, :]))[part]
                    dve.tensor_tensor(h[:, :], h[:, :], src, ALU.mult).then_inc(hid.sem, 1)
                tokens_out(pr + 2, ticks)
                assert done[0] == body
            add(PAIRS)
            dve.wait_ge(added.sem, added.of(n_sc * (PAIRS + 1)))
            inner_v.close(before + body * PAIRS)

        @block.scalar
        def _(act):
            with act.Fori(0, PAIRS) as pr:
                act.wait_ge(used.sem, used.of(6 * pr + 2))
                act.wait_ge(htr.sem, htr.of((1 + C) * pr))
                act.activation(hidL[:, :], k.psf[:, GB * BANK:(GB + 2) * BANK], ACT.Silu).then_inc(silu.sem, 1)
                if C:
                    act.activation(hidC[:, :], k.ps[:, CG, :], ACT.Silu).then_inc(silu.sem, 1)
                act.wait_ge(scat.sem, scat.of(n_sc * pr + n_sc))
                act.wait_ge(gtr.sem, gtr.of((1 + C) * pr + 1))
                act.copy(gtL[:, :, :], k.ps[:, MISC + 1, :].rearrange("p (t q) -> p t q", t=NTL)).then_inc(gts.sem, 1)
                if C:
                    act.wait_ge(gtr.sem, gtr.of((1 + C) * pr + 2))
                    act.copy(gtC[:, :, :, :], k.ps[:, MISC, :].rearrange("p (t h q) -> p t h q", t=2, h=2)).then_inc(gts.sem, 1)
                act.wait_ge(htr.sem, htr.of((1 + C) * pr + 1))
                act.copy(htL[:, :, :], k.psf[:, GB * BANK:(GB + 2) * BANK].rearrange("p (k s) -> p k s", k=KD)).then_inc(hts.sem, 1)
                if C:
                    act.wait_ge(htr.sem, htr.of((1 + C) * pr + 2))
                    act.copy(htC[:, :, :], k.ps[:, CG, :].rearrange("p (k s) -> p k s", k=4)).then_inc(hts.sem, 1)
                act.wait_ge(used.sem, used.of(6 * pr + 6))
                act.copy(yeL[:, :], k.psf[:, UB * BANK:(UB + 2) * BANK]).then_inc(yes.sem, 1)
                if C:
                    act.copy(yeC[:, :], k.ps[:, CU, :]).then_inc(yes.sem, 1)
            act.wait_ge(yes.sem, yes.of((1 + C) * PAIRS))
            act.wait_ge(gts.sem, gts.of((1 + C) * PAIRS))
    used.close(6 * PAIRS)
    choice.close(PAIRS + 1)
    gath.close(NG * (PAIRS + 1))
    xs_.close(NG * (PAIRS + 1))
    gatd.close(PAIRS)
    for s in (gtr, gts, silu, hid, htr, hts, yes):
        s.close((1 + C) * PAIRS)
    scat.close(n_sc * (PAIRS + 1))
    added.close(n_sc * (PAIRS + 1))
    stream.taken = stream.issued = base + PER * PAIRS
    for j in range(PER - RING, PER):
        stream.freed(base + PER * (PAIRS - 1) + j, used.sem, used.base - 5 + j // 4)
    stream.limit = k.moe_at[l + 1] if l + 1 < LAYERS else len(stream.chunks)


def route(k, sb, uT, aff, pos, ntq):
    nc, c, c2 = k.nc, k.c, k.c2
    made, moved, low = k.sig["made"], k.sig["moved"], k.sig["low"]
    ps = k.ps
    nx = sb("nx", [P, NT2])
    affT = sb("affT", [N_EXP, T2])
    work = sb("work", [N_EXP, T2])
    best = sb("best", [N_EXP, 8])
    one = sb("one_", [N_EXP, T2])
    parts = [(0, SEQ, CAP_L)] + ([(SEQ, CTX, CAP_C)] if ntq > NTL else [])
    r = c2("router", 0, KD * N_EXP).rearrange("p (k e) -> p k e", k=KD)
    with nc.Block() as block:
        @block.tensor
        def _(pe):
            for t in range(ntq):
                for c_ in range(KD):
                    mm = pe.matmul(ps[:, 0, t * N_EXP:(t + 1) * N_EXP], uT[:, c_, P * t:P * t + P], r[:, c_, :],
                                   start=c_ == 0, stop=c_ == KD - 1, skip_group_check=True)
            mm.then_inc(made.sem, 1)
            pe.wait_ge(moved.sem, moved.of(1))
            for t in range(ntq):
                mm = pe.transpose(ps[0:N_EXP, 1 + t // 4, (t % 4) * P:(t % 4 + 1) * P], aff[:, t, :], c("ident"))
            mm.then_inc(made.sem, 1)
            pe.wait_ge(moved.sem, moved.of(2))
            for t in range(ntq):
                mm = pe.transpose(ps[:, 3, t * N_EXP:(t + 1) * N_EXP], work[:, P * t:P * t + P],
                                  c("ident")[0:N_EXP, 0:N_EXP])
            mm.then_inc(made.sem, 1)

        @block.scalar
        def _(act):
            steps = k.steps(act, "s")
            act.wait_ge(low.sem, low.of(1))
            steps.free(act.activation(aff[:, 0:ntq, :], aff[:, 0:ntq, :], ACT.Exp))
            steps.tell(low.sem)

        @block.vector
        def _(dve):
            steps = k.steps(dve, "v")
            dve.wait_ge(made.sem, made.of(1))
            lg = ps[:, 0, 0:ntq * N_EXP].rearrange("p (t e) -> p t e", e=N_EXP)
            b = nx[:, 0:ntq].unsqueeze(2).to_broadcast([P, ntq, N_EXP])
            A = aff[:, 0:ntq, :]
            steps(dve.tensor_reduce(nx[:, 0:ntq], lg, AX.X, ALU.max))
            steps.free(dve.tensor_tensor(A, lg, b, ALU.subtract))
            steps.tell(low.sem)
            dve.wait_ge(low.sem, low.of(2))
            steps(dve.tensor_reduce(nx[:, 0:ntq], A, AX.X, ALU.add))
            steps(dve.reciprocal(nx[:, 0:ntq], nx[:, 0:ntq]))
            steps.free(dve.tensor_tensor(A, A, b, ALU.mult))
            steps.tell(moved.sem)
            steps.free(dve.memset(one[:, :], 1.0))
            steps(dve.memset(pos[:, :, N_EXP:N_EXP + 2], -1.0))
            dve.wait_ge(made.sem, made.of(2))
            steps(dve.tensor_copy(affT[:, 0:ntq * P], k.psf[0:N_EXP, BANK:BANK + ntq * P]))
            for lo, n, cap in parts:
                w = affT[:, lo:lo + n]
                for _ in range(cap // 8):
                    steps(dve.max(best[:, :], w))
                    steps(dve.match_replace(w, best[:, :], w, -1.0))
                m = work[:, lo:lo + n]
                steps(dve.tensor_scalar(w, w, 0.0, None, ALU.is_lt))
                steps(dve.tensor_tensor_scan(m, one[:, 0:n], w, 0.0, ALU.mult, ALU.add))
                steps(dve.tensor_tensor(m, m, w, ALU.mult))
                steps(dve.tensor_scalar(m, m, -1.0, None, ALU.add))
            dve.sem_inc(moved.sem, 1)
            dve.wait_ge(made.sem, made.of(3))
            steps(dve.tensor_copy(pos[:, 0:ntq, 0:N_EXP], ps[:, 3, 0:ntq * N_EXP].rearrange("p (t e) -> p t e", e=N_EXP)))
    made.close(3)
    moved.close(2)
    low.close(2)


SIGNALS = ["product", "taken_v", "taken_s", "load", "squared", "rooted", "meant", "scores", "row_max", "exp",
           "probs", "turned", "pt", "out", "out_taken", "low", "fine", "fin2", "made", "moved", "stored",
           "used", "choice", "gath", "xs", "gatd", "gtr", "gts", "silu", "hid", "htr", "hts", "yes", "scat",
           "added", "inner_v", "inner_s"]


def program(nc, dram, out):
    k = Kernel()
    k.nc, k.dram, k.out = nc, dram, out
    with ExitStack() as ctx:
        k.ctx = ctx
        k.uid = 0

        def alloc(scope):
            def sb(name, shape, dt=F32):
                k.uid += 1
                return scope.enter_context(nc.sbuf_tensor(f"{name}_{k.uid}", shape, dt))
            return sb
        k.alloc = alloc
        sb = alloc(ctx)
        k.ps = ctx.enter_context(nc.psum_tensor("ps", [P, 8, BANK], F32))
        k.psf = k.ps[:, :, :].rearrange("p b c -> p (b c)")
        k.sig = {n: Signal(ctx.enter_context(nc.semaphore(n))) for n in SIGNALS}
        done = {w: Steps(None, ctx.enter_context(nc.semaphore("steps_" + w))) for w in ("v", "s", "g")}

        def steps(eng, who):
            done[who].eng = eng
            return done[who]
        k.steps = steps

        ring = sb("ring", [P, RING, CHUNK])
        loaded = [ctx.enter_context(nc.semaphore(f"loaded{i}")) for i in range(RING)]
        chunks = [dram["w1"][i] for i in range(FIRST_CHUNKS)]
        k.moe_at = []
        for l in range(LAYERS):
            chunks += [dram["w2"][l, i] for i in range(LAYER_CHUNKS)]
            k.moe_at.append(len(chunks))
            chunks += [None] * 12 * N_EXP
        k.stream = Stream(ring, loaded, chunks)
        k.stream.limit = RING // 2
        const = sb("const", [P, CONSTS[0][0].shape[1]])
        k.h1 = sb("h1", [P, NT2, D])
        with ExitStack() as first:
            const1 = alloc(first)("const1", [P, CONSTS[1][0].shape[1]])
            cols1 = alloc(first)("cols1", [P, NP1])
            at = {**{n: (const, x) for n, x in CONSTS[0][1].items()}, **{n: (const1, x) for n, x in CONSTS[1][1].items()}}
            k.c = lambda name: at[name][0][:, at[name][1][0]:at[name][1][0] + at[name][1][1]]
            k.c1 = lambda name, i, n=1: cols1[:, AT1[name] + i:AT1[name] + i + n]
            k.c1m = lambda name, n: cols1[:, AT1[name]:AT1[name] + n]
            k.one = const[:, CONSTS[0][1]["ones"][0]:CONSTS[0][1]["ones"][0] + 1]
            load(k, [(const[:, :], dram["const0"]), (const1[:, :], dram["const1"]), (cols1[:, :], dram["cols1"])])
            first_block(k)
        second_block(k)
        stored = k.sig["stored"]
        with nc.Block() as block:
            @block.sync
            def _(sp):
                for j in range(NTL):
                    sp.dma_start(out[0, P * j:P * j + P, :], k.h1[:, j, :]).then_inc(stored.sem, 16)
                sp.wait_ge(stored.sem, stored.of(16 * NTL))


def by_channel(v):
    v = np.asarray(v)
    return v.reshape(-1, P).T


def k_tiles(w):
    w = np.asarray(w)
    return w.reshape(-1, P, w.shape[1]).transpose(1, 0, 2).reshape(P, -1)


def column_chunks(w, width=256):
    w = np.asarray(w)
    return w.reshape(KD, P, -1, width).transpose(2, 1, 0, 3).reshape(-1, P, CHUNK)


def row_chunks(w):
    w = np.asarray(w)
    return w.reshape(2, 4, P, 2, BANK).transpose(3, 0, 2, 1, 4).reshape(-1, P, CHUNK)


def block_diagonal(w):
    w = np.asarray(w)
    out = np.zeros((P, 2, P), w.dtype)
    for h in range(4):
        b = HD * (h % 2)
        out[b:b + HD, h // 2, b:b + HD] = w[h]
    return out.reshape(P, -1)


def lay_out(i):
    f = np.float32
    a = {n: np.asarray(v) for n, v in i.items()}
    w_in = a["w_in"][0]
    first = 2 * LRU_W
    fox = w_in[:, first:first + 3 * FOX_W + FOX_HEADS]
    heads = w_in[:, first + 3 * FOX_W + FOX_HEADS:]
    up = a["ffn_up"][0].reshape(KD, P, 2, FT, P).transpose(3, 1, 0, 2, 4).reshape(FT, P, CHUNK)
    down = a["ffn_down"][0].reshape(FT // 2, 2, P, D).transpose(0, 2, 1, 3).reshape(FT // 2, P, CHUNK)
    w1 = np.concatenate([column_chunks(heads), column_chunks(w_in[:, :first]), column_chunks(fox[:, :3 * FOX_W]),
                         row_chunks(a["w_out"][0]), up, down])
    cols = dict(norm_mix_pre=by_channel(a["norm_mix_pre"][0]), norm_ffn_pre=by_channel(a["norm_ffn_pre"][0]),
                lru_conv_w=by_channel(a["lru_conv_w"][0]), lru_conv_b=by_channel(a["lru_conv_b"][0]),
                lru_gate_a_b=by_channel(a["lru_gate_a_b"][0]), lru_gate_x_b=by_channel(a["lru_gate_x_b"][0]),
                lru_lambda=by_channel(a["lru_lambda"][0]), rwkv_mu=by_channel(a["rwkv_mu"][0]),
                rwkv_w0=by_channel(a["rwkv_w0"][0]), rwkv_a0=by_channel(a["rwkv_a0"][0]),
                rwkv_k_k=by_channel(a["rwkv_k_k"][0]), rwkv_k_a=by_channel(a["rwkv_k_a"][0]),
                rwkv_r_k=by_channel(a["rwkv_r_k"][0]), rwkv_ln_w=by_channel(a["rwkv_ln_w"][0]),
                rwkv_ln_b=by_channel(a["rwkv_ln_b"][0]),
                fox_f_bias=np.pad(a["fox_f_bias"][0], (0, P - FOX_HEADS))[:, None],
                w_f=k_tiles(fox[:, 3 * FOX_W:]),
                gate_a=block_diagonal(a["lru_gate_a_w"][0]), gate_x=block_diagonal(a["lru_gate_x_w"][0]),
                wa_up=np.concatenate([a["rwkv_w_up"][0], a["rwkv_a_up"][0]]), g_up=a["rwkv_g_up"][0],
                ffn_conv=by_channel(a["ffn_conv"][0]),
                )
    cols1 = np.concatenate([cols[n] for n in COLS1], 1)
    sent = {"x": a["x"][0].reshape(NTL, P, D).transpose(1, 0, 2), "meta": a["meta_tokens"],
            "cond": np.stack([by_channel(a["c_2"][0]), by_channel(a["c_ctx_2"])], 2),
            "w1": w1, "cols1": cols1, "rows1": np.concatenate([a["norm_mix_post"], a["norm_ffn_post"]]),
            "const0": CONSTS[0][0], "const1": CONSTS[1][0], "const2": CONSTS[2][0]}
    order = np.arange(A_WIDTH).reshape(2, 4, HD).transpose(1, 0, 2).reshape(-1)
    w2, cols2, rows2 = [], [], []
    for l in range(LAYERS):
        w_in2, w_out2 = a["w_in_2"][l], a["w_out_2"][l]
        w_in2 = np.concatenate([w_in2[:, order], w_in2[:, A_WIDTH:]], 1)
        w_out2 = np.concatenate([w_out2[order], w_out2[A_WIDTH:]])
        w2.append(np.concatenate([column_chunks(a["w_mod_2"][l]), column_chunks(w_in2), row_chunks(w_out2)]))
        cc = dict(b_mod=by_channel(a["b_mod_2"][l]), conv_w=by_channel(a["conv_w_2"][l]),
                  conv_b=by_channel(a["conv_b_2"][l]), ln_g=by_channel(a["conv_ln_g_2"][l]),
                  ln_b=by_channel(a["conv_ln_b_2"][l]), router=k_tiles(a["w_router_2"][l]),
                  sink=np.broadcast_to(a["a_sink_2"][l], (P, 8)))
        cols2.append(np.concatenate([cc[n] for n in COLS2], 1))
        rows2.append(np.stack([a[n][l] for n in ("ln1_g_2", "ln1_b_2", "ln2_g_2", "ln2_b_2")]))
    bias = np.zeros((LAYERS, 4, BIAS_ROWS + 1, BIAS_PAD), f)
    lo = GRID_W - 1 - (NA_COLS - 1)
    bias[:, :, 1:, lo:lo + 2 * NA_COLS - 1] = a["nat_bias_2"]
    sent.update(w2=np.stack(w2), cols2=np.stack(cols2), rows2=np.stack(rows2), bias=bias,
                ctx=a["ctx_2"][0].reshape(2, P, D).transpose(1, 0, 2),
                w_gate=a["w_gate_2"], w_up=a["w_up_2"], w_down=a["w_down_2"])
    return {n: np.ascontiguousarray(v) for n, v in sent.items()}


def kernel(**inputs):
    import concourse.bacc as bacc
    from concourse.bass_utils import run_bass_kernel_spmd

    nc = bacc.Bacc("TRN2", target_bir_lowering=False, num_devices=1)
    sent = lay_out(inputs)
    arrays, dram = {}, {}
    for name, a in sent.items():
        arrays["in_" + name] = a
        dram[name] = nc.dram_tensor("in_" + name, a.shape, mybir.dt.from_np(a.dtype), kind="ExternalInput").ap()
    out = nc.dram_tensor("out_0_dram", (1, SEQ, D), F32, kind="ExternalOutput").ap()
    program(nc, dram, out)
    r = run_bass_kernel_spmd(nc, [arrays], core_ids=[0])
    return r.results[0]["out_0_dram"]
```

```python
from contextlib import ExitStack

import numpy as np

import concourse.bass as bass
from concourse import mybir

F32 = mybir.dt.float32
ALU = mybir.AluOpType
ACT = mybir.ActivationFunctionType
AX = mybir.AxisListType

P = 128
D = 1024
KD = D // P
SEQ = 512
N_META = 16
T1 = SEQ + N_META
HALF1 = T1 // 2
HD = 64
BANK = 512
NEG = -1e30

LRU_W = 256
FOX_W = 512
FOX_HEADS = FOX_W // HD
RW = 256
RW_HEADS = RW // HD
D_FF = 2816
FT = D_FF // P
CH = 16
NCH = T1 // CH
CPT = P // CH
EXP_HALF = float(np.exp(-0.5))
GN_EPS = 64e-5
RMS_EPS = 1e-6

CTX = 256
T2 = SEQ + CTX
NT2 = T2 // P
NTL = SEQ // P
LAYERS = 2
A_WIDTH = 512
CW = 31
CH_HALF = CW // 2
N_EXP = 16
CAP_L = 2 * SEQ // N_EXP
CAP_C = 2 * CTX // N_EXP
SLOTS = CAP_L + CAP_C
FF = 1024
ALPHA = float((2 * LAYERS) ** 0.25)
LN_EPS = 1e-6
GRID_W = 64
GRID_H = SEQ // GRID_W
NA_COLS = 16
BIAS_ROWS = 2 * GRID_H - 1
BIAS_PAD = 128

RING = 8
CHUNK = 2048


def constants():
    p = np.arange(P)
    f = np.float32
    parts = {}
    parts["ident"] = np.eye(P)
    parts["ones"] = np.ones((P, P))
    parts["fold"] = p[:, None] % 32 == np.arange(2)[None, :]
    parts["head_ones"] = (p[:, None] // HD == p[None, :] // HD)
    parts["causal"] = np.where(p[None, :] <= p[:, None], 0, NEG)
    parts["band_prev"] = np.where(p[None, :] >= p[:, None], 0, NEG)
    parts["band_next"] = np.where(p[None, :] <= p[:, None], 0, NEG)
    same = p[:, None] // CH == p[None, :] // CH
    upper = same & (p[:, None] < p[None, :])
    upper_in = same & (p[:, None] <= p[None, :])
    lower = same & (p[:, None] > p[None, :])
    parts["mask_u"] = np.concatenate([-1.0 * upper, 1.0 * upper], 1)
    parts["mask_o"] = np.concatenate([-1.0 * upper_in, 1.0 * upper_in], 1)
    parts["mask_l"] = -1.0 * lower
    parts["chunk_of"] = (p[:, None] // CH == np.arange(CPT)[None, :])
    parts["eye_head"] = (p[:, None] % HD == np.arange(HD)[None, :])
    parts["scan_keep"] = np.broadcast_to(np.arange(T1) % CH != 0, (P, T1))
    first_only = len(parts)
    parts["iota"] = np.broadcast_to(np.arange(CAP_L), (P, CAP_L))
    rot = np.zeros((P, P))
    for m in range(P):
        first = (m % 32) < 16
        rot[m + 16 if first else m - 16, m] = -1.0 if first else 1.0
    parts["rot"] = rot
    n_freq = HD // 4
    inv = (f(10000.0) ** (-np.arange(n_freq, dtype=f) / f(n_freq))).astype(f)
    t = np.arange(SEQ)
    ang = np.zeros((P, SEQ), f)
    for m in range(P):
        pos = (t // GRID_W if (m % HD) < 32 else t % GRID_W).astype(f)
        ang[m] = pos * inv[m % 16]
    parts["cos"] = np.cos(ang)
    parts["sin"] = np.sin(ang)
    parts["flip"] = (p[:, None] // GRID_W == p[None, :] // GRID_W) & (p[:, None] % GRID_W + p[None, :] % GRID_W == GRID_W - 1)
    qc = p % GRID_W
    c0 = np.clip(qc - NA_COLS // 2, 0, GRID_W - NA_COLS)
    kc = np.arange(GRID_W)
    parts["col_mask"] = np.where((kc[None] >= c0[:, None]) & (kc[None] < c0[:, None] + NA_COLS), 0, NEG)
    both = ("ident", "ones", "fold")
    first = [n for i, n in enumerate(parts) if i < first_only and n not in both and not n.startswith("band")]
    second = [n for n in parts if n not in both and n not in first]
    packed = []
    for names in (both, first, second):
        at, n = {}, 0
        for name in names:
            at[name] = (n, parts[name].shape[1])
            n += parts[name].shape[1]
        packed.append((np.ascontiguousarray(np.concatenate([np.asarray(parts[x], f) for x in names], 1)), at))
    return packed


CONSTS = constants()

COLS1 = ["norm_mix_pre", "norm_ffn_pre", "lru_conv_w", "lru_conv_b", "lru_gate_a_b", "lru_gate_x_b",
         "lru_lambda", "rwkv_mu", "rwkv_w0", "rwkv_a0", "rwkv_k_k", "rwkv_k_a", "rwkv_r_k", "rwkv_ln_w",
         "rwkv_ln_b", "fox_f_bias", "w_f", "gate_a", "gate_x", "wa_up", "g_up", "ffn_conv"]
WIDTH1 = dict(norm_mix_pre=8, norm_ffn_pre=8, lru_conv_w=8, lru_conv_b=2, lru_gate_a_b=2, lru_gate_x_b=2,
              lru_lambda=2, rwkv_mu=8, rwkv_w0=2, rwkv_a0=2, rwkv_k_k=2, rwkv_k_a=2, rwkv_r_k=2,
              rwkv_ln_w=2, rwkv_ln_b=2, fox_f_bias=1, w_f=8 * FOX_HEADS, gate_a=256, gate_x=256,
              wa_up=256, g_up=256, ffn_conv=3 * 44)
COLS2 = ["conv_w", "conv_b", "ln_g", "ln_b", "router", "sink"]
WIDTH2 = dict(conv_w=2 * CW, conv_b=2, ln_g=2, ln_b=2, router=8 * N_EXP, sink=8)


def offsets(names, widths):
    at, n = {}, 0
    for name in names:
        at[name] = n
        n += widths[name]
    return at, n


AT1, NP1 = offsets(COLS1, WIDTH1)
AT2, NP2 = offsets(COLS2, WIDTH2)

N_IN, N_OUT, N_UP, N_DOWN = 12, 4, FT, FT // 2
N_MOD, N_IN2, N_OUT2 = 24, 8, 4
N_DELTA = 4
FIRST_CHUNKS = N_IN + N_OUT + N_UP + N_DOWN
LAYER_CHUNKS = N_IN2 + N_OUT2


class Signal:

    def __init__(self, sem):
        self.sem, self.base = sem, 0

    def of(self, n):
        return self.base + n

    def close(self, n):
        self.base += n


class Steps:

    def __init__(self, eng, sem):
        self.eng, self.sem, self.n = eng, sem, 0

    def __call__(self, ins):
        self.free(ins)
        self.join()

    def free(self, ins):
        ins.then_inc(self.sem, 1)
        self.n += 1

    def join(self):
        self.eng.wait_ge(self.sem, self.n)

    def tell(self, sem):
        self.join()
        self.eng.sem_inc(sem, 1)


class Stream:

    def __init__(self, ring, loaded, chunks, slots):
        self.ring, self.loaded, self.chunks, self.slots = ring, loaded, chunks, slots
        self.issued = self.taken = 0
        self.limit = len(chunks)
        self.ahead, self.loads = [], None
        self.freed_by = {}
        self.before, self.turn = [], []
        last = {}
        for n, s in enumerate(slots):
            self.before.append(last.get(s))
            self.turn.append(1 if s not in last else self.turn[last[s]] + 1)
            last[s] = n

    def take(self):
        self.taken += 1
        return self.taken - 1

    def slot(self, n):
        return self.ring[:, self.slots[n], :]

    def landed(self, n):
        return self.loaded[self.slots[n]], 16 * self.turn[n]

    def wait(self, eng, n):
        eng.wait_ge(*self.landed(n))

    def freed(self, n, sem, value):
        self.freed_by[n] = (sem, value)

    def issue(self, sp):
        for dst, src in self.ahead:
            sp.dma_start(dst, src).then_inc(self.loads, 16)
        self.ahead = []
        while self.issued < self.limit:
            n, before = self.issued, self.before[self.issued]
            if before is not None:
                if before not in self.freed_by:
                    break
                sp.wait_ge(*self.freed_by[before])
            sp.dma_start(self.slot(n), self.chunks[n]).then_inc(self.landed(n)[0], 16)
            self.issued += 1


class Kernel:
    pass


def split(off, width):
    out, at = [], 0
    while at < width:
        n = min(width - at, BANK - (off + at) % BANK)
        out.append((at, n))
        at += n
    return out


def products(k, groups, evacuate, beside=None):
    nc = k.nc
    ready, free_v, free_s = k.sig["product"], k.sig["taken_v"], k.sig["taken_s"]
    places = groups[0]["places"]

    def turn(i):
        return i // 2 + 1

    with nc.Block() as block:
        @block.tensor
        def _(pe):
            for i, g in enumerate(groups):
                for n in g.get("needs", ()):
                    k.stream.wait(pe, n)
                if i >= places:
                    before = i - places
                    free = free_v if before % 2 == 0 else free_s
                    pe.wait_ge(free.sem, free.of(turn(before)))
                for out, lhsT, rhs, start, stop in g.get("mm", ()):
                    mm = pe.matmul(out, lhsT, rhs, start=start, stop=stop, skip_group_check=True)
                for out, src, n in g.get("tr", ()):
                    mm = pe.transpose(out, src, k.c("ident")[0:n, 0:n])
                mm.then_inc(ready.sem, 1)
                for n in g.get("last", ()):
                    k.stream.freed(n, ready.sem, ready.of(i + 1))

        @block.vector
        def _(dve):
            steps = k.steps(dve, "v")
            if beside:
                beside[0](dve, steps)
            for i in range(0, len(groups), 2):
                dve.wait_ge(ready.sem, ready.of(i + 1))
                finish(steps, free_v.sem, evacuate(k, "v", i, steps))
            dve.wait_ge(free_v.sem, free_v.of((len(groups) + 1) // 2))

        @block.scalar
        def _(act):
            steps = k.steps(act, "s")
            if beside:
                beside[1](act, steps)
            for i in range(1, len(groups), 2):
                act.wait_ge(ready.sem, ready.of(i + 1))
                finish(steps, free_s.sem, evacuate(k, "s", i, steps))
            if len(groups) > 1:
                act.wait_ge(free_s.sem, free_s.of(len(groups) // 2))

        @block.sync
        def _(sp):
            k.stream.issue(sp)
    ready.close(len(groups))
    free_v.close((len(groups) + 1) // 2)
    free_s.close(len(groups) // 2)


def finish(steps, sem, made):
    if isinstance(made, list):
        for x in made:
            steps.free(x)
        steps.tell(sem)
    else:
        made.then_inc(sem, 1)


def copy_out(k, who, out, src, scale=None, bias=None):
    nc = k.nc
    if who == "v":
        if scale is None and bias is None:
            return nc.vector.tensor_copy(out, src)
        if bias is None:
            return nc.vector.tensor_scalar(out, src, scale, None, ALU.mult)
        if scale is None:
            return nc.vector.tensor_scalar(out, src, bias, None, ALU.add)
        return nc.vector.tensor_scalar(out, src, scale, bias, ALU.mult, ALU.add)
    kw = {}
    if scale is not None:
        kw["scale"] = scale
    if bias is not None:
        kw["bias"] = bias
    return nc.scalar.activation(out, src, ACT.Identity, **kw)


def load(k, pairs):
    loads = k.sig["load"]
    with k.nc.Block() as block:
        @block.sync
        def _(sp):
            for dst, src in pairs:
                sp.dma_start(dst, src).then_inc(loads.sem, 16)
            k.stream.issue(sp)
            sp.wait_ge(loads.sem, loads.of(16 * len(pairs)))
    loads.close(16 * len(pairs))


def arrive(k, n):
    loads = k.sig["load"]
    with k.nc.Block() as block:
        @block.sync
        def _(sp):
            sp.wait_ge(loads.sem, loads.of(16 * n))
    loads.close(16 * n)


def to_channels(k, tiles, dst, scale, bias=None):
    groups, todo = [], []
    for src, n, at, which in tiles:
        for c in range(0, KD, 4):
            bank = len(groups) % 8
            groups.append(dict(places=8, tr=[(k.ps[0:P, bank, j * P:j * P + n], src[:, (c + j) * P:(c + j + 1) * P], n)
                                             for j in range(4)]))
            todo.append((bank, c, n, at, which))

    def take(k, who, i, steps):
        bank, c, n, at, which = todo[i]
        return [copy_out(k, who, dst[:, c + j, at:at + n], k.ps[:, bank, j * P:j * P + n],
                         scale(which, c + j), bias(which, c + j) if bias else None) for j in range(4)]
    products(k, groups, take)


class Modulation:

    STEPS = N_MOD + 2

    def __init__(self, k, rows, l):
        self.k, self.l, self.step = k, l, 0
        self.rows = rows
        self.chunks = [k.stream.take() for _ in range(N_MOD)]

    def multiply(self, pe, j, bank):
        k = self.k
        mm = None
        if j >= 2:
            for b in range(2):
                mm = pe.matmul(bank[:, P + 2 * b:P + 2 * b + 2], self.rows[:, j % 2, b * P:(b + 1) * P], k.c("fold"),
                               start=True, stop=True, skip_group_check=True)
        if j < N_MOD:
            k.stream.wait(pe, self.chunks[j])
            w = k.stream.slot(self.chunks[j]).rearrange("p (k c) -> p k c", k=KD)
            for c_ in range(KD):
                q = 32 * (c_ % 4)
                mm = pe.matmul(bank[q:q + 32, 2 * P:4 * P], k.cond[:, c_, :], w[:, c_, :], start=c_ < 4, stop=c_ >= 4,
                               skip_group_check=True)
        return mm

    def freed(self, j, sem, value):
        if j < N_MOD:
            self.k.stream.freed(self.chunks[j], sem, value)

    def collect(self, dve, steps, j, bank):
        k = self.k
        if j >= 2:
            n = j - 2
            dst = k.mod[:, self.l, 2 * n:2 * n + 2, :]
            src = bank[:, P:P + 4].rearrange("p (c w) -> p c w", w=2)
            b = k.b_mod[:, self.l, 2 * n:2 * n + 2].unsqueeze(2).to_broadcast([P, 2, 2])
            if 2 * n // KD in (1, 4):
                steps.free(dve.scalar_tensor_tensor(dst, src, 1.0, b, ALU.add, ALU.add))
            else:
                steps.free(dve.tensor_tensor(dst, src, b, ALU.add))
        if j < N_MOD:
            steps.free(dve.tensor_copy(self.rows[:, j % 2, :], bank[:, 2 * P:4 * P]))


def attention(k, units, spare=None, modulation=None, extra=()):
    nc = k.nc
    sg = k.sig
    scores, maxed, exped, probs = sg["scores"], sg["row_max"], sg["exp"], sg["probs"]
    turned, pt_ready, out_ready, out_taken = sg["turned"], sg["pt"], sg["out"], sg["out_taken"]
    N = len(units)
    n_mod = Modulation.STEPS if modulation else 0
    assert N % 2 == 0 and n_mod <= N // 2
    with ExitStack() as ctx:
        sb = k.alloc(ctx)
        if spare is None:
            spare = sb("prob", [P, 2 * (T2 + 1)])
        prob = spare[:, 0:2 * (T2 + 1)].rearrange("p (a c) -> p a c", a=2)
        probT = sb("probT", [P, 4, 6, P])
        nmax = sb("nmax", [P, 4])
        rsum = sb("rsum", [P, 4])
        rinv = sb("rinv", [P, 4])
        S = [k.psf[:, 2 * BANK * s:2 * BANK * (s + 1)] for s in range(2)]
        T = k.psf[:, 4 * BANK:6 * BANK].rearrange("p (t q) -> p t q", q=P)
        O = [k.psf[:, (6 + s) * BANK:(7 + s) * BANK] for s in range(2)]

        def full(u):
            return u["width"] + (u["sink"] is not None)

        with nc.Block() as block:
            @block.tensor
            def _(pe):
                def score(i):
                    u, qn = units[i], units[i]["q"].shape[1]
                    if i >= 2:
                        pe.wait_ge(exped.sem, exped.of(i - 1))
                    for col, terms in u["scores"]:
                        n_col = terms[0][1].shape[1]
                        for at, n in split(col, n_col):
                            for t, (lhsT, rhs) in enumerate(terms):
                                mm = pe.matmul(S[i % 2][0:qn, col + at:col + at + n], lhsT, rhs[:, at:at + n],
                                               start=t == 0, stop=t == len(terms) - 1, skip_group_check=True)
                    mm.then_inc(scores.sem, 1)

                def turn(i):
                    u, qn = units[i], units[i]["q"].shape[1]
                    pe.wait_ge(probs.sem, probs.of(i + 1))
                    if i >= 1:
                        pe.wait_ge(pt_ready.sem, pt_ready.of(i))
                    for t, (v, kn, col) in enumerate(u["values"]):
                        mm = pe.transpose(T[0:kn, t, 0:qn], prob[0:qn, i % 2, col:col + kn], k.c("ident")[0:qn, 0:qn])
                    mm.then_inc(turned.sem, 1)

                def mix(m):
                    bank, pair = O[m % 2], units[2 * m:2 * m + 2]
                    if m >= 2:
                        pe.wait_ge(out_taken.sem, out_taken.of(m - 1))
                    if m < n_mod:
                        modulation.multiply(pe, m, bank)
                    pe.wait_ge(pt_ready.sem, pt_ready.of(2 * m + 2))
                    for t in range(len(pair[0]["values"])):
                        for half, u in enumerate(pair):
                            v, kn, col = u["values"][t]
                            qn = u["q"].shape[1]
                            mm = pe.matmul(bank[HD * half:HD * half + HD, 0:qn], v, probT[0:kn, (2 * m + half) % 4, t, 0:qn],
                                           start=t == 0, stop=t == len(u["values"]) - 1, skip_group_check=True)
                    mm.then_inc(out_ready.sem, 1)
                    if m < n_mod:
                        modulation.freed(m, out_ready.sem, out_ready.of(m + 1))

                for i in range(2):
                    score(i)
                for i in range(N):
                    turn(i)
                    if i + 2 < N:
                        score(i + 2)
                    if i % 2 == 1:
                        mix(i // 2)

            @block.vector
            def _(dve):
                steps = k.steps(dve, "v")

                def row_max(i):
                    u, qn = units[i], units[i]["q"].shape[1]
                    dve.wait_ge(scores.sem, scores.of(i + 1))
                    for col, mask in u["adds"]:
                        s = S[i % 2][0:qn, col:col + mask.shape[1]]
                        steps.free(dve.tensor_tensor(s, s, mask, ALU.subtract))
                    if u["sink"] is not None:
                        steps.free(dve.tensor_scalar(S[i % 2][0:qn, u["width"]:u["width"] + 1], u["sink"], -1.0, None,
                                                     ALU.mult))
                    steps.join()
                    dve.tensor_reduce(nmax[0:qn, i % 4:i % 4 + 1], S[i % 2][0:qn, 0:full(u)], AX.X,
                                      ALU.min).then_inc(maxed.sem, 1)

                def normalise(i):
                    u, qn = units[i], units[i]["q"].shape[1]
                    dve.wait_ge(exped.sem, exped.of(i + 1))
                    steps(dve.reciprocal(rinv[0:qn, i % 4:i % 4 + 1], rsum[0:qn, i % 4:i % 4 + 1]))
                    pr = prob[0:qn, i % 2, 0:u["width"]]
                    dve.tensor_scalar(pr, pr, rinv[0:qn, i % 4:i % 4 + 1], None, ALU.mult).then_inc(probs.sem, 1)

                def take(m):
                    u = units[2 * m]
                    dve.wait_ge(out_ready.sem, out_ready.of(m + 1))
                    steps.free(dve.tensor_copy(u["out"], O[m % 2][:, 0:u["q"].shape[1]]))
                    if m < n_mod:
                        modulation.collect(dve, steps, m, O[m % 2])
                    steps.tell(out_taken.sem)

                for i in range(2):
                    row_max(i)
                normalise(0)
                for i in range(N):
                    if i + 1 < N:
                        normalise(i + 1)
                    if i + 2 < N:
                        row_max(i + 2)
                    if i % 2 == 1:
                        take(i // 2)
                    for f in extra[len(extra) * i // N:len(extra) * (i + 1) // N]:
                        f(dve, steps)
                steps.join()

            @block.scalar
            def _(act):
                def exps(i):
                    u, qn = units[i], units[i]["q"].shape[1]
                    act.wait_ge(maxed.sem, maxed.of(i + 1))
                    if i >= 2:
                        act.wait_ge(turned.sem, turned.of(i - 1))
                    act.activation(prob[0:qn, i % 2, 0:full(u)], S[i % 2][0:qn, 0:full(u)], ACT.Exp,
                                   bias=nmax[0:qn, i % 4:i % 4 + 1], scale=-1.0,
                                   accum_out=rsum[0:qn, i % 4:i % 4 + 1]).then_inc(exped.sem, 1)

                steps = k.steps(act, "s")

                def copies(i):
                    u, qn = units[i], units[i]["q"].shape[1]
                    act.wait_ge(turned.sem, turned.of(i + 1))
                    if i >= 4:
                        act.wait_ge(out_ready.sem, out_ready.of(i // 2 - 1))
                    whole = sum(kn == P for _, kn, _ in u["values"])
                    rest = u["values"][whole:]
                    last = None
                    if whole:
                        last = act.copy(probT[:, i % 4, 0:whole, 0:qn], T[:, 0:whole, 0:qn])
                    if rest:
                        if whole:
                            steps(last)
                        kn = rest[0][1]
                        last = act.copy(probT[0:kn, i % 4, whole, 0:qn], T[0:kn, whole, 0:qn])
                    last.then_inc(pt_ready.sem, 1)

                for i in range(2):
                    exps(i)
                for i in range(N):
                    copies(i)
                    if i + 2 < N:
                        exps(i + 2)
                act.wait_ge(pt_ready.sem, pt_ready.of(N))

            @block.sync
            def _(sp):
                k.stream.issue(sp)
    for s in (scores, maxed, exped, probs, turned, pt_ready):
        s.close(N)
    for s in (out_ready, out_taken):
        s.close(N // 2)


def token_tiles(src_x, src_meta):
    return [(src_meta, N_META, 0, 0)] + [(src_x[:, j, :], P, N_META + P * j, 0) for j in range(NTL)]


def rms_scale(k, jobs):
    nc = k.nc
    squared, rooted, meant = k.sig["squared"], k.sig["rooted"], k.sig["meant"]
    with ExitStack() as ctx:
        sb = k.alloc(ctx)
        junk = sb("junk", [P, 2, D])
        ssq = sb("ssq", [P, 8])
        root = sb("root", [P, 8])
        with nc.Block() as block:
            @block.scalar
            def _(act):
                def root_of(i):
                    n = jobs[i][2]
                    act.wait_ge(meant.sem, meant.of(i + 1))
                    act.activation(root[0:n, i:i + 1], ssq[0:n, i:i + 1], ACT.Sqrt).then_inc(rooted.sem, 1)

                for i, (x, out, n, gain, res) in enumerate(jobs):
                    if i >= 2:
                        act.wait_ge(squared.sem, squared.of(i - 1))
                    act.activation(junk[0:n, i % 2, :], x, ACT.Square,
                                   accum_out=ssq[0:n, i:i + 1]).then_inc(squared.sem, 1)
                    if i >= 1:
                        root_of(i - 1)
                root_of(len(jobs) - 1)

            @block.vector
            def _(dve):
                steps = k.steps(dve, "v")
                def scale(i):
                    x, out, n, gain, res = jobs[i]
                    dve.wait_ge(rooted.sem, rooted.of(i + 1))
                    steps(dve.reciprocal(root[0:n, i:i + 1], root[0:n, i:i + 1]))
                    if gain is None:
                        steps.free(dve.tensor_scalar(out, x, root[0:n, i:i + 1], None, ALU.mult))
                    else:
                        steps(dve.scalar_tensor_tensor(out, x, root[0:n, i:i + 1], gain, ALU.mult, ALU.mult))
                        steps.free(dve.tensor_tensor(res, out, res, ALU.add))

                for i, (x, out, n, gain, res) in enumerate(jobs):
                    dve.wait_ge(squared.sem, squared.of(i + 1))
                    dve.tensor_scalar(ssq[0:n, i:i + 1], ssq[0:n, i:i + 1], 1.0 / D, RMS_EPS, ALU.mult,
                                      ALU.add).then_inc(meant.sem, 1)
                    if i >= 1:
                        scale(i - 1)
                scale(len(jobs) - 1)
                steps.join()

            @block.sync
            def _(sp):
                k.stream.issue(sp)
    for s in (squared, rooted, meant):
        s.close(len(jobs))


def project_channels(k, hT, tiles, take, beside=None):
    groups = []
    for i, (w, m, needs, last, *_) in enumerate(tiles):
        slot = i % 4
        mm = [(k.ps[0:m, 2 * slot + h, 0:HALF1], w(c), hT[:, c, h * HALF1:(h + 1) * HALF1], c == 0, c == KD - 1)
              for c in range(KD) for h in range(2)]
        groups.append(dict(places=4, mm=mm, needs=needs, last=last))

    def evacuate(k, who, i, steps):
        slot = i % 4
        m = tiles[i][1]
        return take(who, i, k.ps[0:m, 2 * slot:2 * slot + 2, 0:HALF1], steps)
    products(k, groups, evacuate, beside)


def halves(ap):
    return ap.rearrange("p (h t) -> p h t", h=2)


def first_block(k):
    nc = k.nc
    stream, c1 = k.stream, k.c1
    with ExitStack() as ctx:
        sb = k.alloc(ctx)
        hT = sb("hT", [P, KD, T1])
        OT = sb("OT", [P, 2, T1])
        xt = k.h1
        rms_scale(k, [(xt[0:N_META, NTL, :], xt[0:N_META, NTL, :], N_META, None, None)] +
                  [(xt[:, j, :], xt[:, j, :], P, None, None) for j in range(NTL)])
        to_channels(k, token_tiles(xt, xt[0:N_META, NTL, :]), hT, lambda w, c: c1("norm_mix_pre", c))
        delta_rule(k, hT, OT)
        k.stream.limit = k.moe_at[0] + RING
        mixT = sb("mixT", [P, 6, T1])
        with ExitStack() as scope:
            lru = Recurrence(k, k.alloc(scope), hT, mixT)
            forgetting(k, hT, mixT, lru)
        mix_out(k, sb, mixT, OT)
    feed_forward(k)


def column_chunk(k, n, j):
    s = k.stream.slot(n).rearrange("p (k c) -> p k c", k=KD)
    return lambda c: s[:, c, j * P:(j + 1) * P]


def column_tiles(k, count):
    out = []
    for _ in range(count):
        n = k.stream.take()
        out.append((column_chunk(k, n, 0), P, [n], []))
        out.append((column_chunk(k, n, 1), P, [], [n]))
    return out


def delta_rule(k, hT, OT):
    nc = k.nc
    c1, c = k.c1, k.c
    GT = [(0, 1), (2, 3), (4,)]
    with ExitStack() as ctx:
        sb = k.alloc(ctx)
        G = sb("G", [P, 2, T1])
        bonusT = sb("bonusT", [P, 2, T1])
        kap = sb("kap", [P, 2, T1])
        bet = sb("bet", [P, 2, T1])
        kti = sb("kti", [P, 2, T1])
        rho = sb("rho", [P, 2, T1])
        bend = sb("bend", [P, 2, T1])
        kend = sb("kend", [P, 2, T1])
        vv = sb("vv", [P, 2, T1])
        Wend = sb("Wend", [P, 2, NCH])
        with ExitStack() as inner:
            sbi = k.alloc(inner)
            pc = sbi("pc", [P, 8, T1 + 1])

            def take(who, i, src, steps):
                return copy_out(k, who, halves(pc[:, i, 1:T1 + 1]), src)
            with nc.Block() as block:
                @block.vector
                def _(dve):
                    steps = k.steps(dve, "v")
                    steps(dve.memset(pc[:, :, 0:1], 0.0))
            project_channels(k, hT, column_tiles(k, 4), take)
            rwkv_inputs(k, sbi, pc, G, bonusT, kap, bet, kti, rho, bend, kend, vv, Wend)
        with ExitStack() as inner:
            sbi = k.alloc(inner)
            X = sbi("X", [P, 2, HD])
            modulation = Modulation(k, k.h1[:, NT2 - 1, D // 2:D].rearrange("p (a c) -> p a c", a=2), 0)
            with nc.Block() as block:
                @block.vector
                def _(dve):
                    steps = k.steps(dve, "v")
                    steps(dve.memset(X[:, :, :], 0.0))

                @block.scalar
                def _(act):
                    steps = k.steps(act, "s")
                    steps(act.activation(k.cond[:, :, :], k.cond[:, :, :], ACT.Silu))
            for tiles in GT:
                with ExitStack() as scope:
                    chunk_group(k, k.alloc(scope), tiles, X, OT, kap, bet, kti, rho, bend, kend, vv, Wend, modulation)
        with ExitStack() as inner:
            group_norm(k, k.alloc(inner), OT, bonusT, G)


def rwkv_inputs(k, sb, pc, G, bonusT, kap, bet, kti, rho, bend, kend, vv, Wend):
    nc, c1, c = k.nc, k.c1, k.c
    t1 = sb("t1", [P, 8, T1])
    a = t1[:, 0:2, :]
    sg = t1[:, 2:4, :]
    kk = t1[:, 4:6, :]
    tmp = t1[:, 6:8, :]
    cum = sb("cum", [P, 2, T1])
    low, fine, fin2 = k.sig["low"], k.sig["fine"], k.sig["fin2"]
    r, kr, v = pc[:, 0:2, 1:], pc[:, 2:4, 1:], pc[:, 4:6, 1:]
    with nc.Block() as block:
        @block.vector
        def _(dve):
            steps = k.steps(dve, "v")
            steps(dve.tensor_tensor(t1[:, :, :], pc[:, :, 0:T1], pc[:, :, 1:T1 + 1], ALU.subtract))
            for i in range(8):
                x = pc[:, i, 1:T1 + 1]
                steps.free(dve.scalar_tensor_tensor(x, t1[:, i, :], c1("rwkv_mu", i), x, ALU.mult, ALU.add))
            steps.join()

        @block.sync
        def _(sp):
            k.stream.issue(sp)
    with nc.Block() as block:
        @block.scalar
        def _(act):
            steps = k.steps(act, "s")
            steps(act.activation(pc[0:HD, 6, 1:], pc[0:HD, 6, 1:], ACT.Tanh))
            steps(act.activation(pc[:, 7, 1:], pc[:, 7, 1:], ACT.Sigmoid))
    up = k.c1m("wa_up", 256)
    gu = k.c1m("g_up", 256)
    wt, at_, gt = pc[0:HD, 6, 1:], pc[HD:P, 6, 1:], pc[:, 7, 1:]
    groups, where = [], []
    for kind, (w, x, b) in enumerate(((up[0:HD], wt, 0), (up[HD:P], at_, 1), (gu, gt, 0))):
        for g in range(2):
            slot = len(groups) % 4
            groups.append(dict(places=4, mm=[(k.ps[:, 2 * slot + h, 0:HALF1], w[:, g * P:(g + 1) * P],
                                              x[:, h * HALF1:(h + 1) * HALF1], True, True) for h in range(2)]))
            where.append((kind, g))

    def take(k, who, i, steps):
        kind, g = where[i]
        src = k.ps[:, 2 * (i % 4):2 * (i % 4) + 2, 0:HALF1]
        dst = (sg, a, G)[kind][:, g, :]
        return copy_out(k, who, halves(dst), src)
    products(k, groups, take)
    with nc.Block() as block:
        @block.scalar
        def _(act):
            for g in range(2):
                act.activation(sg[:, g, :], sg[:, g, :], ACT.Sigmoid, bias=c1("rwkv_w0", g)).then_inc(low.sem, 1)
            for g in range(2):
                act.activation(a[:, g, :], a[:, g, :], ACT.Sigmoid, bias=c1("rwkv_a0", g)).then_inc(low.sem, 1)
            act.wait_ge(fine.sem, fine.of(1))
            act.activation(rho[:, :, :], cum[:, :, :], ACT.Exp, scale=-EXP_HALF).then_inc(fin2.sem, 1)
            act.activation(kti[:, :, :], cum[:, :, :], ACT.Exp, scale=EXP_HALF).then_inc(fin2.sem, 1)
            act.wait_ge(fine.sem, fine.of(3))
            act.activation(kap[:, :, :], sg[:, :, :], ACT.Exp, scale=-EXP_HALF).then_inc(fin2.sem, 1)
            act.activation(kend[:, :, :], bend[:, :, :], ACT.Exp, scale=-EXP_HALF).then_inc(fin2.sem, 1)
            act.wait_ge(fin2.sem, fin2.of(4))

        @block.vector
        def _(dve):
            steps = k.steps(dve, "v")
            dve.wait_ge(low.sem, low.of(2))
            for g in range(2):
                steps.free(dve.tensor_tensor_scan(cum[:, g, :], c("scan_keep"), sg[:, g, :], 0.0, ALU.mult, ALU.add))
            steps.tell(fine.sem)
            dve.tensor_tensor(sg[:, :, :], cum[:, :, :], sg[:, :, :], ALU.subtract).then_inc(fine.sem, 1)
            for g in range(2):
                e = cum[:, g, CH - 1:T1:CH].unsqueeze(2).to_broadcast([P, NCH, CH])
                x = dve.tensor_tensor(bend[:, g, :].rearrange("p (c t) -> p c t", t=CH), e,
                                      cum[:, g, :].rearrange("p (c t) -> p c t", t=CH), ALU.subtract)
                steps.free(x)
            steps.tell(fine.sem)
            for g in range(2):
                steps.free(dve.tensor_scalar(kk[:, g, :], kr[:, g, :], c1("rwkv_k_k", g), None, ALU.mult))
            steps.join()
            steps(dve.tensor_tensor(tmp[:, :, :], kk[:, :, :], kk[:, :, :], ALU.mult))
            dve.wait_ge(low.sem, low.of(4))
            dve.wait_ge(fin2.sem, fin2.of(4))
            steps(dve.tensor_copy(Wend[:, :, :], rho[:, :, CH - 1:T1:CH]))
    low.close(4)
    fine.close(3)
    fin2.close(4)

    def head_sums(src):
        groups = [dict(places=2, mm=[(k.ps[:, 2 * g + h, 0:HALF1], c("head_ones"),
                                      src[:, g, h * HALF1:(h + 1) * HALF1], True, True) for h in range(2)])
                  for g in range(2)]
        return groups

    norm = sb("norm", [P, 2, T1])

    def take_norm(k, who, i, steps):
        return copy_out(k, who, halves(norm[:, i, :]), k.ps[:, 2 * i:2 * i + 2, 0:HALF1])
    products(k, head_sums(tmp), take_norm)
    with nc.Block() as block:
        @block.scalar
        def _(act):
            act.activation(norm[:, :, :], norm[:, :, :], ACT.Sqrt).then_inc(low.sem, 1)

        @block.vector
        def _(dve):
            steps = k.steps(dve, "v")
            for g in range(2):
                steps(dve.tensor_scalar(tmp[:, g, :], a[:, g, :], -1.0, c1("rwkv_k_a", g), ALU.add, ALU.mult))
                steps.free(dve.scalar_tensor_tensor(kr[:, g, :], tmp[:, g, :], 1.0, kr[:, g, :], ALU.add, ALU.mult))
            dve.wait_ge(low.sem, low.of(1))
            steps.join()
            steps(dve.tensor_scalar(norm[:, :, :], norm[:, :, :], 1e-12, None, ALU.max))
            steps(dve.reciprocal(norm[:, :, :], norm[:, :, :]))
            steps(dve.tensor_tensor(kk[:, :, :], kk[:, :, :], norm[:, :, :], ALU.mult))
            steps(dve.tensor_tensor(a[:, :, :], kk[:, :, :], a[:, :, :], ALU.mult))
            steps.free(dve.tensor_tensor(kap[:, :, :], kap[:, :, :], kk[:, :, :], ALU.mult))
            steps.free(dve.tensor_tensor(bet[:, :, :], kti[:, :, :], a[:, :, :], ALU.mult))
            steps.free(dve.tensor_tensor(bend[:, :, :], kend[:, :, :], a[:, :, :], ALU.mult))
            steps.join()
            steps.free(dve.tensor_tensor(kti[:, :, :], kti[:, :, :], kr, ALU.mult))
            steps.free(dve.tensor_tensor(kend[:, :, :], kend[:, :, :], kr, ALU.mult))
            steps.free(dve.tensor_tensor(rho[:, :, :], rho[:, :, :], r, ALU.mult))
            for g in range(2):
                steps.free(dve.scalar_tensor_tensor(tmp[:, g, :], r[:, g, :], c1("rwkv_r_k", g), kr[:, g, :],
                                                    ALU.mult, ALU.mult))
            steps.free(dve.tensor_copy(vv[:, :, :], v))
            steps.join()
    low.close(1)

    def take_bonus(k, who, i, steps):
        return copy_out(k, who, halves(bonusT[:, i, :]), k.ps[:, 2 * i:2 * i + 2, 0:HALF1])
    products(k, head_sums(tmp), take_bonus)
    with nc.Block() as block:
        @block.vector
        def _(dve):
            steps = k.steps(dve, "v")
            steps(dve.tensor_tensor(bonusT[:, :, :], bonusT[:, :, :], vv[:, :, :], ALU.mult))


def chunk_group(k, sb, tiles, X, OT, kap, bet, kti, rho, bend, kend, vv, Wend, modulation):
    nc, c = k.nc, k.c
    ps = k.ps
    n_t = len(tiles)
    ns = [P if t < NTL else N_META for t in tiles]
    H = RW_HEADS
    mats = k.h1[:, :, :].rearrange("p a c -> p (a c)")[:, 0:n_t * 5 * H * P].rearrange(
        "p (n a h t) -> p n a h t", n=n_t, a=5, h=H)
    pw = sb("pw", [P, n_t, 3, H, P])
    tok = sb("tok", [P, n_t, 4, RW])
    tk = sb("tk", [P, n_t, 3, RW])
    spare = k.stream.ring[:, RING // 2:RING, :].rearrange("p s c -> p (s c)")
    n_ex, n_a = 3 * CPT * RW, n_t * 2 * CPT * HD
    ex = spare[:, 0:n_ex].rearrange("p (a c h) -> p a c h", a=3, c=CPT)
    aT = spare[:, n_ex:n_ex + n_a].rearrange("p (n g c j) -> p n g c j", n=n_t, g=2, c=CPT)
    gT = sb("gT", [P, n_t, 2, P])
    hT_ = sb("hT_", [P, n_t, 2, P])
    fT = sb("fT", [P, n_t, 2, CPT, HD])
    xs = sb("xs", [P, 2, n_t * CPT + 1, HD])
    made, moved, multiplied = k.sig["made"], k.sig["moved"], k.sig["multiplied"]

    def ts(t):
        return slice(P * t, P * t + (P if t < NTL else N_META))

    def steps_of(it):
        t, n = tiles[it], ns[it]
        m, q, tkn, w = mats[:, it], pw[:, it], tok[:, it], tk[:, it]
        b0 = 4 * (it % 2)
        nc_ = n // CH

        def hp(x, g, p):
            return x[HD * p:HD * p + HD, g, ts(t)]

        out = []

        def pe1(pe):
            for a, src in enumerate((kap, bend, kend, vv)):
                for g in range(2):
                    mm = pe.transpose(ps[0:n, b0 + a // 2, (a % 2) * RW + g * P:(a % 2) * RW + g * P + P], src[:, g, ts(t)],
                                      c("ident"))
            return mm

        def dv1(dve):
            return [dve.tensor_copy(tkn[0:n, 0:2, :], ps[0:n, b0, :].rearrange("p (a c) -> p a c", a=2)),
                    dve.tensor_copy(tkn[0:n, 2:4, :], ps[0:n, b0 + 1, :].rearrange("p (a c) -> p a c", a=2))]
        out.append((pe1, dv1))

        def grams(kinds):
            def pe2(pe):
                for a, (l, r) in enumerate(kinds):
                    for p in range(2):
                        for g in range(2):
                            col = ((a % 2) * 2 + g) * P
                            mm = pe.matmul(ps[0:n, b0 + 2 * (a // 2) + p, col:col + n], hp(l, g, p), hp(r, g, p), start=True, stop=True,
                                           skip_group_check=True)
                return mm
            return pe2

        def masked(mask, dsts, bank):
            def f(dve):
                res = []
                for a, dst in enumerate(dsts):
                    for p in range(2):
                        src = ps[0:n, b0 + bank + p, a * 256:(a + 1) * 256].rearrange("p (g t) -> p g t", g=2)[:, :, 0:n]
                        mk = c(mask)[0:n, a * P:a * P + n].unsqueeze(1).to_broadcast([n, 2, n])
                        res.append(dve.tensor_tensor(m[0:n, dst, 2 * p:2 * p + 2, 0:n], src, mk, ALU.mult))
                return res
            return f
        out.append((grams(((bet, kap), (kti, kap), (bet, rho), (kti, rho))),
                    lambda dve: masked("mask_u", (0, 2), 0)(dve) + masked("mask_o", (3, 4), 2)(dve)))
        out.append((grams(((kap, bet),)), masked("mask_l", (1,), 0)))

        def mm4(dst_bank, lhs, rhs):
            def f(pe):
                for h in range(H):
                    mm = pe.matmul(ps[0:n, b0 + dst_bank, h * P:h * P + n], lhs[0:n, h, 0:n], rhs[0:n, h, 0:n], start=True, stop=True,
                                   skip_group_check=True)
                return mm
            return f

        def both(*fs):
            def f(e):
                for x in fs:
                    r = x(e)
                return r
            return f

        def bank4(bank):
            return ps[0:n, b0 + bank, :].rearrange("p (h t) -> p h t", h=H)[:, :, 0:n]
        U, UT, U2, U2T, R = m[:, 0], m[:, 1], q[:, 0], q[:, 1], q[:, 2]
        eye = c("ident")[0:n, 0:n].unsqueeze(1).to_broadcast([n, H, n])
        v = lambda x: x[0:n, :, 0:n]
        out.append((both(mm4(0, UT, U), mm4(1, U, UT)),
                    lambda dve: [dve.tensor_copy(v(U2), bank4(0)), dve.tensor_copy(v(U2T), bank4(1)),
                                 dve.tensor_tensor(v(R), v(U), eye, ALU.add)]))
        out.append((both(mm4(0, U2T, R), mm4(1, U2T, U2), mm4(2, U2, U2T)),
                    lambda dve: [dve.tensor_tensor(v(R), bank4(0), v(R), ALU.add), dve.tensor_copy(v(U), bank4(1)),
                                 dve.tensor_copy(v(UT), bank4(2))]))
        out.append((both(mm4(0, UT, R), mm4(1, U, UT)),
                    lambda dve: [dve.tensor_tensor(v(R), bank4(0), v(R), ALU.add), dve.tensor_copy(v(U2T), bank4(1))]))

        def head_cols(p, g):
            return slice(g * P + p * HD, g * P + p * HD + HD)

        def by_head(bank, col, lhs, rhs, a):
            def f(pe):
                for p in range(2):
                    for g in range(2):
                        s = head_cols(p, g)
                        mm = pe.matmul(ps[0:n, b0 + bank, col + s.start:col + s.stop], lhs[0:n, 2 * p + g, 0:n], rhs[0:n, a, s],
                                       start=True, stop=True, skip_group_check=True)
                return mm
            return f
        out.append((both(mm4(0, U2T, R), by_head(1, 0, m[:, 2], tkn, 3)),
                    lambda dve: [dve.tensor_tensor(v(R), bank4(0), v(R), ALU.add),
                                 dve.tensor_copy(w[0:n, 2, :], ps[0:n, b0 + 1, 0:RW])]))
        out.append((both(by_head(0, 0, R, tkn, 0), by_head(0, RW, R, w, 2)),
                    lambda dve: [dve.tensor_copy(w[0:n, 0:2, :], ps[0:n, b0, :].rearrange("p (a c) -> p a c", a=2))]))

        def pe9(pe):
            for g in range(2):
                for p in range(2):
                    s, h = head_cols(p, g), 2 * p + g
                    o = ps[HD * p:HD * p + HD, b0, g * P:g * P + n]
                    pe.matmul(o, w[0:n, 0, s], m[0:n, 3, h, 0:n], start=True, stop=True, skip_group_check=True)
                    o = ps[HD * p:HD * p + HD, b0 + 1, g * P:g * P + n]
                    pe.matmul(o, tkn[0:n, 3, s], m[0:n, 4, h, 0:n], start=True, stop=False, skip_group_check=True)
                    mm = pe.matmul(o, w[0:n, 1, s], m[0:n, 3, h, 0:n], start=False, stop=True, skip_group_check=True)
            return mm

        def dv9(dve):
            x = lambda bank: ps[:, b0 + bank, 0:2 * P].rearrange("p (g t) -> p g t", g=2)[:, :, 0:n]
            res = [dve.tensor_tensor(gT[:, it, :, 0:n], x(0), rho[:, :, ts(t)], ALU.add),
                   dve.tensor_copy(hT_[:, it, :, 0:n], x(1))]
            for a, src in enumerate((tkn[0:n, 1, :], tkn[0:n, 3, :], w[0:n, 1, :])):
                for ch in range(nc_):
                    col = c("chunk_of")[0:n, ch:ch + 1]
                    if a < 2:
                        res.append(dve.tensor_scalar(ex[0:n, a, ch, :], src, col, None, ALU.mult))
                    else:
                        res.append(dve.tensor_scalar(ex[0:n, a, ch, :], src, col, -1.0, ALU.mult, ALU.mult))
            return res
        out.append((pe9, dv9))

        def pe10(pe):
            for g in range(2):
                for p in range(2):
                    s = head_cols(p, g)
                    o = ps[HD * p:HD * p + HD, b0 + g, 0:nc_ * HD]
                    pe.matmul(o, w[0:n, 0, s], ex[0:n, 0, 0:nc_, s], start=True, stop=True, skip_group_check=True)
                    o = ps[HD * p:HD * p + HD, b0 + 2 + g, 0:nc_ * HD]
                    pe.matmul(o, tkn[0:n, 2, s], ex[0:n, 1, 0:nc_, s], start=True, stop=False, skip_group_check=True)
                    mm = pe.matmul(o, tkn[0:n, 1, s], ex[0:n, 2, 0:nc_, s], start=False, stop=True, skip_group_check=True)
            return mm

        def dv10(dve):
            steps = k.v_steps
            res = []
            for g in range(2):
                d_ = Wend[:, g, CPT * t:CPT * t + nc_].unsqueeze(2).to_broadcast([P, nc_, HD])
                e_ = c("eye_head").unsqueeze(1).to_broadcast([P, nc_, HD])
                steps(dve.tensor_tensor(aT[:, it, g, 0:nc_, :], d_, e_, ALU.mult))
                x = lambda bank: ps[:, b0 + bank, 0:nc_ * HD].rearrange("p (c j) -> p c j", j=HD)
                res.append(dve.tensor_tensor(aT[:, it, g, 0:nc_, :], aT[:, it, g, 0:nc_, :], x(g), ALU.subtract))
                steps.free(res.pop())
                res.append(dve.tensor_copy(fT[:, it, g, 0:nc_, :], x(2 + g)))
                steps.free(res.pop())
            return res
        out.append((pe10, dv10))
        return out

    lists = [steps_of(it) for it in range(n_t)]
    n_steps = len(lists[0])
    order = [(s, it) for s in range(n_steps - 2) for it in range(n_t)]
    order += [(s, it) for it in range(n_t) for s in (n_steps - 2, n_steps - 1)]
    at = {x: i + 1 for i, x in enumerate(order)}
    with nc.Block() as block:
        @block.tensor
        def _(pe):
            for s, it in order:
                if s >= 1:
                    pe.wait_ge(moved.sem, moved.of(at[s - 1, it]))
                lists[it][s][0](pe).then_inc(made.sem, 1)

        @block.vector
        def _(dve):
            steps = k.steps(dve, "v")
            k.v_steps = steps
            for s, it in order:
                dve.wait_ge(made.sem, made.of(at[s, it]))
                for x in lists[it][s][1](dve):
                    steps.free(x)
                steps.tell(moved.sem)
    made.close(n_t * n_steps)
    moved.close(n_t * n_steps)

    chunks = [(it, ch) for it in range(n_t) for ch in range(ns[it] // CH)]
    first = modulation.step
    n_mod = min(len(chunks) - 1, (Modulation.STEPS + 1) // 2, Modulation.STEPS - first)
    modulation.step += n_mod
    with nc.Block() as block:
        @block.tensor
        def _(pe):
            for i, (it, ch) in enumerate(chunks):
                pe.wait_ge(moved.sem, moved.of(i + 1))
                for p in range(2):
                    for g in range(2):
                        b = slice(HD * p, HD * p + HD)
                        mm = pe.matmul(ps[b, 2 * (i % 2) + p, g * HD:(g + 1) * HD], aT[b, it, g, ch, :], xs[b, g, i, :],
                                       start=True, stop=True, skip_group_check=True)
                mm.then_inc(made.sem, 1)
                if i < n_mod:
                    modulation.multiply(pe, first + i, ps[:, 4 + i % 2, :]).then_inc(multiplied.sem, 1)
                    modulation.freed(first + i, multiplied.sem, multiplied.of(i + 1))

        @block.sync
        def _(sp):
            k.stream.issue(sp)

        @block.vector
        def _(dve):
            steps = k.steps(dve, "v")
            dve.tensor_copy(xs[:, :, 0, :], X[:, :, :]).then_inc(moved.sem, 1)
            for i, (it, ch) in enumerate(chunks):
                dve.wait_ge(made.sem, made.of(i + 1))
                for p in range(2):
                    b = slice(HD * p, HD * p + HD)
                    x = dve.tensor_tensor(xs[b, :, i + 1, :],
                                          ps[b, 2 * (i % 2) + p, 0:2 * HD].rearrange("p (g j) -> p g j", g=2),
                                          fT[b, it, :, ch, :], ALU.add)
                    steps.free(x)
                if 1 <= i <= n_mod:
                    dve.wait_ge(multiplied.sem, multiplied.of(i))
                    modulation.collect(dve, steps, first + i - 1, ps[:, 4 + (i - 1) % 2, :])
                steps.tell(moved.sem)
            dve.wait_ge(moved.sem, moved.of(len(chunks) + 1))
            steps(dve.tensor_copy(X[:, :, :], xs[:, :, len(chunks), :]))
    made.close(len(chunks))
    multiplied.close(n_mod)
    moved.close(len(chunks) + 1)

    with nc.Block() as block:
        @block.tensor
        def _(pe):
            for i, (it, ch) in enumerate(chunks):
                for p in range(2):
                    for g in range(2):
                        b = slice(HD * p, HD * p + HD)
                        mm = pe.matmul(ps[b, 2 * it + p, g * P + ch * CH:g * P + ch * CH + CH], xs[b, g, i, :],
                                       gT[b, it, g, ch * CH:ch * CH + CH], start=True, stop=True, skip_group_check=True)
            mm.then_inc(made.sem, 1)

        @block.vector
        def _(dve):
            steps = k.steps(dve, "v")
            dve.wait_ge(made.sem, made.of(1))
            for it in range(n_t):
                for p in range(2):
                    b = slice(HD * p, HD * p + HD)
                    n = ns[it]
                    x = ps[b, 2 * it + p, 0:2 * P].rearrange("p (g t) -> p g t", g=2)[:, :, 0:n]
                    steps.free(dve.tensor_tensor(OT[b, :, ts(tiles[it])], x, hT_[b, it, :, 0:n], ALU.add))
            steps.join()
    made.close(1)


def group_norm(k, sb, OT, bonusT, G):
    nc, c, c1 = k.nc, k.c, k.c1
    sq = sb("sq", [P, 2, T1])
    low = k.sig["low"]

    def means(src):
        return [dict(places=2, mm=[(k.ps[:, 2 * g + h, 0:HALF1], c("head_ones"), src[:, g, h * HALF1:(h + 1) * HALF1],
                                    True, True) for h in range(2)]) for g in range(2)]

    def take(k, who, i, steps):
        return copy_out(k, who, halves(sq[:, i, :]), k.ps[:, 2 * i:2 * i + 2, 0:HALF1], 1.0 / HD)
    products(k, means(OT), take)
    with nc.Block() as block:
        @block.vector
        def _(dve):
            steps = k.steps(dve, "v")
            steps(dve.tensor_tensor(OT[:, :, :], OT[:, :, :], sq[:, :, :], ALU.subtract))
            steps(dve.tensor_tensor(sq[:, :, :], OT[:, :, :], OT[:, :, :], ALU.mult))
    products(k, means(sq), take)
    with nc.Block() as block:
        @block.vector
        def _(dve):
            steps = k.steps(dve, "v")
            dve.tensor_scalar(sq[:, :, :], sq[:, :, :], GN_EPS, None, ALU.add).then_inc(low.sem, 1)
            dve.wait_ge(low.sem, low.of(2))
            steps(dve.reciprocal(sq[:, :, :], sq[:, :, :]))
            steps(dve.tensor_tensor(OT[:, :, :], OT[:, :, :], sq[:, :, :], ALU.mult))
            for g in range(2):
                steps(dve.scalar_tensor_tensor(OT[:, g, :], OT[:, g, :], c1("rwkv_ln_w", g), bonusT[:, g, :],
                                               ALU.mult, ALU.add))
                steps(dve.scalar_tensor_tensor(OT[:, g, :], OT[:, g, :], c1("rwkv_ln_b", g), G[:, g, :],
                                               ALU.add, ALU.mult))

        @block.scalar
        def _(act):
            act.wait_ge(low.sem, low.of(1))
            act.activation(sq[:, :, :], sq[:, :, :], ACT.Sqrt).then_inc(low.sem, 1)
    low.close(2)


class Recurrence:

    PAD = 3

    def __init__(self, k, sb, hT, mixT):
        self.k, self.mixT = k, mixT
        flat = k.h1[:, :, :].rearrange("p t d -> p (t d)")
        parts = [flat[:, 2 * T1 * i:2 * T1 * (i + 1)].rearrange("p (g t) -> p g t", g=2) for i in range(4)]
        self.ya, self.u, self.rg, self.ig = parts
        n = 2 * (T1 + self.PAD)
        self.xa = flat[:, 8 * T1:8 * T1 + n].rearrange("p (g t) -> p g t", g=2)
        xa, ya = self.xa, self.ya
        self.w = sb("w", [P, 2, T1])
        self.softplus = sb("softplus", [P, 4, 2])

        def take(who, i, src, steps):
            dst = xa[:, i, self.PAD:] if i < 2 else ya[:, i - 2, :]
            return copy_out(k, who, halves(dst), src)

        def zeros(dve, steps):
            steps(dve.memset(xa[:, :, 0:self.PAD], 0.0))
        project_channels(k, hT, column_tiles(k, 2), take, (zeros, lambda act, steps: None))

    def prepare(self):
        k, c1, u, ya, sp_ = self.k, self.k.c1, self.u, self.ya, self.softplus
        low = k.sig["low"]

        def vector(dve, steps):
            for tap in range(4):
                for g in range(2):
                    x = self.xa[:, g, tap:tap + T1]
                    cw = c1("lru_conv_w", 2 * tap + g)
                    if tap == 0:
                        steps.free(dve.tensor_scalar(u[:, g, :], x, cw, c1("lru_conv_b", g), ALU.mult, ALU.add))
                    else:
                        steps.free(dve.scalar_tensor_tensor(u[:, g, :], x, cw, u[:, g, :], ALU.mult, ALU.add))
                steps.join()
            dve.wait_ge(low.sem, low.of(1))
            log1p_fix(dve, steps, sp_[:, 0, :], sp_[:, 1, :], sp_[:, 2, :], sp_[:, 3, :])
            steps(dve.tensor_scalar(sp_[:, 2, :], sp_[:, 2, :], 8.0, None, ALU.mult))

        def scalar(act, steps):
            steps(act.activation(sp_[:, 0, :], c1("lru_lambda", 0, 2), ACT.Exp, scale=-1.0))
            steps(act.activation(sp_[:, 1, :], sp_[:, 0, :], ACT.Identity, bias=k.one))
            steps.free(act.activation(sp_[:, 2, :], sp_[:, 1, :], ACT.Ln))
            steps.tell(low.sem)
            for g in range(2):
                steps.free(act.activation(ya[:, g, :], ya[:, g, :], ACT.Gelu_apprx_tanh))
            steps.join()
        return vector, scalar

    def gates(self):
        k, u = self.k, self.u
        groups = []
        for name in ("gate_a", "gate_x"):
            for g in range(2):
                i = len(groups)
                groups.append(dict(places=4, mm=[(k.ps[:, 2 * i + h, 0:HALF1], k.c1m(name, 256)[:, g * P:(g + 1) * P],
                                                  u[:, g, h * HALF1:(h + 1) * HALF1], True, True) for h in range(2)]))

        def take(k, who, i, steps):
            dst = (self.rg if i < 2 else self.ig)[:, i % 2, :]
            return copy_out(k, who, halves(dst), k.ps[:, 2 * i:2 * i + 2, 0:HALF1])
        products(k, groups, take)

    def finish(self):
        k, c1, u, rg, ig, w, sp_ = self.k, self.k.c1, self.u, self.rg, self.ig, self.w, self.softplus
        low, fine = k.sig["low"], k.sig["fine"]

        def scalar(act, steps):
            for g in range(2):
                steps.free(act.activation(rg[:, g, :], rg[:, g, :], ACT.Sigmoid, bias=c1("lru_gate_a_b", g)))
                steps.free(act.activation(ig[:, g, :], ig[:, g, :], ACT.Sigmoid, bias=c1("lru_gate_x_b", g)))
            steps.tell(low.sem)
            act.wait_ge(fine.sem, fine.of(1))
            steps.free(act.activation(w[:, :, :], rg[:, :, :], ACT.Tanh))
            steps.tell(low.sem)
            steps(act.activation(rg[:, :, :], rg[:, :, :], ACT.Exp, scale=-1.0))
            act.wait_ge(fine.sem, fine.of(2))
            steps.free(act.activation(w[:, :, :], w[:, :, :], ACT.Sqrt))
            steps.tell(low.sem)

        def vector(dve, steps):
            dve.wait_ge(low.sem, low.of(1))
            for g in range(2):
                steps.free(dve.tensor_scalar(rg[:, g, :], rg[:, g, :], sp_[:, 2, g:g + 1], None, ALU.mult))
            steps.tell(fine.sem)
            steps(dve.tensor_tensor(u[:, :, :], ig[:, :, :], u[:, :, :], ALU.mult))
            dve.wait_ge(low.sem, low.of(2))
            steps(dve.tensor_scalar(ig[:, :, :], w[:, :, :], 1.0, None, ALU.add))
            steps(dve.reciprocal(ig[:, :, :], ig[:, :, :]))
            steps.free(dve.scalar_tensor_tensor(w[:, :, :], w[:, :, :], 2.0, ig[:, :, :], ALU.mult, ALU.mult))
            steps.tell(fine.sem)
            dve.wait_ge(low.sem, low.of(3))
            steps(dve.tensor_tensor(u[:, :, :], u[:, :, :], w[:, :, :], ALU.mult))
            for g in range(2):
                steps.free(dve.tensor_tensor_scan(w[:, g, :], rg[:, g, :], u[:, g, :], 0.0, ALU.mult, ALU.add))
            steps.join()
            steps(dve.tensor_tensor(self.mixT[:, 0:2, :], w[:, :, :], self.ya[:, :, :], ALU.mult))
        return vector, scalar


def log1p_fix(dve, steps, z, w, lnw, tmp):
    steps(dve.tensor_scalar(tmp, w, -1.0, None, ALU.add))
    steps(dve.tensor_tensor(tmp, z, tmp, ALU.subtract))
    steps(dve.reciprocal(w, w))
    steps(dve.tensor_tensor(tmp, tmp, w, ALU.mult))
    steps(dve.tensor_tensor(lnw, lnw, tmp, ALU.add))


def forgetting(k, hT, mixT, lru):
    nc, c1, c = k.nc, k.c1, k.c
    with ExitStack() as ctx:
        sb = k.alloc(ctx)
        qT = sb("qT", [P, 4, T1])
        kT = sb("kT", [P, 4, T1])
        v = sb("v", [P, 5, FOX_W])
        fl = sb("fl", [FOX_HEADS, 5, T1])

        def take(who, i, src, steps):
            if i < 4:
                return copy_out(k, who, halves(qT[:, i, :]), src, -HD ** -0.5)
            if i < 8:
                return copy_out(k, who, halves(kT[:, i - 4, :]), src)
            return copy_out(k, who, halves(fl[:, 0, :]), src)
        tiles = column_tiles(k, 4)
        wf = k.c1m("w_f", 8 * FOX_HEADS).rearrange("p (k h) -> p k h", k=KD)
        tiles.append((lambda c_: wf[:, c_, :], FOX_HEADS, [], []))
        project_channels(k, hT, tiles, take, lru.prepare())
        low, fine = k.sig["low"], k.sig["fine"]
        low.close(1)
        lru.gates()
        groups, where = [], []
        for half in range(2):
            n = k.stream.take()
            s = k.stream.slot(n).rearrange("p (k c) -> p k c", k=KD)
            for t in range(5):
                m = P if t < NTL else N_META
                i = len(groups)
                groups.append(dict(places=8, needs=[n] if t == 0 else [], last=[n] if t == 4 else [],
                                   mm=[(k.ps[0:m, i % 8, 0:256], hT[:, c_, P * t:P * t + m], s[:, c_, :], c_ == 0, c_ == KD - 1)
                                       for c_ in range(KD)]))
                where.append((t, half, m))

        def take_v(k, who, i, steps):
            t, half, m = where[i]
            return copy_out(k, who, v[0:m, t, half * 256:half * 256 + 256], k.ps[0:m, i % 8, 0:256])
        lru_vector, lru_scalar = lru.finish()

        def vector(dve, steps):
            lru_vector(dve, steps)
            x = fl[:, 0, :]
            steps(dve.tensor_scalar(x, x, c1("fox_f_bias", 0)[0:FOX_HEADS], None, ALU.add))
            steps(dve.tensor_scalar(fl[:, 1, :], x, -1.0, None, ALU.mult))
            steps.free(dve.tensor_tensor(fl[:, 1, :], fl[:, 1, :], x, ALU.min))
            steps.tell(low.sem)
            steps.free(dve.tensor_scalar(x, x, 0.0, None, ALU.min))
            dve.wait_ge(fine.sem, fine.of(3))
            log1p_fix(dve, steps, fl[:, 1, :], fl[:, 2, :], fl[:, 3, :], fl[:, 4, :])
            steps(dve.tensor_tensor(x, x, fl[:, 3, :], ALU.subtract))
            steps(dve.memset(fl[:, 2, :], 1.0))
            steps(dve.tensor_tensor_scan(fl[:, 1, :], fl[:, 2, :], x, 0.0, ALU.mult, ALU.add))

        def scalar(act, steps):
            lru_scalar(act, steps)
            act.wait_ge(low.sem, low.of(4))
            steps(act.activation(fl[:, 1, :], fl[:, 1, :], ACT.Exp))
            steps(act.activation(fl[:, 2, :], fl[:, 1, :], ACT.Identity, bias=k.one[0:FOX_HEADS]))
            steps.free(act.activation(fl[:, 3, :], fl[:, 2, :], ACT.Ln))
            steps.tell(fine.sem)
        products(k, groups, take_v, (vector, scalar))
        low.close(4)
        fine.close(3)
        units = []
        for t in range(5):
            n = P if t < NTL else N_META
            width = P * t + n
            for h in range(FOX_HEADS):
                b = slice(HD * (h % 2), HD * (h % 2) + HD)
                q = qT[b, h // 2, P * t:P * t + n]
                sel = c("ident")[0:FOX_HEADS, h:h + 1].to_broadcast([FOX_HEADS, n])
                units.append(dict(q=q, width=width, sink=None,
                                  scores=[(0, [(q, kT[b, h // 2, 0:width]), (sel, fl[:, 1, 0:width])])],
                                  adds=[(P * t, c("causal")[0:n, 0:n])],
                                  values=[(v[0:(P if s < NTL else N_META), s, HD * h:HD * h + HD],
                                           P if s < NTL else N_META, P * s) for s in range(t + 1)],
                                  out=mixT[:, 2 + h // 2, P * t:P * t + n]))
        attention(k, units)


def mix_out(k, sb, mixT, OT):
    nc = k.nc
    y = k.h1
    lhs = lambda c_, at, n: (mixT[:, c_, at:at + n] if c_ < 6 else OT[:, c_ - 6, at:at + n])
    tiles = [(N_META + P * j, P, j) for j in range(NTL)] + [(0, N_META, NTL)]
    groups, where = [], []
    for half in range(2):
        a, b = k.stream.take(), k.stream.take()
        s = [k.stream.slot(x).rearrange("p (k c) -> p k c", k=4) for x in (a, b)]
        for at, n, j in tiles:
            i = len(groups)
            groups.append(dict(places=8, needs=[a, b] if j == 0 else [], last=[a, b] if j == NTL else [],
                               mm=[(k.ps[0:n, i % 8, :], lhs(c_, at, n), s[c_ // 4][:, c_ % 4, :], c_ == 0, c_ == KD - 1)
                                   for c_ in range(KD)]))
            where.append((j, n, half))
    mo = sb("mo", [P, 5, D])

    def take(k, who, i, steps):
        j, n, half = where[i]
        return copy_out(k, who, mo[0:n, j, half * BANK:(half + 1) * BANK], k.ps[0:n, i % 8, :])
    row = sb("row", [P, D])
    k.stream.ahead = [(row[:, :], k.dram["rows1"][0].partition_broadcast(P)), (y[:, 0:NTL, :], k.dram["x"]),
                      (y[0:N_META, NTL, :], k.dram["meta"])]
    products(k, groups, take)
    arrive(k, 3)
    rms_scale(k, [(mo[0:n, j, :], mo[0:n, j, :], n, row[0:n, :], y[0:n, j, :]) for _, n, j in tiles])


def feed_forward(k):
    nc, c1 = k.nc, k.c1
    y = k.h1
    with ExitStack() as ctx:
        sb = k.alloc(ctx)
        actT = sb("actT", [P, FT, SEQ])
        with ExitStack() as inner:
            sbi = k.alloc(inner)
            hT = sbi("hT2", [P, KD, T1])
            with ExitStack() as i2:
                un = k.alloc(i2)("un", [P, 5, D])
                rms_scale(k, [(y[0:N_META, NTL, :], un[0:N_META, NTL, :], N_META, None, None)] +
                          [(y[:, j, :], un[:, j, :], P, None, None) for j in range(NTL)])
                to_channels(k, token_tiles(un, un[0:N_META, NTL, :]), hT, lambda w, c: c1("norm_ffn_pre", c))
            feed_up(k, sbi, hT, actT)
        row = sb("row2", [P, D])
        k.stream.ahead = [(row[:, :], k.dram["rows1"][1].partition_broadcast(P)), (y[:, NTL:NT2, :], k.dram["ctx"])]
        with nc.Block() as block:
            ready = k.sig["product"]

            @block.tensor
            def _(pe):
                for cc in range(N_DOWN):
                    n = k.stream.take()
                    k.stream.wait(pe, n)
                    s = k.stream.slot(n).rearrange("p (k c) -> p k c", k=2)
                    for kk in range(2):
                        f = 2 * cc + kk
                        for j in range(NTL):
                            for half in range(2):
                                mm = pe.matmul(k.ps[:, 2 * j + half, :], actT[:, f, P * j:P * j + P],
                                               s[:, kk, half * BANK:(half + 1) * BANK], start=f == 0, stop=f == FT - 1,
                                               skip_group_check=True)
                    mm.then_inc(ready.sem, 1)
                    k.stream.freed(n, ready.sem, ready.of(cc + 1))

            @block.sync
            def _(sp):
                k.stream.issue(sp)
        ready.close(N_DOWN)
        mo = sb("mo2", [P, NTL, D])
        arrive(k, 2)
        rms_scale(k, [(k.psf[:, D * j:D * j + D], mo[:, j, :], P, row[:, :], y[:, j, :]) for j in range(NTL)])


def feed_up(k, sb, hT, actT):
    nc, c1 = k.nc, k.c1
    raw = sb("raw", [P, 2, 2, T1])
    conv = sb("conv", [P, 2, 2, SEQ])
    ready, copied, conved, gelued, mixed = (k.sig[x] for x in ("product", "taken_s", "fine", "low", "taken_v"))
    FIRST = N_META - 2
    with nc.Block() as block:
        @block.tensor
        def _(pe):
            for j in range(FT):
                n = k.stream.take()
                k.stream.wait(pe, n)
                if j >= 2:
                    pe.wait_ge(copied.sem, copied.of(j - 1))
                for gv in range(2):
                    w = column_chunk(k, n, gv)
                    for c_ in range(KD):
                        for h in range(2):
                            mm = pe.matmul(k.ps[:, 4 * (j % 2) + 2 * gv + h, 0:HALF1], w(c_),
                                           hT[:, c_, h * HALF1:(h + 1) * HALF1], start=c_ == 0, stop=c_ == KD - 1,
                                           skip_group_check=True)
                mm.then_inc(ready.sem, 1)
                k.stream.freed(n, ready.sem, ready.of(j + 1))

        @block.scalar
        def _(act):
            steps = k.steps(act, "s")

            def gelu(j):
                act.wait_ge(conved.sem, conved.of(j + 1))
                g = conv[:, j % 2, 0, :]
                act.activation(g, g, ACT.Gelu_apprx_tanh).then_inc(gelued.sem, 1)
            for j in range(FT):
                act.wait_ge(ready.sem, ready.of(j + 1))
                if j >= 2:
                    act.wait_ge(conved.sem, conved.of(j - 1))
                for gv in range(2):
                    b = 4 * (j % 2) + 2 * gv
                    steps.free(act.copy(halves(raw[:, j % 2, gv, :]), k.ps[:, b:b + 2, 0:HALF1]))
                steps.tell(copied.sem)
                if j >= 1:
                    gelu(j - 1)
            gelu(FT - 1)
            act.wait_ge(gelued.sem, gelued.of(FT))

        @block.vector
        def _(dve):
            steps = k.steps(dve, "v")

            def mix(j):
                dve.wait_ge(gelued.sem, gelued.of(j + 1))
                dve.tensor_tensor(actT[:, j, :], conv[:, j % 2, 0, :], conv[:, j % 2, 1, :],
                                  ALU.mult).then_inc(mixed.sem, 1)
            for j in range(FT):
                dve.wait_ge(copied.sem, copied.of(j + 1))
                if j >= 2:
                    dve.wait_ge(mixed.sem, mixed.of(j - 1))
                for tap in range(3):
                    for gv in range(2):
                        x = raw[:, j % 2, gv, FIRST + tap:FIRST + tap + SEQ]
                        y = conv[:, j % 2, gv, :]
                        cw = c1("ffn_conv", tap * 2 * FT + gv * FT + j)
                        if tap == 0:
                            steps.free(dve.tensor_scalar(y, x, cw, None, ALU.mult))
                        else:
                            steps.free(dve.scalar_tensor_tensor(y, x, cw, y, ALU.mult, ALU.add))
                    steps.join()
                dve.sem_inc(conved.sem, 1)
                if j >= 1:
                    mix(j - 1)
            mix(FT - 1)
            dve.wait_ge(mixed.sem, mixed.of(FT))

        @block.sync
        def _(sp):
            k.stream.issue(sp)
    for s in (ready, copied, conved, gelued, mixed):
        s.close(FT)


def second_block(k):
    nc = k.nc
    x = k.h1
    with ExitStack() as ctx:
        sb = k.alloc(ctx)
        const2 = sb("const2", [P, CONSTS[2][0].shape[1]])
        cols2 = sb("cols2", [P, LAYERS, NP2])
        at = {n: (const2, v) for n, v in CONSTS[2][1].items()}
        first = k.c
        k.c = lambda name: (at[name][0][:, at[name][1][0]:at[name][1][0] + at[name][1][1]] if name in at
                            else first(name))
        a, b = sb("tokens_a", [P, NT2 * D]), sb("tokens_b", [P, NT2 * D])
        k.stream.ahead = [(const2[:, :], k.dram["const2"]), (cols2[:, :, :], k.dram["cols2"].rearrange("l p c -> p l c"))]
        norm_tiles(k, NT2, x, to_next=(by_token(b), by_channel_tile(a), k.mod[:, 0], 0))
        arrive(k, 2)
        for l in range(LAYERS):
            k.c2 = lambda name, i, n=1, l=l: cols2[:, l, AT2[name] + i:AT2[name] + i + n]
            mod = k.mod[:, l]
            layer(k, l, x, mod, a, b)
            a, b = b, a


def by_token(buf):
    return buf[:, :].rearrange("p (t d) -> p t d", d=D)


def by_channel_tile(buf):
    return buf[:, :].rearrange("p (k t) -> p k t", k=KD)


def norm_tiles(k, nt, x, residual=None, to_next=None, store=None):
    nc, sg = k.nc, k.sig
    ready, taken, meant, rooted = sg["product"], sg["taken_v"], sg["meant"], sg["rooted"]
    meant2, rooted2, normed, made, moved = sg["meant2"], sg["rooted2"], sg["normed"], sg["made"], sg["moved"]
    stored = sg["stored"]
    o, grow, gb = residual or (None, None, None)
    products_ = o if callable(o) else None
    u, uT, mod, base = to_next or (None, None, None, 0)
    with ExitStack() as ctx:
        sb = k.alloc(ctx)
        tmp = sb("tmp", [P, 2, BANK])
        stats = sb("stats", [P, 2, NT2, 2, 6])
        mv = sb("mv", [P, 2, NT2, 2])
        rstd = sb("rstd", [P, 2, NT2])

        def half_of(ap, half):
            return ap[:, half * BANK:(half + 1) * BANK]

        with nc.Block() as block:
            @block.tensor
            def _(pe):
                for t in range(nt + 2):
                    for half in range(2):
                        if products_ and t < nt:
                            i = 2 * t + half
                            if i >= 4:
                                pe.wait_ge(taken.sem, taken.of(i - 3))
                            products_(pe, t, half, k.ps[:, i % 4, :]).then_inc(ready.sem, 1)
                        if half == 0 and to_next and t >= 2:
                            s = t - 2
                            pe.wait_ge(normed.sem, normed.of(s + 1))
                            if s >= 2:
                                pe.wait_ge(moved.sem, moved.of(s - 1))
                            for c_ in range(KD):
                                mm = pe.transpose(k.ps[:, 4 + 2 * (s % 2) + c_ // 4, (c_ % 4) * P:(c_ % 4 + 1) * P],
                                                  u[:, s, c_ * P:(c_ + 1) * P], k.c("ident"))
                            mm.then_inc(made.sem, 1)

            @block.vector
            def _(dve):
                steps = k.steps(dve, "v")

                def combine(t, half):
                    w, i = int(t >= NTL), 2 * t + half
                    if products_:
                        dve.wait_ge(ready.sem, ready.of(i + 1))
                        src = k.ps[:, i % 4, :]
                    else:
                        src = half_of(o[:, t, :], half)
                    xh = half_of(x[:, t, :], half)
                    steps(dve.tensor_tensor(tmp[:, half, :], src, half_of(grow[:, w, :], half), ALU.mult))
                    if products_:
                        dve.sem_inc(taken.sem, 1)
                    steps(dve.scalar_tensor_tensor(xh, xh, ALPHA, tmp[:, half, :], ALU.mult, ALU.add))
                    steps.free(dve.bn_stats(stats[:, 0, t, half, :], xh))

                def spread(which, t, signal):
                    steps.join()
                    steps(dve.bn_aggr(mv[:, which, t, :], stats[:, which, t, :, :]))
                    dve.tensor_scalar(rstd[:, which, t:t + 1], mv[:, which, t, 1:2], LN_EPS, None,
                                      ALU.add).then_inc(signal.sem, 1)

                def apply(which, t, dst, signal):
                    dve.wait_ge(signal.sem, signal.of(t + 1))
                    r = rstd[:, which, t:t + 1]
                    steps(dve.reciprocal(r, r))
                    return dve.tensor_scalar(dst, x[:, t, :], mv[:, which, t, 0:1], r, ALU.subtract, ALU.mult)

                for t in range(nt + 1):
                    if residual and t < nt:
                        combine(t, 0)
                    s = t - 1
                    if s >= 0:
                        if residual:
                            steps(apply(0, s, x[:, s, :], rooted))
                            steps(dve.tensor_tensor(x[:, s, :], x[:, s, :], gb[:, 0, :], ALU.mult))
                            steps(dve.tensor_tensor(x[:, s, :], x[:, s, :], gb[:, 1, :], ALU.add))
                        if to_next:
                            for half in range(2):
                                steps.free(dve.bn_stats(stats[:, 1, s, half, :], half_of(x[:, s, :], half)))
                            spread(1, s, meant2)
                        else:
                            dve.sem_inc(normed.sem, 1)
                    if residual and t < nt:
                        combine(t, 1)
                        spread(0, t, meant)
                    if s >= 0 and to_next:
                        apply(1, s, u[:, s, :], rooted2).then_inc(normed.sem, 1)
                dve.wait_ge(normed.sem, normed.of(nt))

            @block.scalar
            def _(act):
                steps = k.steps(act, "s")
                for t in range(nt + 2):
                    if to_next and 0 <= t - 1 < nt:
                        act.wait_ge(meant2.sem, meant2.of(t))
                        r = rstd[:, 1, t - 1:t]
                        act.activation(r, r, ACT.Sqrt).then_inc(rooted2.sem, 1)
                    if residual and t < nt:
                        act.wait_ge(meant.sem, meant.of(t + 1))
                        r = rstd[:, 0, t:t + 1]
                        act.activation(r, r, ACT.Sqrt).then_inc(rooted.sem, 1)
                    if to_next and t >= 2:
                        s, w = t - 2, int(t - 2 >= NTL)
                        act.wait_ge(made.sem, made.of(s + 1))
                        for c_ in range(KD):
                            steps.free(act.activation(uT[:, c_, P * s:P * s + P],
                                                      k.ps[:, 4 + 2 * (s % 2) + c_ // 4, (c_ % 4) * P:(c_ % 4 + 1) * P],
                                                      ACT.Identity, scale=mod[:, (base + 1) * KD + c_, w:w + 1],
                                                      bias=mod[:, base * KD + c_, w:w + 1]))
                        steps.tell(moved.sem)

            @block.sync
            def _(sp):
                k.stream.issue(sp)
                if store is not None:
                    for t in range(nt):
                        sp.wait_ge(normed.sem, normed.of(t + 1))
                        sp.dma_start(store(t), x[:, t, :]).then_inc(stored.sem, 16)
                    sp.wait_ge(stored.sem, stored.of(16 * nt))
    normed.close(nt)
    if products_:
        ready.close(2 * nt)
        taken.close(2 * nt)
    if residual:
        meant.close(nt)
        rooted.close(nt)
    if to_next:
        for s in (meant2, rooted2, made, moved):
            s.close(nt)


def gate_rows(k, sb, l, which, mod, nw):
    nc, c = k.nc, k.c
    made, moved, loads = k.sig["made"], k.sig["moved"], k.sig["load"]
    gb = sb("gb", [P, 2, D])
    grow = sb("grow", [P, nw, D])
    diag = sb("diag", [P, 2, 4, P])
    todo = [(w, c_) for w in range(nw) for c_ in range(0, KD, 4)]
    with nc.Block() as block:
        @block.sync
        def _(sp):
            for i in range(2):
                sp.dma_start(gb[:, i, :], k.dram["rows2"][l, 2 * which + i].partition_broadcast(P)).then_inc(loads.sem, 16)
            k.stream.issue(sp)
            sp.wait_ge(loads.sem, loads.of(32))

        @block.vector
        def _(dve):
            steps = k.steps(dve, "v")
            for i, (w, c_) in enumerate(todo):
                if i >= 2:
                    dve.wait_ge(made.sem, made.of(i - 1))
                gate = mod[:, (3 * which + 2) * KD + c_:(3 * which + 2) * KD + c_ + 4, w:w + 1].to_broadcast([P, 4, P])
                dve.tensor_tensor(diag[:, i % 2, :, :], c("ident").unsqueeze(1).to_broadcast([P, 4, P]), gate,
                                  ALU.mult).then_inc(moved.sem, 1)
            for i, (w, c_) in enumerate(todo):
                dve.wait_ge(made.sem, made.of(i + 1))
                steps.free(dve.tensor_copy(grow[:, w, c_ * P:(c_ + 4) * P], k.ps[:, i, :]))
            steps.join()

        @block.tensor
        def _(pe):
            for i in range(len(todo)):
                pe.wait_ge(moved.sem, moved.of(i + 1))
                pe.matmul(k.ps[:, i, :], c("ones"), diag[:, i % 2, :, :].rearrange("p a q -> p (a q)"), start=True,
                          stop=True).then_inc(made.sem, 1)
    made.close(len(todo))
    moved.close(len(todo))
    loads.close(32)
    return grow, gb


def layer_norm(k, jobs):
    nc = k.nc
    meant, rooted = k.sig["meant"], k.sig["rooted"]
    width = jobs[0][0].shape[1]
    nb = (width + BANK - 1) // BANK
    with ExitStack() as ctx:
        sb = k.alloc(ctx)
        stats = sb("stats", [P, NT2, nb, 6])
        mv = sb("mv", [P, NT2, 2])
        rstd = sb("rstd", [P, NT2])
        with nc.Block() as block:
            @block.vector
            def _(dve):
                steps = k.steps(dve, "v")
                for i, (x, out, gain, bias) in enumerate(jobs):
                    for b in range(nb):
                        steps.free(dve.bn_stats(stats[:, i, b, :], x[:, b * BANK:min(width, (b + 1) * BANK)]))
                    steps.join()
                    steps(dve.bn_aggr(mv[:, i, :], stats[:, i, :, :]))
                    dve.tensor_scalar(rstd[:, i:i + 1], mv[:, i, 1:2], LN_EPS, None, ALU.add).then_inc(meant.sem, 1)
                for i, (x, out, gain, bias) in enumerate(jobs):
                    dve.wait_ge(rooted.sem, rooted.of(i + 1))
                    steps(dve.reciprocal(rstd[:, i:i + 1], rstd[:, i:i + 1]))
                    steps(dve.tensor_scalar(out, x, mv[:, i, 0:1], rstd[:, i:i + 1], ALU.subtract, ALU.mult))
                    if gain is not None:
                        steps(dve.tensor_tensor(out, out, gain, ALU.mult))
                        steps(dve.tensor_tensor(out, out, bias, ALU.add))

            @block.scalar
            def _(act):
                for i in range(len(jobs)):
                    act.wait_ge(meant.sem, meant.of(i + 1))
                    act.activation(rstd[:, i:i + 1], rstd[:, i:i + 1], ACT.Sqrt).then_inc(rooted.sem, 1)

            @block.sync
            def _(sp):
                k.stream.issue(sp)
    meant.close(len(jobs))
    rooted.close(len(jobs))


def layer(k, l, x, mod, a, b):
    last = l == LAYERS - 1
    nq = SEQ if last else T2
    ntq = nq // P
    nw = 1 if last else 2
    mixT = by_channel_tile(a)
    u = by_token(b)
    with ExitStack() as inner:
        sbi = k.alloc(inner)
        qa = sbi("qa", [P, 4, T2])
        ka = sbi("ka", [P, T2])
        qb = sbi("qb", [P, 2, T2])
        kb = sbi("kb", [P, 2, T2])
        va = sbi("va", [P, NT2, 2 * HD])
        vb = sbi("vb", [P, NT2, 4 * HD])
        pad = sbi("pad", [P, 2, conv_width(nq) + 2 * CH_HALF])
        z = sbi("z", [P, 2, conv_width(nq)])
        NB = 4
        cin = b[:, 0:4 * T2].rearrange("p (a g t) -> p a g t", a=2, g=2)
        n_bias = NB * BIAS_ROWS * GRID_W
        bias = b[:, 0:n_bias].rearrange("p (h r c) -> p h r c", h=NB, r=BIAS_ROWS)
        rest = b[:, n_bias:]
        far = rest[:, 0:n_bias // 2].rearrange("p (h r c) -> p h r c", h=NB // 2, r=BIAS_ROWS)
        with ExitStack() as scope:
            near = k.alloc(scope)("near", [P, NB // 2, BIAS_ROWS, GRID_W])
            raw = [near[:, 0], near[:, 1], far[:, 0], far[:, 1]]
            k.stream.ahead = bias_loads(k, l, raw)
            project2(k, mixT, nq, qa, ka, qb, kb, va, vb, cin)
            mixer_inputs(k, l, cin, pad, nq, [(qa, i) for i in range(4)] + [(ka, None)], raw, bias)
        modulation = None if last else Modulation(k, b[:, NT2 * D - BANK:].rearrange("p (a c) -> p a c", a=2), l + 1)
        mixers(k, ntq, qa, ka, qb, kb, va, vb, mixT, bias, rest, modulation, conv_taps(k, pad, z, nq))
        conv_output(k, z, mixT, nq)
    with ExitStack() as inner:
        rows = gate_rows(k, k.alloc(inner), l, 0, mod, nw)
        norm_tiles(k, ntq, x, residual=(project_out(k, mixT, ntq),) + rows, to_next=(u, mixT, mod, 3))
    with ExitStack() as inner:
        moe = by_token(a)
        experts(k, k.alloc(inner), l, x, mod, ntq, moe, u, mixT)
    with ExitStack() as inner:
        rows = gate_rows(k, k.alloc(inner), l, 1, mod, nw)
        if last:
            norm_tiles(k, ntq, x, residual=(moe,) + rows, store=lambda t: k.out[0, P * t:P * t + P, :])
        else:
            norm_tiles(k, ntq, x, residual=(moe,) + rows, to_next=(moe, by_channel_tile(b), k.mod[:, l + 1], 0))


def project2(k, uT, nq, qa, ka, qb, kb, va, vb, cin):
    groups, where = [], []

    def channels(n, j, dst, tokens, scale, needs, last):
        w = column_chunk(k, n, j)
        half = tokens // 2
        i = len(groups)
        groups.append(dict(places=4, needs=needs, last=last,
                           mm=[(k.ps[:, 2 * (i % 4) + h, 0:half], w(c_), uT[:, c_, h * half:(h + 1) * half], c_ == 0,
                                c_ == KD - 1) for c_ in range(KD) for h in range(2)]))
        where.append((dst, 0, half, scale))

    def tokens_(n, lo, width, dst, needs, last):
        s = k.stream.slot(n).rearrange("p (k c) -> p k c", k=KD)
        for t in range(NT2):
            i = len(groups)
            groups.append(dict(places=4, needs=needs if t == 0 else [], last=last if t == NT2 - 1 else [],
                               mm=[(k.ps[:, 2 * (i % 4), 0:width], uT[:, c_, P * t:P * t + P], s[:, c_, lo:lo + width],
                                    c_ == 0, c_ == KD - 1) for c_ in range(KD)]))
            where.append((dst[:, t, :], 1, width, None))

    for i in range(2):
        n = k.stream.take()
        channels(n, 0, qa[:, 2 * i, :], nq, -HD ** -0.5, [n], [])
        channels(n, 1, qa[:, 2 * i + 1, :], nq, -HD ** -0.5, [], [n])
    n = k.stream.take()
    channels(n, 0, ka[:, :], T2, None, [n], [])
    tokens_(n, P, 2 * HD, va, [], [n])
    n = k.stream.take()
    channels(n, 0, qb[:, 0, :], nq, -HD ** -0.5, [n], [])
    channels(n, 1, qb[:, 1, :], nq, -HD ** -0.5, [], [n])
    n = k.stream.take()
    channels(n, 0, kb[:, 0, :], T2, None, [n], [])
    channels(n, 1, kb[:, 1, :], T2, None, [], [n])
    n = k.stream.take()
    tokens_(n, 0, 4 * HD, vb, [n], [n])
    for i in range(2):
        n = k.stream.take()
        channels(n, 0, cin[:, i, 0, :], nq, None, [n], [])
        channels(n, 1, cin[:, i, 1, :], nq, None, [], [n])

    def take(k, who, i, steps):
        dst, kind, width, scale = where[i]
        b = 2 * (i % 4)
        if kind:
            return copy_out(k, who, dst, k.ps[:, b, 0:width])
        return copy_out(k, who, dst[:, 0:2 * width].rearrange("p (h t) -> p h t", h=2), k.ps[:, b:b + 2, 0:width], scale)
    products(k, groups, take)


CONV_GAP = CH_HALF
CONV_CTX = SEQ + CONV_GAP


def conv_width(nq):
    return CONV_CTX + CTX if nq > SEQ else SEQ


def mixer_inputs(k, l, cin, pad, nq, tiles, raw, bias):
    nc, c = k.nc, k.c
    low, made, flipped, loads = k.sig["low"], k.sig["made"], k.sig["flipped"], k.sig["load"]
    NB = len(raw)
    N = len(tiles)
    cut = BANK // GRID_W

    def lat(i):
        t, j = tiles[i]
        return t[:, j, 0:SEQ] if j is not None else t[:, 0:SEQ]
    with ExitStack() as ctx:
        tmp = k.alloc(ctx)("rtmp", [P, 2, SEQ])
        with nc.Block() as block:
            @block.tensor
            def _(pe):
                for i in range(N):
                    if i >= 2:
                        pe.wait_ge(low.sem, low.of(i))
                    pe.matmul(k.ps[:, i % 2, :], c("rot"), lat(i), start=True, stop=True).then_inc(made.sem, 1)
                pe.wait_ge(loads.sem, loads.of(16 * 2 * NB))
                for h in range(NB):
                    b = 2 + 2 * (h % 3)
                    if h == 3:
                        pe.wait_ge(low.sem, low.of(N + 2))
                    pe.matmul(k.ps[:, b, :], c("flip"), raw[h][:, 0:cut, :].rearrange("p r c -> p (r c)"), start=True,
                              stop=True)
                    pe.matmul(k.ps[:, b + 1, 0:(BIAS_ROWS - cut) * GRID_W], c("flip"),
                              raw[h][:, cut:BIAS_ROWS, :].rearrange("p r c -> p (r c)"), start=True,
                              stop=True).then_inc(flipped.sem, 1)

            @block.scalar
            def _(act):
                steps = k.steps(act, "s")
                steps.free(act.activation(cin[:, 1, :, 0:nq], cin[:, 1, :, 0:nq], ACT.Sigmoid))
                steps.tell(low.sem)

            @block.vector
            def _(dve):
                steps = k.steps(dve, "v")
                dve.wait_ge(low.sem, low.of(1))
                steps.free(dve.memset(pad[:, :, :], 0.0))
                for i in range(N):
                    dve.wait_ge(made.sem, made.of(i + 1))
                    steps.free(dve.tensor_tensor(tmp[:, i % 2, :], k.ps[:, i % 2, :], c("sin"), ALU.mult))
                    steps(dve.tensor_tensor(lat(i), lat(i), c("cos"), ALU.mult))
                    dve.sem_inc(low.sem, 1)
                    steps.free(dve.tensor_tensor(lat(i), lat(i), tmp[:, i % 2, :], ALU.add))
                steps.join()
                steps.free(dve.tensor_tensor(pad[:, :, CH_HALF:CH_HALF + SEQ], cin[:, 0, :, 0:SEQ], cin[:, 1, :, 0:SEQ],
                                             ALU.mult))
                if nq > SEQ:
                    at = CONV_CTX + CH_HALF
                    steps.free(dve.tensor_tensor(pad[:, :, at:at + CTX], cin[:, 0, :, SEQ:T2], cin[:, 1, :, SEQ:T2],
                                                 ALU.mult))
                steps.join()
                for h in range(NB):
                    dve.wait_ge(flipped.sem, flipped.of(h + 1))
                    b = 2 + 2 * (h % 3)
                    rows = k.psf[:, b * BANK:b * BANK + BIAS_ROWS * GRID_W].rearrange("p (r c) -> p r c", c=GRID_W)
                    steps(dve.tensor_tensor(bias[:, h, :, :], rows,
                                            c("col_mask").unsqueeze(1).to_broadcast([P, BIAS_ROWS, GRID_W]), ALU.add))
                    if h == 0:
                        dve.sem_inc(low.sem, 1)
    made.close(N)
    low.close(N + 2)
    flipped.close(NB)
    loads.close(16 * 2 * NB)


def bias_loads(k, l, raw):
    out = []
    for half in range(2):
        for h in range(len(raw)):
            a = k.dram["bias"][l, h, 1 - half:1 - half + BIAS_ROWS, 0:GRID_W]
            out.append((raw[h][GRID_W * half:GRID_W * (half + 1), :, :],
                        bass.AP(a.tensor, a.offset, [[1, GRID_W], [BIAS_PAD, BIAS_ROWS], [1, GRID_W]])))
    return out


def conv_taps(k, pad, z, nq):
    n_out, c2 = conv_width(nq), k.c2

    def one(tap, g):
        def work(dve, steps):
            w = c2("conv_w", 2 * tap + g)
            src = pad[:, g, tap:tap + n_out]
            if tap == 0:
                steps.free(dve.tensor_scalar(z[:, g, :], src, w, c2("conv_b", g), ALU.mult, ALU.add))
            else:
                steps.join()
                steps.free(dve.scalar_tensor_tensor(z[:, g, :], src, w, z[:, g, :], ALU.mult, ALU.add))
        return work
    return [one(tap, g) for tap in range(CW) for g in range(2)]


def conv_output(k, z, mixT, nq):
    nc, c2 = k.nc, k.c2
    ntq = nq // P
    with ExitStack() as ctx:
        zt = k.alloc(ctx)("zt", [P, NT2, 2 * P])

        def column(t):
            return P * t if t < NTL else CONV_CTX + P * (t - NTL)
        with nc.Block() as block:
            @block.tensor
            def _(pe):
                for t in range(ntq):
                    for g in range(2):
                        pe.transpose(k.ps[:, t, g * P:(g + 1) * P], z[:, g, column(t):column(t) + P], k.c("ident"))
        layer_norm(k, [(k.ps[:, t, 0:2 * P], zt[:, t, :], None, None) for t in range(ntq)])
        made = k.sig["made"]
        with nc.Block() as block:
            @block.tensor
            def _(pe):
                for t in range(ntq):
                    for g in range(2):
                        mm = pe.transpose(k.ps[:, t, g * P:(g + 1) * P], zt[:, t, g * P:(g + 1) * P], k.c("ident"))
                    mm.then_inc(made.sem, 1)

            @block.scalar
            def _(act):
                steps = k.steps(act, "s")
                for t in range(ntq):
                    act.wait_ge(made.sem, made.of(t + 1))
                    for g in range(2):
                        steps.free(act.activation(mixT[:, 6 + g, P * t:P * t + P], k.ps[:, t, g * P:(g + 1) * P], ACT.Silu,
                                                  bias=c2("ln_b", g), scale=c2("ln_g", g)))
                steps.join()
        made.close(ntq)


def mixers(k, ntq, qa, ka, qb, kb, va, vb, mixT, bias, rest, modulation, extra):
    c, c2 = k.c, k.c2
    NB = bias.shape[1]
    units = []
    ctx_values = lambda v, s: [(v[:, NTL + i, s], P, P * i) for i in range(2)]
    for t in range(ntq):
        for i in range(8):
            kv, g = i % 2, i // 2
            h = 4 * kv + g
            b = slice(HD * kv, HD * kv + HD)
            q = qa[b, g, P * t:P * t + P]
            scores = [(0, [(q, ka[b, SEQ:T2])])]
            values, adds, width = ctx_values(va, b), [], CTX
            if t < NTL:
                w0, w1 = max(0, t - 1), min(NTL - 1, t + 1)
                scores.append((CTX, [(q, ka[b, P * w0:P * (w1 + 1)])]))
                for w in range(w0, w1 + 1):
                    col = CTX + P * (w - w0)
                    values.append((va[:, w, b], P, col))
                    if w != t:
                        adds.append((col, c("band_prev" if w < t else "band_next")))
                width += P * (w1 - w0 + 1)
            units.append(dict(q=q, width=width, sink=c2("sink", h), scores=scores,
                              adds=adds, values=values, out=mixT[:, g, P * t:P * t + P]))
        for h in range(NB):
            b = slice(HD * (h % 2), HD * (h % 2) + HD)
            s = slice(HD * h, HD * h + HD)
            q = qb[b, h // 2, P * t:P * t + P]
            if t < NTL:
                m0 = GRID_H - 1 - 2 * t
                units.append(dict(q=q, width=T2, sink=None,
                                  scores=[(0, [(q, kb[b, h // 2, 0:SEQ])]), (SEQ, [(q, kb[b, h // 2, SEQ:T2])])],
                                  adds=[(0, bias[:, h, m0:m0 + GRID_H, :].rearrange("p r c -> p (r c)"))],
                                  values=[(vb[:, w, s], P, P * w) for w in range(NT2)],
                                  out=mixT[:, 4 + h // 2, P * t:P * t + P]))
            else:
                units.append(dict(q=q, width=CTX, sink=None,
                                  scores=[(0, [(q, kb[b, h // 2, SEQ:T2])])], adds=[], values=ctx_values(vb, s),
                                  out=mixT[:, 4 + h // 2, P * t:P * t + P]))
    attention(k, units, rest, modulation, extra)


def project_out(k, mixT, ntq):
    chunks = [k.stream.take() for _ in range(N_OUT2)]
    ready = k.sig["product"]

    def products_(pe, t, half, bank):
        pair = chunks[2 * half:2 * half + 2]
        if t == 0:
            for n in pair:
                k.stream.wait(pe, n)
        if t == ntq - 1:
            for n in pair:
                k.stream.freed(n, ready.sem, ready.of(2 * t + half + 1))
        for c_ in range(KD):
            w = k.stream.slot(pair[c_ // 4]).rearrange("p (k c) -> p k c", k=4)
            mm = pe.matmul(bank, mixT[:, c_, P * t:P * t + P], w[:, c_ % 4, :], start=c_ == 0, stop=c_ == KD - 1)
        return mm
    return products_


PAIR_CHUNKS = 24


def expert_chunk(dram, l, e, j):
    m, kh, half, par = j // 8, j % 8 // 4, j % 4 // 2, j % 2
    return dram[("w_gate", "w_up", "w_down")[m]][l, e + par, BANK * kh:BANK * (kh + 1),
                                                 BANK * half:BANK * (half + 1)].rearrange("(k p) c -> p k c", p=P)


def experts(k, sb, l, x, mod, ntq, moe, u, uT):
    nc, c, c2 = k.nc, k.c, k.c2
    with_ctx = ntq > NTL
    aff = sb("aff", [P, NT2, N_EXP])
    pos = sb("pos", [P, NT2, N_EXP + 2])
    xsL = sb("xsL", [P, KD, 2, CAP_L])
    xsC = sb("xsC", [P, KD, 2, CAP_C])
    choL = sb("choL", [P, NTL, 2, CAP_L])
    choC = sb("choC", [P, 2, 2, CAP_C])
    gatL = sb("gatL", [P, NTL, 2, CAP_L])
    gatC = sb("gatC", [P, 2, 2, 2, 2, CAP_C])
    gtL = sb("gtL", [P, NTL, P])
    gtC = sb("gtC", [P, 2, 2, P])
    hidL = sb("hidL", [P, FF])
    hidC = sb("hidC", [P, BANK])
    htL = sb("htL", [P, KD, P])
    htC = sb("htC", [P, KD // 2, P])
    yeL = sb("yeL", [P, D])
    yeC = sb("yeC", [P, BANK])
    with ExitStack() as ctx:
        route(k, k.alloc(ctx), uT, aff, pos, ntq, [moe] + [b[tuple([slice(None)] * len(b.shape))]
                                                           for b in (gatC, yeL, yeC, gtL, gtC)])
    sg = k.sig
    used, choice, gath, xs_, gatd, gtr, gts = (sg[n] for n in ("used", "choice", "gath", "xs", "gatd", "gtr", "gts"))
    silu, hid, htr, hts, yes, scat, added = (sg[n] for n in ("silu", "hid", "htr", "hts", "yes", "scat", "added"))
    inner_v, inner_s = sg["inner_v"], sg["inner_s"]
    base = k.moe_at[l]
    stream = k.stream
    assert stream.taken == base and 24 % RING == 0 and RING == 8
    PAIRS = N_EXP // 2
    PER = PAIR_CHUNKS
    C = int(with_ctx)
    NG = 2 + C
    n_sc = 2 * NTL + 4 * C
    GB, UB, CG, CU, MISC = 0, 2, 4, 5, 6

    def slot(j):
        return stream.slot(base + j).rearrange("p (k c) -> p k c", k=4)

    with nc.Block() as block:
        @block.vector
        def _(dve):
            for s in (yes, gtr, htr):
                dve.sem_inc(s.sem, 1)

        @block.sync
        def _(sp):
            stream.issue(sp)
            assert stream.issued == base + RING
    for s in (yes, gtr, htr):
        s.close(1)

    with nc.Block() as block:
        @block.sync
        def _(sp):
            def fetch(pr, j, freed):
                sp.wait_ge(used.sem, used.of(freed))
                sp.dma_start(slot(j), expert_chunk(k.dram, l, 2 * pr, j)).then_inc(stream.landed(base + j)[0], 16)
            with sp.Fori(0, PAIRS - 1) as pr:
                for j in range(RING, PER):
                    fetch(pr, j, 6 * pr + j // 4 - 1)
                for j in range(RING):
                    fetch(pr + 1, j, 6 * pr + 5 + j // 4)
            for j in range(RING, PER):
                fetch(PAIRS - 1, j, 6 * (PAIRS - 1) + j // 4 - 1)

        @block.tensor
        def _(pe):
            def gather(n):
                pe.wait_ge(choice.sem, choice.of(n))
                for part in range(2):
                    for c_ in range(4):
                        for t in range(NTL):
                            ch = 4 * part + c_
                            mm = pe.matmul(k.ps[:, MISC + part, c_ * P:(c_ + 1) * P], u[:, t, ch * P:(ch + 1) * P],
                                           choL[:, t, :, :].rearrange("p a s -> p (a s)"), start=t == 0,
                                           stop=t == NTL - 1, skip_group_check=True)
                    mm.then_inc(gath.sem, 1)
                if C:
                    pe.wait_ge(xs_.sem, xs_.of(NG * (n - 1) + 1))
                    for ch in range(KD):
                        for t in range(2):
                            mm = pe.matmul(k.ps[:, MISC, ch * HD:(ch + 1) * HD], u[:, NTL + t, ch * P:(ch + 1) * P],
                                           choC[:, t, :, :].rearrange("p a s -> p (a s)"), start=t == 0, stop=t == 1,
                                           skip_group_check=True)
                    mm.then_inc(gath.sem, 1)

            def matrix(pr, m, bank, cbank, lhsL, lhsC):
                for kh in range(2):
                    for x in range(4):
                        j = 8 * m + 4 * kh + x
                        sem, first = stream.landed(base + j)
                        pe.wait_ge(sem, first + 16 * (PER // RING) * pr)
                    w = [[slot(8 * m + 4 * kh + 2 * half + par) for par in range(2)] for half in range(2)]
                    for kk in range(4):
                        for half in range(2):
                            for par in range(2):
                                mm = pe.matmul(k.ps[HD * par:HD * par + HD, bank + half, :], lhsL(4 * kh + kk, par),
                                               w[half][par][:, kk, :], start=kh + kk == 0, stop=kh == 1 and kk == 3,
                                               skip_group_check=True)
                    if C:
                        for kk in range(4):
                            for par in range(2):
                                for half in range(2):
                                    q = 32 * (2 * par + half)
                                    mm = pe.matmul(k.ps[q:q + CAP_C, cbank, :], lhsC(4 * kh + kk, par),
                                                   w[half][par][:, kk, :], start=kh + kk == 0, stop=kh == 1 and kk == 3,
                                                   skip_group_check=True)
                    mm.then_inc(used.sem, 1)

            def scatter(n):
                for i in range(n_sc):
                    if i >= 2:
                        pe.wait_ge(added.sem, added.of(n_sc * n + i - 1))
                    lat = i < 2 * NTL
                    half = i % 2
                    if lat:
                        lhsT, rhs = gtL[:, i // 2, :], yeL[:, half * BANK:(half + 1) * BANK]
                    else:
                        lhsT, rhs = gtC[:, i // 2 - NTL, half, :], yeC[:, :]
                    pe.matmul(k.ps[:, MISC + i % 2, :], lhsT, rhs, start=True, stop=True,
                              skip_group_check=True).then_inc(scat.sem, 1)

            gather(1)
            with pe.Fori(0, PAIRS) as pr:
                pe.wait_ge(xs_.sem, xs_.of(NG * pr + NG))
                matrix(pr, 0, GB, CG, lambda c_, par: xsL[:, c_, par, :], lambda c_, par: xsC[:, c_, par, :])
                pe.wait_ge(yes.sem, yes.of((1 + C) * pr))
                scatter(pr)
                matrix(pr, 1, UB, CU, lambda c_, par: xsL[:, c_, par, :], lambda c_, par: xsC[:, c_, par, :])
                pe.wait_ge(added.sem, added.of(n_sc * pr + n_sc))
                gather(pr + 2)
                pe.wait_ge(gatd.sem, gatd.of(pr + 1))
                pe.wait_ge(xs_.sem, xs_.of(NG * (pr + 1) + 2))
                for t in range(NTL):
                    mm = pe.transpose(k.ps[:, MISC + 1, t * P:(t + 1) * P], gatL[:, t, :, :].rearrange("p a s -> p (a s)"),
                                      c("ident"))
                mm.then_inc(gtr.sem, 1)
                if C:
                    pe.wait_ge(xs_.sem, xs_.of(NG * (pr + 1) + 3))
                    for t in range(2):
                        for half in range(2):
                            mm = pe.transpose(k.ps[:, MISC, (2 * t + half) * P:(2 * t + half + 1) * P],
                                              gatC[:, t, half, :, :, :].rearrange("p a h s -> p (a h s)"), c("ident"))
                    mm.then_inc(gtr.sem, 1)
                for part in range(1 + C):
                    pe.wait_ge(hid.sem, hid.of((1 + C) * pr + part + 1))
                    for c_ in range(KD if part == 0 else KD // 2):
                        bank = GB + c_ // 4 if part == 0 else CG
                        src = (hidL if part == 0 else hidC)[:, c_ * P:(c_ + 1) * P]
                        mm = pe.transpose(k.ps[:, bank, (c_ % 4) * P:(c_ % 4 + 1) * P], src, c("ident"))
                    mm.then_inc(htr.sem, 1)
                pe.wait_ge(hts.sem, hts.of((1 + C) * (pr + 1)))
                matrix(pr, 2, UB, CU, lambda c_, par: htL[:, c_, par * HD:(par + 1) * HD],
                       lambda c_, par: htC[:, c_ % 4, par * HD + CAP_C * (c_ // 4):par * HD + CAP_C * (c_ // 4) + CAP_C])
            pe.wait_ge(yes.sem, yes.of((1 + C) * PAIRS))
            pe.wait_ge(gts.sem, gts.of((1 + C) * PAIRS))
            scatter(PAIRS)

        @block.vector
        def _(dve):
            done = [0]

            def tick(ins):
                ins.then_inc(inner_v.sem, 1)
                done[0] += 1

            def settle(ticks):
                dve.wait_ge(inner_v.sem, inner_v.of(ticks + done[0]))

            def shape(ap, n, w):
                return ap.unsqueeze(3).to_broadcast([P, n, 2, w])

            def iota(n, w):
                return c("iota")[:, 0:w].unsqueeze(1).unsqueeze(1).to_broadcast([P, n, 2, w])

            def choose(e, ticks):
                tick(dve.tensor_tensor(choL[:, :, :, :], iota(NTL, CAP_L), shape(pos[:, 0:NTL, bass.ds(e, 2)], NTL, CAP_L),
                                       ALU.is_equal))
                if C:
                    tick(dve.tensor_tensor(choC[:, :, :, :], iota(2, CAP_C), shape(pos[:, NTL:NT2, bass.ds(e, 2)], 2, CAP_C),
                                           ALU.is_equal))
                settle(ticks)
                dve.sem_inc(choice.sem, 1)

            def gate(e, ticks):
                tick(dve.tensor_tensor(gatL[:, :, :, :], iota(NTL, CAP_L), shape(pos[:, 0:NTL, bass.ds(e, 2)], NTL, CAP_L),
                                       ALU.is_equal))
                if C:
                    for half in range(2):
                        tick(dve.tensor_tensor(gatC[:, :, half, :, half, :], iota(2, CAP_C),
                                               shape(pos[:, NTL:NT2, bass.ds(e, 2)], 2, CAP_C), ALU.is_equal))
                settle(ticks)
                tick(dve.tensor_tensor(gatL[:, :, :, :], gatL[:, :, :, :], shape(aff[:, 0:NTL, bass.ds(e, 2)], NTL, CAP_L),
                                       ALU.mult))
                if C:
                    for half in range(2):
                        g = gatC[:, :, half, :, half, :]
                        tick(dve.tensor_tensor(g, g, shape(aff[:, NTL:NT2, bass.ds(e, 2)], 2, CAP_C), ALU.mult))
                settle(ticks)
                dve.sem_inc(gatd.sem, 1)

            def tokens_out(n, ticks):
                for part in range(NG):
                    dve.wait_ge(gath.sem, gath.of(NG * (n - 1) + part + 1))
                    w, lo, nc_, m = (0, 4 * part, 4, P) if part < 2 else (1, 0, KD, HD)
                    src = k.ps[:, MISC + part % 2, :].rearrange("p (k s) -> p k s", s=m)
                    dst = (xsL if part < 2 else xsC)[:, lo:lo + nc_, :, :].rearrange("p k a s -> p k (a s)")
                    sc = mod[:, 4 * KD + lo:4 * KD + lo + nc_, w:w + 1].to_broadcast([P, nc_, m])
                    sh = mod[:, 3 * KD + lo:3 * KD + lo + nc_, w:w + 1].to_broadcast([P, nc_, m])
                    tick(dve.tensor_tensor(dst, src, sc, ALU.mult))
                    settle(ticks)
                    tick(dve.tensor_tensor(dst, dst, sh, ALU.add))
                    settle(ticks)
                    dve.sem_inc(xs_.sem, 1)

            def add(n):
                for i in range(n_sc):
                    dve.wait_ge(scat.sem, scat.of(n_sc * n + i + 1))
                    y = moe[:, i // 2, (i % 2) * BANK:(i % 2 + 1) * BANK]
                    dve.tensor_tensor(y, y, k.ps[:, MISC + i % 2, :], ALU.add).then_inc(added.sem, 1)

            choose(0, 0)
            tokens_out(1, 0)
            before = done[0]
            body = (1 + C) + (2 + 4 * C) + 2 * NG
            with dve.Fori(0, PAIRS) as pr:
                ticks = body * pr + before
                done[0] = 0
                choose(2 * pr + 2, ticks)
                dve.wait_ge(gtr.sem, gtr.of((1 + C) * pr))
                gate(2 * pr, ticks)
                add(pr)
                for part in range(1 + C):
                    dve.wait_ge(used.sem, used.of(6 * pr + 4))
                    dve.wait_ge(silu.sem, silu.of((1 + C) * pr + part + 1))
                    h, src = ((hidL, k.psf[:, UB * BANK:(UB + 2) * BANK]), (hidC, k.ps[:, CU, :]))[part]
                    dve.tensor_tensor(h[:, :], h[:, :], src, ALU.mult).then_inc(hid.sem, 1)
                tokens_out(pr + 2, ticks)
                assert done[0] == body
            add(PAIRS)
            dve.wait_ge(added.sem, added.of(n_sc * (PAIRS + 1)))
            inner_v.close(before + body * PAIRS)

        @block.scalar
        def _(act):
            with act.Fori(0, PAIRS) as pr:
                act.wait_ge(used.sem, used.of(6 * pr + 2))
                act.wait_ge(htr.sem, htr.of((1 + C) * pr))
                act.activation(hidL[:, :], k.psf[:, GB * BANK:(GB + 2) * BANK], ACT.Silu).then_inc(silu.sem, 1)
                if C:
                    act.activation(hidC[:, :], k.ps[:, CG, :], ACT.Silu).then_inc(silu.sem, 1)
                act.wait_ge(scat.sem, scat.of(n_sc * pr + n_sc))
                act.wait_ge(gtr.sem, gtr.of((1 + C) * pr + 1))
                act.copy(gtL[:, :, :], k.ps[:, MISC + 1, :].rearrange("p (t q) -> p t q", t=NTL)).then_inc(gts.sem, 1)
                if C:
                    act.wait_ge(gtr.sem, gtr.of((1 + C) * pr + 2))
                    act.copy(gtC[:, :, :, :], k.ps[:, MISC, :].rearrange("p (t h q) -> p t h q", t=2, h=2)).then_inc(gts.sem, 1)
                act.wait_ge(htr.sem, htr.of((1 + C) * pr + 1))
                act.copy(htL[:, :, :], k.psf[:, GB * BANK:(GB + 2) * BANK].rearrange("p (k s) -> p k s", k=KD)).then_inc(hts.sem, 1)
                if C:
                    act.wait_ge(htr.sem, htr.of((1 + C) * pr + 2))
                    act.copy(htC[:, :, :], k.ps[:, CG, :].rearrange("p (k s) -> p k s", k=4)).then_inc(hts.sem, 1)
                act.wait_ge(used.sem, used.of(6 * pr + 6))
                act.copy(yeL[:, :], k.psf[:, UB * BANK:(UB + 2) * BANK]).then_inc(yes.sem, 1)
                if C:
                    act.copy(yeC[:, :], k.ps[:, CU, :]).then_inc(yes.sem, 1)
            act.wait_ge(yes.sem, yes.of((1 + C) * PAIRS))
            act.wait_ge(gts.sem, gts.of((1 + C) * PAIRS))
    used.close(6 * PAIRS)
    choice.close(PAIRS + 1)
    gath.close(NG * (PAIRS + 1))
    xs_.close(NG * (PAIRS + 1))
    gatd.close(PAIRS)
    for s in (gtr, gts, silu, hid, htr, hts, yes):
        s.close((1 + C) * PAIRS)
    scat.close(n_sc * (PAIRS + 1))
    added.close(n_sc * (PAIRS + 1))
    stream.taken = stream.issued = base + PER * PAIRS
    for j in range(PER - RING, PER):
        stream.freed(base + PER * (PAIRS - 1) + j, used.sem, used.base - 5 + j // 4)
    stream.limit = k.moe_at[l + 1] + RING if l + 1 < LAYERS else len(stream.chunks)


def route(k, sb, uT, aff, pos, ntq, zeros):
    nc, c, c2 = k.nc, k.c, k.c2
    made, moved, low = k.sig["made"], k.sig["moved"], k.sig["low"]
    ps = k.ps
    nx = sb("nx", [P, NT2])
    affT = sb("affT", [N_EXP, T2])
    work = sb("work", [N_EXP, T2])
    best = sb("best", [N_EXP, 8])
    one = sb("one_", [N_EXP, T2])
    parts = [(0, SEQ, CAP_L)] + ([(SEQ, CTX, CAP_C)] if ntq > NTL else [])
    r = c2("router", 0, KD * N_EXP).rearrange("p (k e) -> p k e", k=KD)
    with nc.Block() as block:
        @block.tensor
        def _(pe):
            for t in range(ntq):
                for c_ in range(KD):
                    mm = pe.matmul(ps[:, 0, t * N_EXP:(t + 1) * N_EXP], uT[:, c_, P * t:P * t + P], r[:, c_, :],
                                   start=c_ == 0, stop=c_ == KD - 1, skip_group_check=True)
            mm.then_inc(made.sem, 1)
            pe.wait_ge(moved.sem, moved.of(1))
            for t in range(ntq):
                mm = pe.transpose(ps[0:N_EXP, 1 + t // 4, (t % 4) * P:(t % 4 + 1) * P], aff[:, t, :], c("ident"))
            mm.then_inc(made.sem, 1)
            pe.wait_ge(moved.sem, moved.of(2))
            for t in range(ntq):
                mm = pe.transpose(ps[:, 3, t * N_EXP:(t + 1) * N_EXP], work[:, P * t:P * t + P],
                                  c("ident")[0:N_EXP, 0:N_EXP])
            mm.then_inc(made.sem, 1)

        @block.gpsimd
        def _(pool):
            steps = k.steps(pool, "g")
            for buf in zeros[1:]:
                steps.free(pool.memset(buf, 0.0))
            pool.wait_ge(made.sem, made.of(1))
            steps(pool.memset(zeros[0], 0.0))

        @block.scalar
        def _(act):
            steps = k.steps(act, "s")
            act.wait_ge(low.sem, low.of(1))
            steps.free(act.activation(aff[:, 0:ntq, :], aff[:, 0:ntq, :], ACT.Exp))
            steps.tell(low.sem)

        @block.vector
        def _(dve):
            steps = k.steps(dve, "v")
            dve.wait_ge(made.sem, made.of(1))
            lg = ps[:, 0, 0:ntq * N_EXP].rearrange("p (t e) -> p t e", e=N_EXP)
            b = nx[:, 0:ntq].unsqueeze(2).to_broadcast([P, ntq, N_EXP])
            A = aff[:, 0:ntq, :]
            steps(dve.tensor_reduce(nx[:, 0:ntq], lg, AX.X, ALU.max))
            steps.free(dve.tensor_tensor(A, lg, b, ALU.subtract))
            steps.tell(low.sem)
            dve.wait_ge(low.sem, low.of(2))
            steps(dve.tensor_reduce(nx[:, 0:ntq], A, AX.X, ALU.add))
            steps(dve.reciprocal(nx[:, 0:ntq], nx[:, 0:ntq]))
            steps.free(dve.tensor_tensor(A, A, b, ALU.mult))
            steps.tell(moved.sem)
            steps.free(dve.memset(one[:, :], 1.0))
            steps(dve.memset(pos[:, :, N_EXP:N_EXP + 2], -1.0))
            dve.wait_ge(made.sem, made.of(2))
            steps(dve.tensor_copy(affT[:, 0:ntq * P], k.psf[0:N_EXP, BANK:BANK + ntq * P]))
            for lo, n, cap in parts:
                w = affT[:, lo:lo + n]
                for _ in range(cap // 8):
                    steps(dve.max(best[:, :], w))
                    steps(dve.match_replace(w, best[:, :], w, -1.0))
                m = work[:, lo:lo + n]
                steps(dve.tensor_scalar(w, w, 0.0, None, ALU.is_lt))
                steps(dve.tensor_tensor_scan(m, one[:, 0:n], w, 0.0, ALU.mult, ALU.add))
                steps(dve.tensor_tensor(m, m, w, ALU.mult))
                steps(dve.tensor_scalar(m, m, -1.0, None, ALU.add))
            dve.sem_inc(moved.sem, 1)
            dve.wait_ge(made.sem, made.of(3))
            steps(dve.tensor_copy(pos[:, 0:ntq, 0:N_EXP], ps[:, 3, 0:ntq * N_EXP].rearrange("p (t e) -> p t e", e=N_EXP)))
    made.close(3)
    moved.close(2)
    low.close(2)


SIGNALS = ["product", "taken_v", "taken_s", "load", "squared", "rooted", "meant", "meant2", "rooted2", "normed", "scores", "row_max", "exp", "probs",
           "turned", "pt", "out", "out_taken", "low", "fine", "fin2", "made", "moved", "flipped", "stored",
           "multiplied", "used", "choice", "gath", "xs", "gatd", "gtr", "gts", "silu", "hid", "htr", "hts", "yes", "scat",
           "added", "inner_v", "inner_s"]


def program(nc, dram, out):
    k = Kernel()
    k.nc, k.dram, k.out = nc, dram, out
    with ExitStack() as ctx:
        k.ctx = ctx
        k.uid = 0

        def alloc(scope):
            def sb(name, shape, dt=F32):
                k.uid += 1
                return scope.enter_context(nc.sbuf_tensor(f"{name}_{k.uid}", shape, dt))
            return sb
        k.alloc = alloc
        sb = alloc(ctx)
        k.ps = ctx.enter_context(nc.psum_tensor("ps", [P, 8, BANK], F32))
        k.psf = k.ps[:, :, :].rearrange("p b c -> p (b c)")
        k.sig = {n: Signal(ctx.enter_context(nc.semaphore(n))) for n in SIGNALS}
        done = {w: Steps(None, ctx.enter_context(nc.semaphore("steps_" + w))) for w in ("v", "s", "g")}

        def steps(eng, who):
            done[who].eng = eng
            return done[who]
        k.steps = steps

        ring = sb("ring", [P, RING, CHUNK])
        loaded = [ctx.enter_context(nc.semaphore(f"loaded{i}")) for i in range(RING)]
        w1, w2, wm = ([dram[n][i] for i in range(dram[n].shape[0])] for n in ("w1", "w2", "w_mod"))
        chunks = w1[:N_DELTA] + wm[:N_MOD] + w1[N_DELTA:]
        k.whole_ring = N_DELTA + N_MOD
        k.moe_at = []
        for l in range(LAYERS):
            mine = w2[l * LAYER_CHUNKS:(l + 1) * LAYER_CHUNKS]
            after = wm[(l + 1) * N_MOD:(l + 2) * N_MOD]
            chunks += mine[:N_IN2] + after + mine[N_IN2:]
            k.moe_at.append(len(chunks))
            chunks += [expert_chunk(dram, l, 0, j) for j in range(RING)] + [None] * (PAIR_CHUNKS * N_EXP // 2 - RING)
        slots = [n % (RING // 2) if n < k.whole_ring else (n - k.whole_ring) % RING for n in range(len(chunks))]
        k.stream = Stream(ring, loaded, chunks, slots)
        k.stream.limit = k.whole_ring
        k.stream.loads = k.sig["load"].sem
        k.cond = sb("cond", [P, KD, 32])
        k.b_mod = sb("b_mod", [P, LAYERS, 6 * KD])
        k.mod = sb("mod", [P, LAYERS, 6 * KD, 2])
        const = sb("const", [P, CONSTS[0][0].shape[1]])
        k.h1 = sb("h1", [P, NT2, D])
        with ExitStack() as first:
            const1 = alloc(first)("const1", [P, CONSTS[1][0].shape[1]])
            cols1 = alloc(first)("cols1", [P, NP1])
            at = {**{n: (const, x) for n, x in CONSTS[0][1].items()}, **{n: (const1, x) for n, x in CONSTS[1][1].items()}}
            k.c = lambda name: at[name][0][:, at[name][1][0]:at[name][1][0] + at[name][1][1]]
            k.c1 = lambda name, i, n=1: cols1[:, AT1[name] + i:AT1[name] + i + n]
            k.c1m = lambda name, n: cols1[:, AT1[name]:AT1[name] + n]
            k.one = const[:, CONSTS[0][1]["ones"][0]:CONSTS[0][1]["ones"][0] + 1]
            load(k, [(k.h1[:, 0:NTL, :], dram["x"]), (k.h1[0:N_META, NTL, :], dram["meta"]), (const[:, :], dram["const0"]), (const1[:, :], dram["const1"]), (cols1[:, :], dram["cols1"]),
                     (k.cond[:, :, :], dram["cond"]), (k.b_mod[:, :, :], dram["b_mod"])])
            first_block(k)
        second_block(k)


def by_channel(v):
    v = np.asarray(v)
    return v.reshape(-1, P).T


def k_tiles(w):
    w = np.asarray(w)
    return w.reshape(-1, P, w.shape[1]).transpose(1, 0, 2).reshape(P, -1)


def column_chunks(w, width=256):
    w = np.asarray(w)
    return w.reshape(KD, P, -1, width).transpose(2, 1, 0, 3).reshape(-1, P, CHUNK)


def row_chunks(w):
    w = np.asarray(w)
    return w.reshape(2, 4, P, 2, BANK).transpose(3, 0, 2, 1, 4).reshape(-1, P, CHUNK)


def block_diagonal(w):
    w = np.asarray(w)
    out = np.zeros((P, 2, P), w.dtype)
    for h in range(4):
        b = HD * (h % 2)
        out[b:b + HD, h // 2, b:b + HD] = w[h]
    return out.reshape(P, -1)


def lay_out(i):
    f = np.float32
    a = {n: np.asarray(v) for n, v in i.items()}
    w_in = a["w_in"][0]
    first = 2 * LRU_W
    fox = w_in[:, first:first + 3 * FOX_W + FOX_HEADS]
    heads = w_in[:, first + 3 * FOX_W + FOX_HEADS:]
    up = a["ffn_up"][0].reshape(KD, P, 2, FT, P).transpose(3, 1, 0, 2, 4).reshape(FT, P, CHUNK)
    down = a["ffn_down"][0].reshape(FT // 2, 2, P, D).transpose(0, 2, 1, 3).reshape(FT // 2, P, CHUNK)
    w1 = np.concatenate([column_chunks(heads), column_chunks(w_in[:, :first]), column_chunks(fox[:, :3 * FOX_W]),
                         row_chunks(a["w_out"][0]), up, down])
    cols = dict(norm_mix_pre=by_channel(a["norm_mix_pre"][0]), norm_ffn_pre=by_channel(a["norm_ffn_pre"][0]),
                lru_conv_w=by_channel(a["lru_conv_w"][0]), lru_conv_b=by_channel(a["lru_conv_b"][0]),
                lru_gate_a_b=by_channel(a["lru_gate_a_b"][0]), lru_gate_x_b=by_channel(a["lru_gate_x_b"][0]),
                lru_lambda=by_channel(a["lru_lambda"][0]), rwkv_mu=by_channel(a["rwkv_mu"][0]),
                rwkv_w0=by_channel(a["rwkv_w0"][0]), rwkv_a0=by_channel(a["rwkv_a0"][0]),
                rwkv_k_k=by_channel(a["rwkv_k_k"][0]), rwkv_k_a=by_channel(a["rwkv_k_a"][0]),
                rwkv_r_k=by_channel(a["rwkv_r_k"][0]), rwkv_ln_w=by_channel(a["rwkv_ln_w"][0]),
                rwkv_ln_b=by_channel(a["rwkv_ln_b"][0]),
                fox_f_bias=np.pad(a["fox_f_bias"][0], (0, P - FOX_HEADS))[:, None],
                w_f=k_tiles(fox[:, 3 * FOX_W:]),
                gate_a=block_diagonal(a["lru_gate_a_w"][0]), gate_x=block_diagonal(a["lru_gate_x_w"][0]),
                wa_up=np.concatenate([a["rwkv_w_up"][0], a["rwkv_a_up"][0]]), g_up=a["rwkv_g_up"][0],
                ffn_conv=by_channel(a["ffn_conv"][0]),
                )
    cols1 = np.concatenate([cols[n] for n in COLS1], 1)
    sent = {"x": a["x"][0].reshape(NTL, P, D).transpose(1, 0, 2), "meta": a["meta_tokens"],
            "cond": np.pad(np.stack([by_channel(a["c_2"][0]), by_channel(a["c_ctx_2"])], 2), ((0, 0), (0, 0), (0, 30))),
            "b_mod": np.stack([by_channel(b) for b in a["b_mod_2"]], 1),
            "w1": w1, "cols1": cols1, "rows1": np.concatenate([a["norm_mix_post"], a["norm_ffn_post"]]),
            "const0": CONSTS[0][0], "const1": CONSTS[1][0], "const2": CONSTS[2][0]}
    order = np.arange(A_WIDTH).reshape(2, 4, HD).transpose(1, 0, 2).reshape(-1)
    w2, cols2, rows2 = [], [], []
    for l in range(LAYERS):
        w_in2, w_out2 = a["w_in_2"][l], a["w_out_2"][l]
        w_in2 = np.concatenate([w_in2[:, order], w_in2[:, A_WIDTH:]], 1)
        w_out2 = np.concatenate([w_out2[order], w_out2[A_WIDTH:]])
        w2.append(np.concatenate([column_chunks(w_in2), row_chunks(w_out2)]))
        cc = dict(conv_w=by_channel(a["conv_w_2"][l]),
                  conv_b=by_channel(a["conv_b_2"][l]), ln_g=by_channel(a["conv_ln_g_2"][l]),
                  ln_b=by_channel(a["conv_ln_b_2"][l]), router=k_tiles(a["w_router_2"][l]),
                  sink=np.broadcast_to(a["a_sink_2"][l], (P, 8)))
        cols2.append(np.concatenate([cc[n] for n in COLS2], 1))
        rows2.append(np.stack([a[n][l] for n in ("ln1_g_2", "ln1_b_2", "ln2_g_2", "ln2_b_2")]))
    bias = np.zeros((LAYERS, 4, BIAS_ROWS + 1, BIAS_PAD), f)
    lo = GRID_W - 1 - (NA_COLS - 1)
    bias[:, :, 1:, lo:lo + 2 * NA_COLS - 1] = a["nat_bias_2"]
    sent.update(w2=np.concatenate(w2), w_mod=np.concatenate([column_chunks(w) for w in a["w_mod_2"]]), cols2=np.stack(cols2), rows2=np.stack(rows2), bias=bias,
                ctx=a["ctx_2"][0].reshape(2, P, D).transpose(1, 0, 2),
                w_gate=a["w_gate_2"], w_up=a["w_up_2"], w_down=a["w_down_2"])
    return {n: np.ascontiguousarray(v) for n, v in sent.items()}


def kernel(**inputs):
    import concourse.bacc as bacc
    from concourse.bass_utils import run_bass_kernel_spmd

    nc = bacc.Bacc("TRN2", target_bir_lowering=False, num_devices=1)
    sent = lay_out(inputs)
    arrays, dram = {}, {}
    for name, a in sent.items():
        arrays["in_" + name] = a
        dram[name] = nc.dram_tensor("in_" + name, a.shape, mybir.dt.from_np(a.dtype), kind="ExternalInput").ap()
    out = nc.dram_tensor("out_0_dram", (1, SEQ, D), F32, kind="ExternalOutput").ap()
    program(nc, dram, out)
    r = run_bass_kernel_spmd(nc, [arrays], core_ids=[0])
    return r.results[0]["out_0_dram"]
```
